# Optimizing a Trainium2 kernel written in Bass

```python
import math
import jax, jax.numpy as jnp
from jax import lax
import numpy as np

D_MODEL = 1024
BATCH = 1
SEQ = 256
DEPTH = 2

D_A = D_MODEL // 2
HEAD_A = 64
N_HEADS_A = D_A // HEAD_A
LORA_DECAY = 64
LORA_ICLR = 64
LORA_GATE = 128
N_DIR = 2
C_RWKV = 3 * D_A + N_DIR * LORA_DECAY + N_DIR * LORA_ICLR + LORA_GATE
RWKV_SPLITS = [D_A, 2 * D_A, 3 * D_A, 3 * D_A + N_DIR * LORA_DECAY,
               3 * D_A + N_DIR * LORA_DECAY + N_DIR * LORA_ICLR]
DECAY_SCALE = math.exp(-0.5)
GN_EPS = 64e-5
HEAD_B = 64
D_B = D_MODEL // 2
N_HEADS_B = D_B // (2 * HEAD_B)
C_ATTN = 3 * D_B
ALIBI_MAX_EXP = 8.0
Q_BLOCK = 128
N_BRANCH = 2
C_IN = C_RWKV + C_ATTN + N_BRANCH * D_MODEL
D_FF = ((8 * D_MODEL // 3 + 127) // 128) * 128
NORM_EPS = 1e-6


def rms_norm(x, g, eps=NORM_EPS):
    xf = x.astype(jnp.float32)
    y = xf * lax.rsqrt(jnp.mean(xf * xf, axis=-1, keepdims=True) + eps)
    return (y * g.astype(jnp.float32)).astype(x.dtype)

def swiglu(h, w_in, w_out):
    gate, up = jnp.split(h @ w_in, 2, axis=-1)
    return (jax.nn.silu(gate) * up) @ w_out

def centred_shift(p):
    prev = jnp.pad(p[:, :-1], ((0, 0), (1, 0), (0, 0)))
    nxt = jnp.pad(p[:, 1:], ((0, 0), (0, 1), (0, 0)))
    return 0.5 * (prev + nxt)

def to_heads(t, n_heads):
    return t.reshape(t.shape[:-1] + (n_heads, t.shape[-1] // n_heads))

def rwkv7_scan(r, w, k, v, kk, a, reverse):
    b, s, h, n = r.shape
    xs = tuple(jnp.moveaxis(t.astype(jnp.float32), 1, 0) for t in (r, w, k, v, kk, a))

    def step(state, inp):
        r_t, w_t, k_t, v_t, kk_t, a_t = inp
        sa = jnp.einsum('bhvk,bhk->bhv', state, -kk_t)
        state = (state * w_t[:, :, None, :]
                 + sa[..., None] * (kk_t * a_t)[:, :, None, :]
                 + v_t[..., None] * k_t[:, :, None, :])
        y_t = jnp.einsum('bhvk,bhk->bhv', state, r_t)
        return state, y_t

    s0 = jnp.zeros((b, h, n, n), jnp.float32)
    _, ys = lax.scan(step, s0, xs, reverse=reverse)
    return jnp.moveaxis(ys, 0, 1)

def rwkv7_mixer(p, mu, w0, w2, a0, a2, g2, k_k, k_a, r_k, ln_g, ln_b):
    p = p + mu * (centred_shift(p) - p)
    r, k, v, dw, da, dg = jnp.split(p, RWKV_SPLITS, axis=-1)
    b, s, _ = r.shape
    dw = dw.reshape(b, s, N_DIR, LORA_DECAY)
    da = da.reshape(b, s, N_DIR, LORA_ICLR)
    decay = jnp.exp(-DECAY_SCALE * jax.nn.sigmoid(
        w0 + jnp.einsum('bsgr,grc->bsgc', jnp.tanh(dw), w2)))
    iclr = jax.nn.sigmoid(a0 + jnp.einsum('bsgr,grc->bsgc', da, a2))
    gate = jax.nn.sigmoid(dg) @ g2
    kk = to_heads(k * k_k, N_HEADS_A).astype(jnp.float32)
    kk = kk / jnp.maximum(jnp.sqrt(jnp.sum(kk * kk, axis=-1, keepdims=True)), 1e-12)
    k_dir = k[:, :, None, :] * (1.0 + (iclr - 1.0) * k_a)
    r_h = to_heads(r, N_HEADS_A)
    v_h = to_heads(v, N_HEADS_A)
    k_h = to_heads(k_dir, N_HEADS_A)
    w_h = to_heads(decay, N_HEADS_A)
    a_h = to_heads(iclr, N_HEADS_A)
    y = (rwkv7_scan(r_h, w_h[:, :, 0], k_h[:, :, 0], v_h, kk, a_h[:, :, 0], False)
         + rwkv7_scan(r_h, w_h[:, :, 1], k_h[:, :, 1], v_h, kk, a_h[:, :, 1], True))
    mean = jnp.mean(y, axis=-1, keepdims=True)
    var = jnp.mean(jnp.square(y - mean), axis=-1, keepdims=True)
    y = ((y - mean) * lax.rsqrt(var + GN_EPS)).reshape(b, s, D_A) * ln_g + ln_b
    bonus = jnp.einsum('bshn,bsghn,hn->bsh', r_h.astype(jnp.float32),
                       k_h.astype(jnp.float32), r_k.astype(jnp.float32))[..., None] * v_h
    return (y + bonus.reshape(b, s, D_A)) * gate

def diff_attention(p, q_gain, k_gain, lam_vecs, sub_g, lam_init):
    b, s, _ = p.shape
    q, k, v = jnp.split(p, 3, axis=-1)
    q = rms_norm(q.reshape(b, s, N_HEADS_B, 2, HEAD_B), q_gain)
    k = rms_norm(k.reshape(b, s, N_HEADS_B, 2, HEAD_B), k_gain)
    v = v.reshape(b, s, N_HEADS_B, 2 * HEAD_B)
    lv = lam_vecs.astype(jnp.float32)
    lam = jnp.exp(jnp.sum(lv[0] * lv[1])) - jnp.exp(jnp.sum(lv[2] * lv[3])) + lam_init
    n_blk = s // Q_BLOCK
    q_blk = q.reshape(b, n_blk, Q_BLOCK, N_HEADS_B, 2, HEAD_B).transpose(1, 0, 3, 4, 2, 5)
    k_t = k.transpose(0, 2, 3, 1, 4)
    v_t = v.transpose(0, 2, 1, 3)
    slopes = 2.0 ** (-ALIBI_MAX_EXP * jnp.arange(1, N_HEADS_B + 1, dtype=jnp.float32) / N_HEADS_B)
    k_pos = jnp.arange(s, dtype=jnp.float32)
    q_pos = k_pos.reshape(n_blk, Q_BLOCK)
    scale = HEAD_B ** -0.5

    def attend_block(args):
        qb, qp = args
        logits = jnp.einsum('bhmqd,bhmkd->bhmqk', qb, k_t,
                            preferred_element_type=jnp.float32) * scale
        bias = -slopes[:, None, None] * jnp.abs(qp[:, None] - k_pos[None, :])
        prob = jax.nn.softmax(logits + bias[None, :, None], axis=-1)
        attn = prob[:, :, 0] - lam * prob[:, :, 1]
        return jnp.einsum('bhqk,bhkc->bhqc', attn.astype(v_t.dtype), v_t)

    o = lax.map(attend_block, (q_blk, q_pos))
    o = o.transpose(1, 0, 3, 2, 4).reshape(b, s, N_HEADS_B, 2 * HEAD_B)
    o = rms_norm(o, sub_g) * (1.0 - lam_init)
    return o.reshape(b, s, D_B)

def first_inputs(seed: int = 0) -> dict:
    key = jax.random.key(seed)
    ks = iter(jax.random.split(key, 32))
    L = DEPTH

    def nrm(shape, scale):
        return jax.random.normal(next(ks), shape, jnp.float32) * scale

    def gain(shape):
        return 1.0 + nrm(shape, 0.02)

    return {
        'x': nrm((BATCH, SEQ, D_MODEL), 1.0),
        'norm_ffn1': gain((L, D_MODEL)),
        'ffn1_in': nrm((L, D_MODEL, 2 * D_FF), D_MODEL ** -0.5),
        'ffn1_out': nrm((L, D_FF, D_MODEL), D_FF ** -0.5),
        'norm_mix': gain((L, D_MODEL)),
        'w_in': nrm((L, D_MODEL, C_IN), D_MODEL ** -0.5),
        'rwkv_mu': jax.random.uniform(next(ks), (L, C_RWKV), jnp.float32),
        'decay_w0': nrm((L, N_DIR, D_A), 1.0),
        'decay_w2': nrm((L, N_DIR, LORA_DECAY, D_A), 0.5 * LORA_DECAY ** -0.5),
        'iclr_a0': nrm((L, N_DIR, D_A), 0.5),
        'iclr_a2': nrm((L, N_DIR, LORA_ICLR, D_A), 0.5 * LORA_ICLR ** -0.5),
        'gate_g2': nrm((L, LORA_GATE, D_A), LORA_GATE ** -0.5),
        'k_k': 0.85 + nrm((L, D_A), 0.05),
        'k_a': 1.0 + nrm((L, D_A), 0.05),
        'r_k': nrm((L, N_HEADS_A, HEAD_A), 0.1),
        'ln_x_g': gain((L, D_A)),
        'ln_x_b': nrm((L, D_A), 0.02),
        'q_gain': gain((L, HEAD_B)),
        'k_gain': gain((L, HEAD_B)),
        'diff_lambda': nrm((L, 4, HEAD_B), 0.1),
        'subln_g': gain((L, 2 * HEAD_B)),
        'w_branch': nrm((L, N_BRANCH, D_A, D_MODEL), D_A ** -0.5),
        'w_out': nrm((L, D_MODEL, D_MODEL), D_MODEL ** -0.5),
        'norm_ffn2': gain((L, D_MODEL)),
        'ffn2_in': nrm((L, D_MODEL, 2 * D_FF), D_MODEL ** -0.5),
        'ffn2_out': nrm((L, D_FF, D_MODEL), D_FF ** -0.5),
    }

def first_block(x, norm_ffn1, ffn1_in, ffn1_out, norm_mix, w_in, rwkv_mu, decay_w0, decay_w2,
              iclr_a0, iclr_a2, gate_g2, k_k, k_a, r_k, ln_x_g, ln_x_b, q_gain, k_gain,
              diff_lambda, subln_g, w_branch, w_out, norm_ffn2, ffn2_in, ffn2_out):
    b, s, d = x.shape
    for l in range(DEPTH):
        lam_init = 0.8 - 0.6 * math.exp(-0.3 * l)
        x = x + 0.5 * swiglu(rms_norm(x, norm_ffn1[l]), ffn1_in[l], ffn1_out[l])
        h = rms_norm(x, norm_mix[l])
        proj = h @ w_in[l]
        p_rwkv, p_attn, p_gate = jnp.split(proj, [C_RWKV, C_RWKV + C_ATTN], axis=-1)
        o_a = rwkv7_mixer(p_rwkv, rwkv_mu[l], decay_w0[l], decay_w2[l], iclr_a0[l],
                          iclr_a2[l], gate_g2[l], k_k[l], k_a[l], r_k[l],
                          ln_x_g[l], ln_x_b[l]).astype(x.dtype)
        o_b = diff_attention(p_attn, q_gain[l], k_gain[l], diff_lambda[l], subln_g[l],
                             lam_init).astype(x.dtype)
        branches = jnp.stack([o_a, o_b], axis=2)
        y = jnp.einsum('bsgc,gcd->bsgd', branches, w_branch[l])
        gates = jax.nn.sigmoid(p_gate.reshape(b, s, N_BRANCH, d))
        merged = jnp.sum(gates * y, axis=2)
        x = x + merged @ w_out[l]
        x = x + 0.5 * swiglu(rms_norm(x, norm_ffn2[l]), ffn2_in[l], ffn2_out[l])
    return x


GRID_W = 64
CTX_LEN = 256
N_EVEN = (DEPTH + 1) // 2
N_ODD = DEPTH // 2
HEAD_DIM = 64
ATTN_HEADS = 8
KV_HEADS = 2
GQA_GROUP = ATTN_HEADS // KV_HEADS
WINDOW = 128
ATTN_BLOCK = 128
ROPE_BASE = 10000.0
GMLP_GROUPS = 8
GMLP_DIM = 64
CHUNK = 128
Q_W = ATTN_HEADS * HEAD_DIM
KV_W = KV_HEADS * HEAD_DIM
A_W = GMLP_GROUPS * GMLP_DIM
IN_W = Q_W + 2 * KV_W + 2 * A_W
MIX_W = Q_W + A_W
POOL_WINDOWS = (2, 4, 8, 16)
POOL_GROUPS = 4
POOL_DIM = D_MODEL // POOL_GROUPS
PEER_HEADS = 8
PEER_NKEYS = 128
PEER_EXPERTS = PEER_NKEYS * PEER_NKEYS
PEER_TOPK = 16
PEER_DKEY = 256
PEER_DHALF = PEER_DKEY // 2
PEER_BLOCK = 128
N_MOD = 6
EPS = 1e-6


def rms_norm_2(x, g):
    xf = x.astype(jnp.float32)
    y = xf * lax.rsqrt(jnp.mean(jnp.square(xf), axis=-1, keepdims=True) + EPS)
    return (y * g).astype(x.dtype)

def axial_rope(t, row, col):
    half = HEAD_DIM // 2
    quarter = half // 2
    inv = jnp.power(ROPE_BASE, -jnp.arange(quarter, dtype=jnp.float32) / quarter)

    def rot(xa, pos):
        ang = pos[:, None] * inv[None, :]
        cos = jnp.cos(ang)[None, :, None, :]
        sin = jnp.sin(ang)[None, :, None, :]
        x1, x2 = xa[..., :quarter], xa[..., quarter:]
        return jnp.concatenate([x1 * cos - x2 * sin, x1 * sin + x2 * cos], axis=-1)

    tf = t.astype(jnp.float32)
    return jnp.concatenate([rot(tf[..., :half], row), rot(tf[..., half:], col)], axis=-1).astype(t.dtype)

def sink_softmax(logits, sink):
    sk = jnp.broadcast_to(sink.astype(jnp.float32).reshape(1, KV_HEADS, GQA_GROUP, 1, 1), logits.shape[:-1] + (1,))
    return jax.nn.softmax(jnp.concatenate([logits, sk], axis=-1), axis=-1)[..., :-1]

def window_attention(q, k, v, k_ctx, v_ctx, sink):
    B_, L_ = q.shape[0], q.shape[1]
    nb = L_ // ATTN_BLOCK
    span = ATTN_BLOCK + 2 * WINDOW
    scale = HEAD_DIM ** -0.5
    pad = ((0, 0), (WINDOW, WINDOW), (0, 0), (0, 0))
    kp = jnp.pad(k, pad)
    vp = jnp.pad(v, pad)
    qb = q.reshape(B_, nb, ATTN_BLOCK, KV_HEADS, GQA_GROUP, HEAD_DIM).swapaxes(0, 1)

    def one_block(args):
        n, qn = args
        start = n * ATTN_BLOCK
        kn = lax.dynamic_slice_in_dim(kp, start, span, axis=1)
        vn = lax.dynamic_slice_in_dim(vp, start, span, axis=1)
        qpos = start + jnp.arange(ATTN_BLOCK)
        kpos = start - WINDOW + jnp.arange(span)
        valid = (jnp.abs(qpos[:, None] - kpos[None, :]) <= WINDOW) & (kpos >= 0)[None, :] & (kpos < L_)[None, :]
        s_loc = jnp.einsum('bqhgd,bkhd->bhgqk', qn, kn).astype(jnp.float32) * scale
        s_loc = jnp.where(valid, s_loc, -jnp.inf)
        s_ctx = jnp.einsum('bqhgd,bkhd->bhgqk', qn, k_ctx).astype(jnp.float32) * scale
        p = sink_softmax(jnp.concatenate([s_loc, s_ctx], axis=-1), sink)
        o = (jnp.einsum('bhgqk,bkhd->bqhgd', p[..., :span], vn.astype(jnp.float32))
             + jnp.einsum('bhgqk,bkhd->bqhgd', p[..., span:], v_ctx.astype(jnp.float32)))
        return o.astype(q.dtype)

    out = lax.map(one_block, (jnp.arange(nb), qb))
    return out.swapaxes(0, 1).reshape(B_, L_, Q_W)

def context_attention(qc, kc, vc, sink):
    B_, C_ = qc.shape[0], qc.shape[1]
    qg = qc.reshape(B_, C_, KV_HEADS, GQA_GROUP, HEAD_DIM)
    s = jnp.einsum('bqhgd,bkhd->bhgqk', qg, kc).astype(jnp.float32) * (HEAD_DIM ** -0.5)
    p = sink_softmax(s, sink)
    o = jnp.einsum('bhgqk,bkhd->bqhgd', p, vc.astype(jnp.float32))
    return o.astype(qc.dtype).reshape(B_, C_, Q_W)

def chunk_gmlp(ua, va, w_s, b_s):
    B_, L_ = ua.shape[0], ua.shape[1]
    u = jax.nn.gelu(ua).reshape(B_, L_, GMLP_GROUPS, GMLP_DIM)
    vf = jax.nn.gelu(va).reshape(B_, L_, GMLP_GROUPS, GMLP_DIM).astype(jnp.float32)
    mu = jnp.mean(vf, axis=-1, keepdims=True)
    var = jnp.mean(jnp.square(vf - mu), axis=-1, keepdims=True)
    v = ((vf - mu) * lax.rsqrt(var + EPS)).astype(ua.dtype)
    vc = v.reshape(B_, L_ // CHUNK, CHUNK, GMLP_GROUPS, GMLP_DIM)
    mixed = jnp.einsum('gpq,bcqgd->bcpgd', w_s, vc) + b_s.T[:, :, None]
    return (u * mixed.reshape(B_, L_, GMLP_GROUPS, GMLP_DIM)).reshape(B_, L_, A_W)

def split_proj(p):
    return jnp.split(p, [Q_W, Q_W + KV_W, Q_W + 2 * KV_W, Q_W + 2 * KV_W + A_W], axis=-1)

def attn_gmlp_mixer(h, hc, w_in, w_out, sink, w_s, b_s, row, col, need_ctx_out):
    B_, L_ = h.shape[0], h.shape[1]
    C_ = hc.shape[1]
    q, k, v, ua, va = split_proj(h @ w_in)
    q = axial_rope(q.reshape(B_, L_, ATTN_HEADS, HEAD_DIM), row, col)
    k = axial_rope(k.reshape(B_, L_, KV_HEADS, HEAD_DIM), row, col)
    v = v.reshape(B_, L_, KV_HEADS, HEAD_DIM)
    if need_ctx_out:
        qc, kc, vc, uac, vac = split_proj(hc @ w_in)
    else:
        kc, vc = jnp.split(hc @ w_in[:, Q_W:Q_W + 2 * KV_W], 2, axis=-1)
    kc = kc.reshape(B_, C_, KV_HEADS, HEAD_DIM)
    vc = vc.reshape(B_, C_, KV_HEADS, HEAD_DIM)
    attn = window_attention(q, k, v, kc, vc, sink)
    mix = chunk_gmlp(ua, va, w_s, b_s)
    y = jnp.concatenate([attn, mix], axis=-1) @ w_out
    yc = None
    if need_ctx_out:
        attn_c = context_attention(qc.reshape(B_, C_, ATTN_HEADS, HEAD_DIM), kc, vc, sink)
        mix_c = chunk_gmlp(uac, vac, w_s, b_s)
        yc = jnp.concatenate([attn_c, mix_c], axis=-1) @ w_out
    return y, yc

def multiscale_pool(h, w_pool, scale):
    B_, L_ = h.shape[0], h.shape[1]
    hf = h.reshape(B_, L_, POOL_GROUPS, POOL_DIM).astype(jnp.float32)
    cs = jnp.pad(lax.cumsum(hf, axis=1), ((0, 0), (1, 0), (0, 0), (0, 0)))
    t = jnp.arange(L_)
    diffs = []
    for g, w in enumerate(POOL_WINDOWS):
        lo = jnp.clip(t - w // 2, 0, L_)
        hi = jnp.clip(t + w // 2, 0, L_)
        mean = (cs[:, hi, g] - cs[:, lo, g]) / (hi - lo).astype(jnp.float32)[None, :, None]
        diffs.append(mean - hf[:, :, g])
    pooled = jnp.stack(diffs, axis=2).astype(h.dtype)
    y = jnp.einsum('blgc,gce->blge', pooled, w_pool).reshape(B_, L_, D_MODEL)
    return y * scale

def peer_ffn(h, w_q, sub_keys, down, up):
    shape = h.shape
    blocks = h.reshape(-1, PEER_BLOCK, D_MODEL)

    def one_block(xb):
        n = xb.shape[0]
        q = (xb @ w_q).reshape(n, PEER_HEADS, 2, PEER_DHALF)
        s = jnp.einsum('thpk,pnk->thpn', q, sub_keys).astype(jnp.float32)
        s_top, i_top = lax.top_k(s, PEER_TOPK)
        cand_s = s_top[:, :, 0, :, None] + s_top[:, :, 1, None, :]
        cand_i = i_top[:, :, 0, :, None] * PEER_NKEYS + i_top[:, :, 1, None, :]
        best_s, best_pos = lax.top_k(cand_s.reshape(n, PEER_HEADS, -1), PEER_TOPK)
        idx = jnp.take_along_axis(cand_i.reshape(n, PEER_HEADS, -1), best_pos, axis=-1)
        gate = jax.nn.softmax(best_s, axis=-1)
        u = jnp.take(down, idx, axis=0)
        act = jax.nn.gelu(jnp.einsum('thkd,td->thk', u, xb))
        v = jnp.take(up, idx, axis=0)
        return jnp.einsum('thk,thkd->td', (gate * act).astype(v.dtype), v)

    return lax.map(one_block, blocks).reshape(shape)

def second_inputs(seed: int = 0) -> dict:
    key = jax.random.key(seed)
    ks = jax.random.split(key, 20)
    D = D_MODEL

    def nrm(k, shape, s):
        return jax.random.normal(k, shape, jnp.float32) * s

    return {
        'x': nrm(ks[0], (BATCH, SEQ, D), 1.0),
        'c': nrm(ks[1], (BATCH, D), 1.0),
        'ctx': nrm(ks[2], (BATCH, CTX_LEN, D), 1.0),
        'c_ctx': nrm(ks[3], (D,), 1.0),
        'mod_w': nrm(ks[4], (DEPTH, D, N_MOD * D), 0.5 * D ** -0.5),
        'mod_b': nrm(ks[5], (DEPTH, N_MOD * D), 0.02),
        'norm1_g': 1.0 + nrm(ks[6], (DEPTH, D), 0.02),
        'norm2_g': 1.0 + nrm(ks[7], (DEPTH, D), 0.02),
        'attn_in_w': nrm(ks[8], (N_EVEN, D, IN_W), D ** -0.5),
        'attn_out_w': nrm(ks[9], (N_EVEN, MIX_W, D), MIX_W ** -0.5),
        'attn_sink': nrm(ks[10], (N_EVEN, ATTN_HEADS), 0.5),
        'gmlp_w_s': nrm(ks[11], (N_EVEN, GMLP_GROUPS, CHUNK, CHUNK), CHUNK ** -0.5),
        'gmlp_b_s': 1.0 + nrm(ks[12], (N_EVEN, GMLP_GROUPS, CHUNK), 0.02),
        'pool_w': nrm(ks[13], (N_ODD, POOL_GROUPS, POOL_DIM, POOL_DIM), POOL_DIM ** -0.5),
        'pool_scale': 1.0 + nrm(ks[14], (N_ODD, D), 0.02),
        'peer_w_q': nrm(ks[15], (DEPTH, D, PEER_HEADS * PEER_DKEY), D ** -0.5),
        'peer_sub_keys': nrm(ks[16], (DEPTH, 2, PEER_NKEYS, PEER_DHALF), PEER_DHALF ** -0.5),
        'peer_down': nrm(ks[17], (DEPTH, PEER_EXPERTS, D), D ** -0.5),
        'peer_up': nrm(ks[18], (DEPTH, PEER_EXPERTS, D), 0.5),
        'final_g': 1.0 + nrm(ks[19], (D,), 0.02),
    }

def second_block(x, c, ctx, c_ctx, mod_w, mod_b, norm1_g, norm2_g, attn_in_w, attn_out_w, attn_sink,
              gmlp_w_s, gmlp_b_s, pool_w, pool_scale, peer_w_q, peer_sub_keys, peer_down, peer_up, final_g):
    L_ = x.shape[1]
    ROWS = L_ // GRID_W
    t = jnp.arange(ROWS * GRID_W)
    row = (t // GRID_W).astype(jnp.float32)
    col = (t % GRID_W).astype(jnp.float32)
    last_reader = ((DEPTH - 1) // 2) * 2
    xc = ctx
    for l in range(DEPTH):
        has_ctx = l <= last_reader
        keep_ctx = l < last_reader
        m = jax.nn.silu(c) @ mod_w[l] + mod_b[l]
        sh1, sc1, g1, sh2, sc2, g2 = jnp.split(m[:, None, :], N_MOD, axis=-1)
        h = rms_norm_2(x, norm1_g[l]) * (1.0 + sc1) + sh1
        hc = None
        if has_ctx:
            mc = jax.nn.silu(c_ctx) @ mod_w[l] + mod_b[l]
            csh1, csc1, cg1, csh2, csc2, cg2 = jnp.split(mc, N_MOD, axis=-1)
            hc = rms_norm_2(xc, norm1_g[l]) * (1.0 + csc1) + csh1
        if l % 2 == 0:
            e = l // 2
            y, yc = attn_gmlp_mixer(h, hc, attn_in_w[e], attn_out_w[e], attn_sink[e],
                                    gmlp_w_s[e], gmlp_b_s[e], row, col, keep_ctx)
        else:
            o = l // 2
            y = multiscale_pool(h, pool_w[o], pool_scale[o])
            yc = multiscale_pool(hc, pool_w[o], pool_scale[o]) if keep_ctx else None
        x = x + g1 * y
        h2 = rms_norm_2(x, norm2_g[l]) * (1.0 + sc2) + sh2
        x = x + g2 * peer_ffn(h2, peer_w_q[l], peer_sub_keys[l], peer_down[l], peer_up[l])
        if keep_ctx:
            xc = xc + cg1 * yc
            hc2 = rms_norm_2(xc, norm2_g[l]) * (1.0 + csc2) + csh2
            xc = xc + cg2 * peer_ffn(hc2, peer_w_q[l], peer_sub_keys[l], peer_down[l], peer_up[l])
    return rms_norm_2(x, final_g)


def setup_inputs(seed=0):
    out = dict(first_inputs(seed))
    for name, value in second_inputs(seed + 1).items():
        if name != "x":
            out[name + "_2"] = value
    return out


def reference(
    x, norm_ffn1, ffn1_in, ffn1_out, norm_mix, w_in, rwkv_mu, decay_w0, decay_w2, iclr_a0,
    iclr_a2, gate_g2, k_k, k_a, r_k, ln_x_g, ln_x_b, q_gain, k_gain, diff_lambda, subln_g,
    w_branch, w_out, norm_ffn2, ffn2_in, ffn2_out, c_2, ctx_2, c_ctx_2, mod_w_2, mod_b_2,
    norm1_g_2, norm2_g_2, attn_in_w_2, attn_out_w_2, attn_sink_2, gmlp_w_s_2, gmlp_b_s_2,
    pool_w_2, pool_scale_2, peer_w_q_2, peer_sub_keys_2, peer_down_2, peer_up_2, final_g_2,
):
    x = first_block(
        x, norm_ffn1, ffn1_in, ffn1_out, norm_mix, w_in, rwkv_mu, decay_w0, decay_w2, iclr_a0,
        iclr_a2, gate_g2, k_k, k_a, r_k, ln_x_g, ln_x_b, q_gain, k_gain, diff_lambda, subln_g,
        w_branch, w_out, norm_ffn2, ffn2_in, ffn2_out,
    )
    return second_block(
        x, c_2, ctx_2, c_ctx_2, mod_w_2, mod_b_2, norm1_g_2, norm2_g_2, attn_in_w_2,
        attn_out_w_2, attn_sink_2, gmlp_w_s_2, gmlp_b_s_2, pool_w_2, pool_scale_2, peer_w_q_2,
        peer_sub_keys_2, peer_down_2, peer_up_2, final_g_2,
    )


_drawn_inputs = setup_inputs


def setup_inputs(seed=0):
    import zlib

    import numpy as np

    out = dict(_drawn_inputs(seed))
    spreads = {}
    factors = {'norm_ffn1': 3.026,
     'k_k': 5.515,
     'ln_x_g': 5.241,
     'ln_x_b': 4.5,
     'q_gain': 4.32,
     'k_gain': 4.563,
     'subln_g': 3.882,
     'norm_ffn2': 3.954,
     'ctx_2': 3.808,
     'norm1_g_2': 6.81,
     'norm2_g_2': 35.608,
     'attn_sink_2': 8.0,
     'gmlp_b_s_2': 32.531,
     'pool_scale_2': 30.259}
    for name, (base, spread) in spreads.items():
        noise = np.random.default_rng([zlib.crc32(name.encode()), seed]).standard_normal(out[name].shape)
        drawn = base * np.exp(spread * noise) if base else spread * noise
        out[name] = __import__('jax').numpy.asarray(drawn.astype(out[name].dtype))
    for name, factor in factors.items():
        out[name] = (out[name] * factor).astype(out[name].dtype)
    return out
```

```python
import math
from contextlib import ExitStack

import numpy as np

import concourse.bass as bass
from concourse import mybir

F32 = mybir.dt.float32
F32R = mybir.dt.float32r
U32 = mybir.dt.uint32
ALU = mybir.AluOpType
ACT = mybir.ActivationFunctionType
AX = mybir.AxisListType

P = 128
D = 1024
SEQ = 256
NT = SEQ // P
KC = D // P
DEPTH = 2
BANK = 512

DA = D // 2
HA = 64
NHA = DA // HA
LORA = 64
C_RWKV = 3 * DA + 3 * P
C_ATTN = 3 * DA
C_IN = C_RWKV + C_ATTN + 2 * D
D_FF = ((8 * D // 3 + 127) // 128) * 128
NF = D_FF // P
DECAY_SCALE = math.exp(-0.5)
GN_EPS = 64e-5
EPS = 1e-6
CH = 64
NPAIR = NHA // 2
NHB = 4

QW, KVW, AW = 512, 128, 512
IN_W = QW + 2 * KVW + 2 * AW
GROUPS = 8
POOL_WINDOWS = (2, 4, 8, 16)
PH, NK, TOPK = 8, 128, 16
SLOTS = PH * TOPK
FAR = -1e30
RING = 8
TILE = KC * BANK
WPROJ = 344


def constant_table():
    parts = {}
    i = np.arange(P)
    row, col = i[:, None], i[None, :]
    same = row // CH == col // CH
    parts["ident"] = np.eye(P)
    parts["ident2"] = np.concatenate([np.eye(CH)] * 2)
    s = np.arange(SEQ)
    neighbour = 0.5 * (np.abs(s[:, None] - s[None, :]) == 1)
    parts["shift"] = neighbour.reshape(NT, P, NT, P).transpose(1, 0, 2, 3)
    before = [row < col, row > col]
    upto = [row <= col, row >= col]
    parts["cum_incl"] = np.stack([-DECAY_SCALE * (same & u) for u in upto], 1)
    parts["cum_excl"] = np.stack([-DECAY_SCALE * (same & b) for b in before], 1)
    parts["cum_rest"] = np.stack([-DECAY_SCALE * (same & ~u) for u in upto], 1)
    parts["cum_chunk"] = -DECAY_SCALE * (row // CH == np.arange(2)[None, :])
    cr, cc = (row % CH), np.arange(CH)[None, :]
    parts["tri"] = np.stack([np.stack([b, u] * 2, 1) for b, u in ((cr < cc, cr <= cc), (cr > cc, cr >= cc))], 1)
    merge = []
    for g in range(2):
        for lv in range(6):
            b = 1 << lv
            later = (cr > cc) if g == 0 else (cr < cc)
            merge.append((cr // (2 * b) == cc // (2 * b)) & (cr // b != cc // b) & later)
    parts["merge"] = np.stack(merge, 1).reshape(P, 2, 6, CH)
    parts["iota16"] = np.broadcast_to(np.arange(16), (P, 16))
    place, at, flat = {}, 0, []
    for name, a in parts.items():
        a = np.ascontiguousarray(np.asarray(a, np.float32))
        shape = a.shape[1:]
        n = int(np.prod(shape))
        place[name] = (at, n, shape)
        flat.append(a.reshape(P, n))
        at += n
    return np.concatenate(flat, 1), place


def distance_tables():
    q = np.arange(P)[:, None, None] + P * np.arange(NT)[None, :, None]
    dist = np.abs(q - np.arange(SEQ)[None, None, :])
    return (-dist).astype(np.float32), np.where(dist <= 128, 0.0, FAR).astype(np.float32)


def rope_table():
    inv = np.power(np.float32(10000.0), -np.arange(16, dtype=np.float32) / np.float32(16)).astype(np.float32)
    t = np.arange(SEQ)
    ang = np.stack([(t // 64).astype(np.float32)[:, None] * inv, (t % 64).astype(np.float32)[:, None] * inv], 1)
    ang = ang.astype(np.float32).reshape(NT, P, 2, 16).transpose(1, 0, 2, 3)
    return np.ascontiguousarray(np.stack([np.cos(ang), np.sin(ang)], 1).astype(np.float32))


def pool_table():
    t = np.arange(SEQ)
    pool = []
    for w in POOL_WINDOWS:
        lo, hi = np.clip(t - w // 2, 0, SEQ), np.clip(t + w // 2, 0, SEQ)
        m = ((t[:, None] >= lo[None, :]) & (t[:, None] < hi[None, :])) / (hi - lo)[None, :].astype(np.float64)
        pool.append((m - np.eye(SEQ)).reshape(NT, P, SEQ))
    return np.ascontiguousarray(np.stack(pool).transpose(2, 0, 1, 3).astype(np.float32))


class Ops:

    def __init__(self, nc, eng, vector):
        self.nc, self.eng, self.on_vector = nc, eng, vector

    def _order(self, free):
        if not free:
            self.eng.drain()

    def tt(self, out, a, b, op, free=False):
        self._order(free)
        return self.nc.vector.tensor_tensor(out, a, b, op)

    def mul(self, out, a, b, free=False):
        return self.tt(out, a, b, ALU.mult, free)

    def add(self, out, a, b, free=False):
        return self.tt(out, a, b, ALU.add, free)

    def sub(self, out, a, b, free=False):
        return self.tt(out, a, b, ALU.subtract, free)

    def ts(self, out, a, s1, op0, s2=None, op1=None, free=False):
        self._order(free)
        if op1 is None:
            return self.nc.vector.tensor_scalar(out, a, s1, None, op0)
        return self.nc.vector.tensor_scalar(out, a, s1, s2, op0, op1)

    def stt(self, out, a, s, b, op0, op1, free=False):
        self._order(free)
        return self.nc.vector.scalar_tensor_tensor(out=out, in0=a, scalar=s, in1=b, op0=op0, op1=op1)

    def dot(self, out, a, b, total, free=False):
        self._order(free)
        return self.nc.vector.tensor_tensor_reduce(out=out, in0=a, in1=b, scale=1.0, scalar=0.0,
                                                   op0=ALU.mult, op1=ALU.add, accum_out=total)

    def sum(self, out, a, free=False):
        self._order(free)
        return self.nc.vector.reduce_sum(out, a, AX.X)

    def max(self, out, a, free=False):
        self._order(free)
        return self.nc.vector.reduce_max(out, a, AX.X)

    def copy(self, out, a, free=False):
        self._order(free)
        if self.on_vector:
            return self.nc.vector.tensor_copy(out, a)
        return self.nc.scalar.copy(out, a)

    def recip(self, out, a, free=False):
        self._order(free)
        return self.nc.vector.reciprocal(out, a)

    def fn(self, out, a, func, scale=1.0, bias=0.0, total=None, free=False):
        self._order(free)
        kw = {} if total is None else {"accum_out": total}
        return self.nc.scalar.activation(out, a, func, bias=bias, scale=scale, **kw)


class Kernel:

    def __init__(self, nc, ctx, sems):
        self.nc, self.ctx = nc, ctx
        self.sem, self.names = {}, 0
        for name in sems:
            self.sem[name] = ctx.enter_context(nc.semaphore(name))
        nums = [s.num for s in self.sem.values()]
        self.span = range(min(nums), max(nums) + 1)
        assert len(self.span) == len(nums)
        self.rows = [ctx.enter_context(nc.semaphore(f"row{r}")) for r in range(RING)]
        self.row_uses = 0
        self.arrived = [ctx.enter_context(nc.semaphore(f"arrived{u}")) for u in range(2)]
        self.fills = [0, 0]
        self.preloaded = False
        self.table, self.place = constant_table()
        self.table_dram = nc.inline_tensor(self.table, name="shape_constants").ap()
        self.C = self.sb("constants", [P, self.table.shape[1]])
        self.X = self.sb("residual", [P, NT, D])
        self.raw = self.sb("raw_weights", [P, 2, TILE])
        self.ps = ctx.enter_context(nc.psum_tensor("banks", [P, 8, BANK], F32))

    def sb(self, name, shape, dt=F32, ctx=None):
        self.names += 1
        return (ctx or self.ctx).enter_context(self.nc.sbuf_tensor(f"{name}_{self.names}", shape, dt))

    def const(self, name):
        at, n, shape = self.place[name]
        a = self.C[:, at:at + n]
        if len(shape) == 1:
            return a
        names = "abc"[:len(shape)]
        return a.rearrange(f"p ({' '.join(names)}) -> p {' '.join(names)}", **dict(zip(names, shape)))

    def bank(self, b, *dims):
        a = self.ps[:, b, :]
        if dims:
            n = int(np.prod(dims))
            names = "abc"[:len(dims)]
            a = a[:, 0:n].rearrange(f"p ({' '.join(names)}) -> p {' '.join(names)}", **dict(zip(names, dims)))
        return a

    def restart_stream(self):
        for u in range(2):
            self.nc.gpsimd.sem_clear(self.arrived[u])
        self.nc.all_engine_barrier()
        self.fills = [0, 0]

    def clear(self):
        self.nc.gpsimd.sem_clear(self.span)
        self.nc.all_engine_barrier()


def spread(ap, n):
    return ap.unsqueeze(2).to_broadcast([ap.shape[0], ap.shape[1], n])


def over(ap, n):
    return ap.unsqueeze(1).to_broadcast([ap.shape[0], n, ap.shape[1]])


def rows(ap):
    return ap.to_broadcast([P, ap.shape[1]])



def load_stage(k, pairs):
    nc = k.nc
    with nc.Block() as block:
        @block.sync
        def _(sp):
            for dst, src in pairs:
                sp.dma_start(dst, src).then_inc(k.sem["loaded"], 16)
            sp.wait_ge(k.sem["loaded"], 16 * len(pairs))
    k.clear()


def turn_stage(k, jobs):
    nc = k.nc
    turned, copied_v, copied_s = k.sem["turned"], k.sem["copied_v"], k.sem["copied_s"]
    ident = k.const("ident")
    with nc.Block() as block:
        @block.tensor
        def _(pe):
            for n, (sources, _) in enumerate(jobs):
                if n >= 8:
                    pe.wait_ge(copied_s if n % 2 else copied_v, (n - 8) // 2 + 1)
                for c, src in enumerate(sources):
                    last = nc.tensor.transpose(k.bank(n % 8)[:, c * P:c * P + P], src, ident)
                last.then_inc(turned, 1)

        @block.vector
        def _(dve):
            for n, (sources, dst) in enumerate(jobs):
                if n % 2 == 0:
                    dve.wait_ge(turned, n + 1)
                    nc.vector.tensor_copy(dst, k.bank(n % 8, len(sources), P)).then_inc(copied_v, 1)

        @block.scalar
        def _(act):
            for n, (sources, dst) in enumerate(jobs):
                if n % 2 == 1:
                    act.wait_ge(turned, n + 1)
                    nc.scalar.copy(dst, k.bank(n % 8, len(sources), P)).then_inc(copied_s, 1)
    k.clear()


def turn_tokens(k, src, dst, chunks):
    jobs = []
    for j in range(NT):
        for c0 in range(0, chunks, 4):
            cs = range(c0, min(c0 + 4, chunks))
            jobs.append(([src[:, j, c * P:c * P + P] for c in cs],
                         dst[:, c0:c0 + len(cs), j * P:j * P + P]))
    (turn_split_stage if isinstance(dst, Split) else turn_stage)(k, jobs)


def norm_stage(k, x, gain, out, scale_row=None, shift_row=None):
    nc = k.nc
    loaded, squared, rooted = k.sem["loaded"], k.sem["squared"], k.sem["rooted"]
    reduced = k.sem["reduced"]
    with ExitStack() as c:
        g = k.sb("gain", [P, D], ctx=c)
        junk = k.sb("junk", [P, D], ctx=c)
        ss = k.sb("square_sums", [P, NT], ctx=c)
        rs = k.sb("root", [P, NT], ctx=c)
        with nc.Block() as block:
            @block.sync
            def _(sp):
                sp.dma_start(g[:, :], rows(gain)).then_inc(loaded, 16)

            @block.scalar
            def _(act):
                o = Ops(nc, act, False)
                for j in range(NT):
                    o.fn(junk[:, :], x[:, j, :], ACT.Square, total=ss[:, j:j + 1]).then_inc(squared, 1)
                act.wait_ge(reduced, 1)
                o.fn(rs[:, :], rs[:, :], ACT.Sqrt).then_inc(rooted, 1)

            @block.vector
            def _(dve):
                o = Ops(nc, dve, True)
                dve.wait_ge(squared, NT)
                o.ts(rs[:, :], ss[:, :], 1.0 / D, ALU.mult, EPS, ALU.add).then_inc(reduced, 1)
                dve.wait_ge(rooted, 1)
                o.recip(rs[:, :], rs[:, :])
                dve.wait_ge(loaded, 16)
                if scale_row is not None:
                    o.stt(g[:, :], scale_row, 1.0, g[:, :], ALU.add, ALU.mult)
                for j in range(NT):
                    o.stt(out[:, j, :], x[:, j, :], rs[:, j:j + 1], g[:, :], ALU.mult, ALU.mult)
                    if shift_row is not None:
                        o.add(out[:, j, :], out[:, j, :], shift_row)
    k.clear()


def steps(eng, lo, hi, body):
    pairs = (hi - lo) // 2
    if pairs > 1:
        with eng.Fori(0, pairs) as i:
            for d in range(2):
                body(i * 2 + (lo + d), (lo + d) % 2, i + (lo + d) // 2)
    else:
        pairs = 0
    for t in range(lo + 2 * pairs, hi):
        body(t, t % 2, t // 2)


class Split:

    def __init__(self, hi, lo):
        self.hi, self.lo = hi, lo

    def __getitem__(self, at):
        return Split(self.hi[at], self.lo[at])

    def rearrange(self, *a, **kw):
        return Split(self.hi.rearrange(*a, **kw), self.lo.rearrange(*a, **kw))


def split_sb(k, name, shape, ctx):
    return Split(k.sb(name + "_hi", shape, F32R, ctx), k.sb(name + "_lo", shape, F32R, ctx))


def multiply(nc, out, lhs, rhs, start, stop):
    nc.tensor.matmul(out, lhs.hi, rhs.hi, start=start, stop=False)
    nc.tensor.matmul(out, lhs.hi, rhs.lo, start=False, stop=False)
    return nc.tensor.matmul(out, lhs.lo, rhs.hi, start=False, stop=stop)


def turn_split_stage(k, jobs):
    nc = k.nc
    turned, high, low = k.sem["turned"], k.sem["copied_s"], k.sem["copied_v"]
    with nc.Block() as block:
        @block.tensor
        def _(pe):
            for n, (sources, _) in enumerate(jobs):
                if n >= 8:
                    pe.wait_ge(low, n - 7)
                for c, src in enumerate(sources):
                    last = nc.tensor.transpose(k.bank(n % 8)[:, c * P:c * P + P], src, k.const("ident"))
                last.then_inc(turned, 1)

        @block.scalar
        def _(act):
            for n, (sources, dst) in enumerate(jobs):
                act.wait_ge(turned, n + 1)
                nc.scalar.copy(dst.hi, k.bank(n % 8, len(sources), P)).then_inc(high, 1)

        @block.vector
        def _(dve):
            for n, (sources, dst) in enumerate(jobs):
                dve.wait_ge(high, n + 1)
                nc.vector.tensor_tensor(dst.lo, k.bank(n % 8, len(sources), P), dst.hi.bitcast(F32),
                                        ALU.subtract).then_inc(low, 1)
    k.clear()


class Weights:

    def __init__(self, tiles, pieces):
        self.tiles, self.pieces = tiles, pieces

    def load(self, k, sp, t, u):
        for at, shape, src in self.pieces(t):
            n = int(np.prod(shape))
            names = "ab"[:len(shape)]
            dst = k.raw[:, u, at:at + n].rearrange(f"p ({' '.join(names)}) -> p {' '.join(names)}",
                                                   **dict(zip(names, shape)))
            sp.dma_start(dst, src).then_inc(k.arrived[u], 16)

    def per_tile(self):
        return 16 * len(self.pieces(0))


def row_weights(w, tiles, width, kc=KC):
    view = w.rearrange("(k p) n -> p k n", p=P)
    return Weights(tiles, lambda t: [(0, (kc, width), view[:, :, bass.ds(t * width, width)])])


def pair_weights(w, cols):
    view = w.rearrange("(k p) n -> p k n", p=P)
    return Weights(cols // 256, lambda t: [(h * KC * 256, (KC, 256), view[:, :, bass.ds(t * 256 + h * cols, 256)])
                                           for h in range(2)])


def sum_weights(w, kc):
    view = w.rearrange("(k p) n -> p k n", p=P)
    step = 4 if kc % 4 == 0 else 2
    return Weights(kc // step, lambda t: [(0, (step, D), view[:, bass.ds(t * step, step), :])])


def stream(k, block, wts, ahead, size, parts, done, done_per, finish_steps, act_steps=None):
    nc = k.nc
    high, low = k.sem["high"], k.sem["low"]
    tiles, per = wts.tiles, wts.per_tile()
    base = [f * 1 for f in k.fills]
    first = min(2, tiles) if k.preloaded else 0

    @block.sync
    def _(sp):
        for t in range(first, min(2, tiles)):
            wts.load(k, sp, t, t)

        def load(t, u, m):
            sp.wait_ge(low, t - 1)
            wts.load(k, sp, t, u)

        steps(sp, 2, tiles, load)
        if ahead is not None:
            for t in range(min(2, ahead.tiles)):
                sp.wait_ge(low, tiles)
                ahead.load(k, sp, t, t)

    @block.scalar
    def _(act):
        def part(t, u, m):
            act.wait_ge(k.arrived[u], m * per + (base[u] + per))
            if not (isinstance(t, int) and t < 2):
                act.wait_ge(done, t * done_per - done_per)
            nc.scalar.copy(parts.hi[:, u, :], k.raw[:, u, 0:size]).then_inc(high, 1)

        o = Ops(nc, act, False)

        def both(t, u, m):
            part(t, u, m)
            if act_steps is not None:
                act_steps(act, o, t - 1, 1 - u)

        part(0, 0, 0)
        if tiles > 1:
            both(1, 1, 0)
        steps(act, 2, tiles, both)
        if act_steps is not None:
            act_steps(act, o, tiles - 1, (tiles - 1) % 2)

    @block.vector
    def _(dve):
        o = Ops(nc, dve, True)

        def part(t, u, m):
            dve.wait_ge(high, t + 1)
            nc.vector.tensor_tensor(parts.lo[:, u, :], k.raw[:, u, 0:size], parts.hi[:, u, :].bitcast(F32),
                                    ALU.subtract).then_inc(low, 1)

        part(0, 0, 0)

        def both(t, u, m):
            part(t, u, m)
            finish_steps(dve, o, t - 1, 1 - u)

        steps(dve, 1, tiles, both)
        finish_steps(dve, o, tiles - 1, (tiles - 1) % 2)

    for t in range(tiles):
        k.fills[t % 2] += per
    k.preloaded = ahead is not None


def slot(parts, u, **dims):
    names = " ".join(dims)
    return parts[:, u, :].rearrange(f"p ({names}) -> p {names}", **dims)


def linear_stage(k, lhs, wts, width, finish, ahead=None, groups=NT):
    nc = k.nc
    summed, drained = k.sem["summed"], k.sem["drained"]
    size = KC * width
    with ExitStack() as c, nc.Block() as block:
        parts = split_sb(k, "weight_parts", [P, 2, size], c)

        @block.tensor
        def _(pe):
            def tile(t, u, m):
                pe.wait_ge(k.sem["low"], t + 1)
                w = slot(parts, u, k=KC, n=width)
                for j in range(groups):
                    if not (isinstance(t, int) and t < 2):
                        pe.wait_ge(drained, t * groups + (j + 1 - 2 * groups))
                    for kc_ in range(KC):
                        last = multiply(nc, k.bank(u * groups + j)[:, 0:width], lhs(kc_, j), w[:, kc_, :], kc_ == 0, kc_ == KC - 1)
                    last.then_inc(summed, 1)

            for t in range(min(2, wts.tiles)):
                tile(t, t, 0)
            steps(pe, 2, wts.tiles, tile)

        def finish_steps(dve, o, t, u):
            for j in range(groups):
                dve.wait_ge(summed, t * groups + (j + 1))
                finish(o, t, j, k.bank(u * groups + j)[:, 0:width]).then_inc(drained, 1)

        stream(k, block, wts, ahead, size, parts, summed, groups, finish_steps)
    k.clear()


def linear_sum_stage(k, lhsT, kc, wts, finish, ahead=None):
    nc = k.nc
    used = k.sem["used"]
    step = kc // wts.tiles
    with ExitStack() as c, nc.Block() as block:
        parts = split_sb(k, "weight_parts", [P, 2, step * D], c)

        @block.tensor
        def _(pe):
            for t in range(wts.tiles):
                pe.wait_ge(k.sem["low"], t + 1)
                w = slot(parts, t % 2, k=step, n=D)
                for s in range(step):
                    for j in range(NT):
                        for half in range(2):
                            last = multiply(nc, k.bank(2 * j + half), lhsT[:, t * step + s, j * P:j * P + P],
                                            w[:, s, half * BANK:(half + 1) * BANK],
                                            t + s == 0, t == wts.tiles - 1 and s == step - 1)
                last.then_inc(used, 1)

        def finish_steps(dve, o, t, u):
            if isinstance(t, int) and t == wts.tiles - 1:
                dve.wait_ge(used, wts.tiles)
                for j in range(NT):
                    for half in range(2):
                        finish(o, j, half, k.bank(2 * j + half))

        stream(k, block, wts, ahead, step * D, parts, used, 1, finish_steps)
    k.clear()


def linear_turned_stage(k, rhs, wts, halves, finish, pre=None, ahead=None):
    nc = k.nc
    summed, drained, pre_done = k.sem["summed"], k.sem["drained"], k.sem["pre_done"]
    size = halves * KC * 256
    with ExitStack() as c, nc.Block() as block:
        parts = split_sb(k, "weight_parts", [P, 2, size], c)

        @block.tensor
        def _(pe):
            def tile(t, u, m):
                pe.wait_ge(k.sem["low"], t + 1)
                w = slot(parts, u, h=halves, k=KC, n=256)
                for s in range(2):
                    if not (isinstance(t, int) and t < 2):
                        pe.wait_ge(drained, t * 2 + (s - 3))
                    for h in range(halves):
                        for kc_ in range(KC):
                            last = multiply(nc, k.bank(2 * u + s)[:, h * SEQ:(h + 1) * SEQ],
                                            w[:, h, kc_, s * P:s * P + P], rhs[:, kc_, :], kc_ == 0, kc_ == KC - 1)
                    last.then_inc(summed, 1)

            for t in range(min(2, wts.tiles)):
                tile(t, t, 0)
            steps(pe, 2, wts.tiles, tile)

        def finish_steps(dve, o, t, u):
            for s in range(2):
                v = 2 * u + s
                dve.wait_ge(summed if pre is None else pre_done, t * 2 + (s + 1))
                finish(o, t * 2 + s, v, k.bank(v)).then_inc(drained, 1)

        def act_steps(act, o, t, u):
            for s in range(2):
                v = 2 * u + s
                act.wait_ge(summed, t * 2 + (s + 1))
                pre(o, t * 2 + s, v, k.bank(v)).then_inc(pre_done, 1)

        stream(k, block, wts, ahead, size, parts, summed, 2, finish_steps, None if pre is None else act_steps)
    k.clear()



def swiglu(k, gain, w_in, w_out, ahead):
    with ExitStack() as c:
        hT = split_sb(k, "normedT", [P, KC, SEQ], c)
        with ExitStack() as c1:
            h = k.sb("normed", [P, NT, D], ctx=c1)
            norm_stage(k, k.X, gain, h)
            turn_tokens(k, h, hT, KC)
        actT = split_sb(k, "hiddenT", [P, NF, SEQ], c)
        gated = k.sb("silu_gate", [P, 4, SEQ], ctx=c)
        hidden = k.sb("hidden", [P, 4, SEQ], ctx=c)

        def pre(o, n, v, bank):
            return o.fn(gated[:, v, :], bank[:, 0:SEQ], ACT.Silu, free=True)

        def finish(o, n, v, bank):
            o.mul(hidden[:, v, :], gated[:, v, :], bank[:, SEQ:], free=True)
            hi, lo = (x[:, bass.ds(n, 1), :].rearrange("p a n -> p (a n)") for x in (actT.hi, actT.lo))
            o.copy(hi, hidden[:, v, :])
            return o.sub(lo, hidden[:, v, :], hi.bitcast(F32))

        linear_turned_stage(k, hT, w_in, 2, finish, pre, w_out)

        def residual(o, j, half, bank):
            x = k.X[:, j, half * BANK:(half + 1) * BANK]
            return o.stt(x, bank, 0.5, x, ALU.mult, ALU.add, free=True)

        linear_sum_stage(k, actT, NF, w_out, residual, ahead)


def project(k, gain, wts, width, out, mod=(None, None), ahead=None):
    with ExitStack() as c:
        h = k.sb("normed", [P, NT, D], ctx=c)
        hT = split_sb(k, "normedT", [P, KC, SEQ], c)
        norm_stage(k, k.X, gain, h, *mod)
        turn_tokens(k, h, hT, KC)
        linear_stage(k, lambda c_, j: hT[:, c_, j * P:j * P + P], wts, width,
                     lambda o, t, j, bank: o.copy(out[:, j, bass.ds(t * width, width)], bank, free=True), ahead)


def rwkv(k, proj, mu, w0, w2, a0, a2, g2, k_k, k_a, r_k, ln_g, ln_b, out):
    nc = k.nc
    y = out
    with ExitStack() as c:
        p = proj
        sig = k.sb("decay_sigmoid", [P, 2, NT, DA], ctx=c)
        kk = k.sb("kk", [P, NT, DA], ctx=c)
        kd = k.sb("k_dir", [P, 2, NT, DA], ctx=c)
        beta = k.sb("beta", [P, 2, NT, DA], ctx=c)
        bonus = k.sb("bonus", [P, NT, NHA], ctx=c)
        cw = C_RWKV // 4
        with ExitStack() as c1:
            mur = k.sb("mu", [P, C_RWKV], ctx=c1)
            delta = k.sb("delta", [P, 4, cw], ctx=c1)
            loaded, summed = k.sem["loaded"], k.sem["summed"]
            with nc.Block() as block:
                @block.sync
                def _(sp):
                    sp.dma_start(mur[:, :], rows(mu)).then_inc(loaded, 16)

                @block.tensor
                def _(pe):
                    for j in range(NT):
                        for q in range(4):
                            for s in range(NT):
                                last = nc.tensor.matmul(k.bank(4 * j + q)[:, 0:cw], k.const("shift")[:, s, j, :],
                                                        proj[:, s, q * cw:(q + 1) * cw], start=s == 0, stop=s == NT - 1)
                            last.then_inc(summed, 1)

                @block.vector
                def _(dve):
                    o = Ops(nc, dve, True)
                    dve.wait_ge(loaded, 16)
                    dve.wait_ge(summed, 8)
                    for j in range(NT):
                        for q in range(4):
                            cs = slice(q * cw, (q + 1) * cw)
                            o.sub(delta[:, q, :], k.bank(4 * j + q)[:, 0:cw], proj[:, j, cs], free=j == 0)
                        o.mul(delta[:, :, :], delta[:, :, :], mur[:, :].rearrange("p (q n) -> p q n", q=4))
                        o.add(proj[:, j, 0:C_RWKV], proj[:, j, 0:C_RWKV], delta[:, :, :].rearrange("p q n -> p (q n)"))
            k.clear()
        r, kx, v = (p[:, :, n * DA:(n + 1) * DA] for n in range(3))
        gate = kx
        with ExitStack() as c1:
            low = k.sb("low", [P, NT, 3 * P], ctx=c1)
            lowT = k.sb("lowT", [P, 3, SEQ], ctx=c1)
            wl = k.sb("lora_w", [P, 3, DA], ctx=c1)
            bias = k.sb("lora_bias", [P, 2, 2, DA], ctx=c1)
            per = k.sb("per_channel", [P, 3, DA], ctx=c1)
            a = k.sb("iclr", [P, 2, NT, DA], ctx=c1)
            pre = k.sb("before_sigmoid", [P, 2, DA], ctx=c1)
            t1 = k.sb("scratch", [P, NT, DA], ctx=c1)
            nrm = k.sb("norms", [P, NT, NHA], ctx=c1)
            gate_now = k.sb("gate_now", [P, NT, DA], ctx=c1)
            with nc.Block() as block:
                @block.sync
                def _(sp):
                    ld = k.sem["loaded"]
                    pairs = [(wl[:, 0, :], w2), (wl[:, 1, :], a2), (wl[:, 2, :], g2),
                             (bias[:, 0, 0], rows(w0[0])), (bias[:, 0, 1], rows(w0[1])),
                             (bias[:, 1, 0], rows(a0[0])), (bias[:, 1, 1], rows(a0[1])),
                             (per[:, 0], rows(k_k)), (per[:, 1], rows(k_a)), (per[:, 2], rows(r_k))]
                    for dst, src in pairs:
                        sp.dma_start(dst, src).then_inc(ld, 16)
                    sp.wait_ge(ld, 16 * len(pairs))

                @block.scalar
                def _(act):
                    o = Ops(nc, act, False)
                    l0 = 3 * DA
                    o.fn(low[:, :, 0:P], p[:, :, l0:l0 + P], ACT.Tanh, free=True)
                    o.copy(low[:, :, P:2 * P], p[:, :, l0 + P:l0 + 2 * P], free=True)
                    o.fn(low[:, :, 2 * P:], p[:, :, l0 + 2 * P:C_RWKV], ACT.Sigmoid, free=True)
            k.clear()
            turn_tokens(k, low, lowT, 3)
            jobs = [(what, g, j) for what in range(2) for g in range(2) for j in range(NT)]
            summed, biased, squashed = k.sem["summed"], k.sem["biased"], k.sem["squashed"]
            with nc.Block() as block:
                @block.tensor
                def _(pe):
                    for n, (what, g, j) in enumerate(jobs):
                        nc.tensor.matmul(k.bank(n), lowT[g * LORA:(g + 1) * LORA, what, j * P:j * P + P],
                                         wl[g * LORA:(g + 1) * LORA, what, :], start=True, stop=True).then_inc(summed, 1)
                    for j in range(NT):
                        pe.wait_ge(biased, 2)
                        nc.tensor.matmul(k.bank(j), lowT[:, 2, j * P:j * P + P], wl[:, 2, :],
                                         start=True, stop=True).then_inc(summed, 1)

                @block.scalar
                def _(act):
                    o = Ops(nc, act, False)
                    for n, (what, g, j) in enumerate(jobs):
                        act.wait_ge(biased, n + 1)
                        dst = (sig, a)[what]
                        o.fn(dst[:, g, j, :], pre[:, n % 2, :], ACT.Sigmoid, free=True).then_inc(squashed, 1)

                @block.vector
                def _(dve):
                    o = Ops(nc, dve, True)
                    for n, (what, g, j) in enumerate(jobs):
                        dve.wait_ge(summed, n + 1)
                        if n >= 2:
                            dve.wait_ge(squashed, n - 1)
                        o.add(pre[:, n % 2, :], k.bank(n), bias[:, what, g, :], free=True).then_inc(biased, 1)
                    for j in range(NT):
                        dve.wait_ge(summed, len(jobs) + j + 1)
                        o.copy(gate_now[:, j, :], k.bank(j), free=True)
                    for j in range(NT):
                        o.mul(kk[:, j, :], kx[:, j, :], per[:, 0, :])
                        o.mul(t1[:, j, :], kk[:, j, :], kk[:, j, :])
                        o.sum(nrm[:, j, :], t1[:, j, :].rearrange("p (h n) -> p h n", h=NHA))
                    o.copy(nrm[:, :, :], nrm[:, :, :]).then_inc(k.sem["reduced"], 1)
            k.clear()
            with nc.Block() as block:
                @block.scalar
                def _(act):
                    nc.scalar.activation(nrm[:, :, :], nrm[:, :, :], ACT.Sqrt).then_inc(k.sem["rooted"], 1)

                @block.vector
                def _(dve):
                    o = Ops(nc, dve, True)
                    dve.wait_ge(k.sem["rooted"], 1)
                    o.ts(nrm[:, :, :], nrm[:, :, :], 1e-12, ALU.max)
                    o.recip(nrm[:, :, :], nrm[:, :, :])
                    for j in range(NT):
                        h3 = kk[:, j, :].rearrange("p (h n) -> p h n", h=NHA)
                        o.mul(h3, h3, spread(nrm[:, j, :], HA))
                    for g in range(2):
                        for j in range(NT):
                            o.stt(kd[:, g, j, :], a[:, g, j, :], -1.0, per[:, 1, :], ALU.add, ALU.mult)
                            o.stt(kd[:, g, j, :], kd[:, g, j, :], 1.0, kx[:, j, :], ALU.add, ALU.mult)
                            o.mul(beta[:, g, j, :], kk[:, j, :], a[:, g, j, :], free=True)
                    for j in range(NT):
                        o.add(t1[:, j, :], kd[:, 0, j, :], kd[:, 1, j, :])
                        o.mul(t1[:, j, :], t1[:, j, :], r[:, j, :])
                        o.mul(t1[:, j, :], t1[:, j, :], per[:, 2, :])
                        o.sum(bonus[:, j, :], t1[:, j, :].rearrange("p (h n) -> p h n", h=NHA))
                        o.copy(gate[:, j, :], gate_now[:, j, :], free=True)
            k.clear()
        qT = k.sb("queryT", [P, 2, NT, 2, NPAIR, CH], ctx=c)
        move = k.sb("transition", [P, 2, NT, 2, NPAIR, HA], ctx=c)
        fresh = k.sb("fresh_state", [P, 2, NT, 2, NPAIR, HA], ctx=c)
        rwkv_tiles(k, r, kk, kd, beta, v, sig, qT, move, fresh, y)
        rwkv_states(k, qT, move, fresh, y)
        with ExitStack() as c1:
            lg = k.sb("ln_gain", [P, DA], ctx=c1)
            lb = k.sb("ln_bias", [P, DA], ctx=c1)
            t1 = k.sb("scratch", [P, NT, DA], ctx=c1)
            mean = k.sb("mean", [P, NT, NHA], ctx=c1)
            var = k.sb("var", [P, NT, NHA], ctx=c1)
            with nc.Block() as block:
                @block.sync
                def _(sp):
                    sp.dma_start(lg[:, :], rows(ln_g)).then_inc(k.sem["loaded"], 16)
                    sp.dma_start(lb[:, :], rows(ln_b)).then_inc(k.sem["loaded"], 16)

                @block.scalar
                def _(act):
                    act.wait_ge(k.sem["reduced"], 1)
                    nc.scalar.activation(var[:, :, :], var[:, :, :], ACT.Sqrt).then_inc(k.sem["rooted"], 1)

                @block.vector
                def _(dve):
                    o = Ops(nc, dve, True)
                    for j in range(NT):
                        h3 = y[:, j, :].rearrange("p (h n) -> p h n", h=NHA)
                        t3 = t1[:, j, :].rearrange("p (h n) -> p h n", h=NHA)
                        o.sum(mean[:, j, :], h3)
                        o.ts(mean[:, j, :], mean[:, j, :], 1.0 / HA, ALU.mult)
                        o.sub(h3, h3, spread(mean[:, j, :], HA))
                        o.mul(t3, h3, h3)
                        o.sum(var[:, j, :], t3)
                    o.ts(var[:, :, :], var[:, :, :], 1.0 / HA, ALU.mult, GN_EPS, ALU.add).then_inc(k.sem["reduced"], 1)
                    dve.wait_ge(k.sem["rooted"], 1)
                    o.recip(var[:, :, :], var[:, :, :])
                    dve.wait_ge(k.sem["loaded"], 32)
                    for j in range(NT):
                        h3 = y[:, j, :].rearrange("p (h n) -> p h n", h=NHA)
                        t3 = t1[:, j, :].rearrange("p (h n) -> p h n", h=NHA)
                        o.mul(h3, h3, spread(var[:, j, :], HA))
                        o.mul(y[:, j, :], y[:, j, :], lg[:, :])
                        o.add(y[:, j, :], y[:, j, :], lb[:, :])
                        o.mul(t3, v[:, j, :].rearrange("p (h n) -> p h n", h=NHA), spread(bonus[:, j, :], HA))
                        o.add(y[:, j, :], y[:, j, :], t1[:, j, :])
                        o.mul(y[:, j, :], y[:, j, :], gate[:, j, :])
            k.clear()


class Milestones:

    def __init__(self, names):
        self.names = names

    def count(self, unit, name):
        return unit * len(self.names) + self.names.index(name) + 1


LEVELS = range(1, 6)
ON_PE = Milestones(["excl", "incl", "rest", "chunk"] + [f"turn{q}" for q in range(4)] + [f"score{b}" for b in range(4)]
                   + ["natural", "akv"] + [f"{w}{n}" for n in LEVELS for w in ("g", "c")]
                   + ["xa", "u0", "qm", "y", "fresh"])
ON_ACT = Milestones(["excl", "incl", "inverse", "rest", "chunk"] + [f"turn{q}" for q in range(4)])
ON_DVE = Milestones(["scaled", "ends"] + [f"score{b}" for b in range(4)] + ["x0", "akv"]
                    + [f"{w}{n}" for n in LEVELS for w in ("g", "x")] + ["xa", "u0", "qm", "y", "fresh"])


def rwkv_tiles(k, r, kk, kd, beta, v, sig, qT, move, fresh, y):
    nc = k.nc
    C = k.const
    A, R, B, K = range(4)
    heads = [2 * q + e for e in range(2) for q in range(NPAIR)]
    cols = [slice(h * HA, h * HA + HA) for h in range(NHA)]
    chunks = [slice(ch * CH, ch * CH + CH) for ch in range(2)]
    on_pe, on_act, on_dve = ([k.sem[f"{e}_lane{g}"] for g in range(2)] for e in ("pe", "act", "dve"))

    def grid(ap, *dims):
        names = "abc"[:len(dims)]
        return ap.rearrange(f"p ({' '.join(names)}) -> p {' '.join(names)}", **dict(zip(names, dims)))

    with ExitStack() as c:
        lanes = []
        for g in range(2):
            if g == 0:
                ex = k.sb("decays", [P, 4, DA], ctx=c)
                m = k.sb("scaled", [P, 4, DA], ctx=c)
                mT = k.sb("scaledT", [P, NPAIR, 4, P], ctx=c)
                s1 = k.sb("scores", [P, NHA, 4, CH], ctx=c)
            else:
                half = TILE // 2
                mT = grid(k.raw[:, 0, 0:half], NPAIR, 4, P)
                s1 = grid(k.raw[:, 0, half:], NHA, 4, CH)
                ex = grid(k.raw[:, 1, 0:half], 4, DA)
                m = grid(k.raw[:, 1, half:], 4, DA)
            ends = k.sb("ends", [P, 2, DA], ctx=c)
            x = k.sb("inverse", [P, NHA, CH], ctx=c)
            dw = k.sb("decay_diagonal", [P, 2, NPAIR, HA], ctx=c)
            wc = k.sb("chunk_decay", [P, 2, NPAIR], ctx=c)
            xT, gm = (grid(ex[:, n, :], NHA, CH) for n in range(2))
            akv, xa, u0 = ex[:, 2, :], ex[:, 3, :], m[:, R, :]
            lanes.append((ex, m, mT, s1, ends, x, dw, wc, xT, gm, akv, xa, u0))

        with nc.Block() as block:
            @block.tensor
            def _(pe):
                def wait_dve(g, j, name):
                    pe.wait_ge(on_dve[g], ON_DVE.count(j, name))

                def wait_act(g, j, name):
                    pe.wait_ge(on_act[g], ON_ACT.count(j, name))

                for j in range(NT):
                    for g, (ex, m, mT, s1, ends, x, dw, wc, xT, gm, akv, xa, u0) in enumerate(lanes):
                        bank = [k.bank(4 * g + b) for b in range(4)]
                        if j:
                            wait_dve(g, j - 1, "fresh")
                        sg = sig[:, g, j, :]
                        for n, name in enumerate(("cum_excl", "cum_incl", "cum_rest")):
                            nc.tensor.matmul(bank[n], C(name)[:, g, :], sg, start=True, stop=True).then_inc(on_pe[g], 1)
                        for q in range(NPAIR):
                            last = nc.tensor.matmul(bank[3][:, 2 * q:2 * q + 2], sg[:, q * P:q * P + P], C("cum_chunk"),
                                                    start=True, stop=True)
                        last.then_inc(on_pe[g], 1)
                    for g, (ex, m, mT, s1, ends, x, dw, wc, xT, gm, akv, xa, u0) in enumerate(lanes):
                        wait_act(g, j, "chunk")
                        wait_dve(g, j, "scaled")
                        for q in range(NPAIR):
                            for n in range(4):
                                last = nc.tensor.transpose(k.bank(4 * g + q)[:, n * P:n * P + P],
                                                           m[:, n, q * P:q * P + P], C("ident"))
                            last.then_inc(on_pe[g], 1)
                    for g, (ex, m, mT, s1, ends, x, dw, wc, xT, gm, akv, xa, u0) in enumerate(lanes):
                        wait_act(g, j, "turn3")
                        for b in range(4):
                            e, qh = divmod(b, 2)
                            ks = slice(e * HA, e * HA + HA)
                            for i2 in range(2):
                                for cs in chunks:
                                    for w in range(2):
                                        at = (2 * i2 + w) * 2 * CH
                                        last = nc.tensor.matmul(k.bank(4 * g + b)[cs, at:at + 2 * CH],
                                                                mT[ks, 2 * qh + i2, (B, K)[w], cs],
                                                                mT[ks, 2 * qh + i2, A:R + 1, cs], start=True, stop=True)
                            last.then_inc(on_pe[g], 1)
                    for g, (ex, m, mT, s1, ends, x, dw, wc, xT, gm, akv, xa, u0) in enumerate(lanes):
                        wait_dve(g, j, "score1")
                        for n, h in enumerate(heads):
                            e, q = divmod(n, NPAIR)
                            ks = slice(e * HA, e * HA + HA)
                            for cs in chunks:
                                last = nc.tensor.matmul(k.bank(4 * g + e)[cs, q * CH:q * CH + CH], mT[ks, q, A, cs],
                                                        mT[ks, q, B, cs], start=True, stop=True)
                        last.then_inc(on_pe[g], 1)
                        wait_dve(g, j, "score3")
                        for n, h in enumerate(heads):
                            for cs in chunks:
                                last = nc.tensor.matmul(k.bank(4 * g + 3)[cs, cols[h]], s1[cs, n, 2, :], v[cs, j, cols[h]],
                                                        start=True, stop=True)
                        last.then_inc(on_pe[g], 1)
                    for n in LEVELS:
                        for g, (ex, m, mT, s1, ends, x, dw, wc, xT, gm, akv, xa, u0) in enumerate(lanes):
                            wait_dve(g, j, f"x{n - 1}")
                            for h in range(NHA):
                                for cs in chunks:
                                    last = nc.tensor.matmul(k.bank(4 * g)[cs, cols[h]], s1[cs, h, 0, :], x[cs, h, :],
                                                            start=True, stop=True)
                            last.then_inc(on_pe[g], 1)
                        for g, (ex, m, mT, s1, ends, x, dw, wc, xT, gm, akv, xa, u0) in enumerate(lanes):
                            wait_dve(g, j, f"g{n}")
                            for h in range(NHA):
                                for cs in chunks:
                                    if n < LEVELS[-1]:
                                        nc.tensor.matmul(k.bank(4 * g + 1)[cs, cols[h]], xT[cs, h, :], gm[cs, h, :],
                                                         start=True, stop=True)
                                    last = nc.tensor.matmul(k.bank(4 * g + 2)[cs, cols[h]], gm[cs, h, :], xT[cs, h, :],
                                                            start=True, stop=True)
                            last.then_inc(on_pe[g], 1)
                    for g, (ex, m, mT, s1, ends, x, dw, wc, xT, gm, akv, xa, u0) in enumerate(lanes):
                        wait_dve(g, j, f"x{LEVELS[-1]}")
                        for b, src in ((0, m[:, A, :]), (1, akv)):
                            if b:
                                wait_dve(g, j, "akv")
                            for n, h in enumerate(heads):
                                for cs in chunks:
                                    last = nc.tensor.matmul(k.bank(4 * g + b)[cs, cols[h]], xT[cs, n, :], src[cs, cols[h]],
                                                            start=True, stop=True)
                            last.then_inc(on_pe[g], 1)
                    for g, (ex, m, mT, s1, ends, x, dw, wc, xT, gm, akv, xa, u0) in enumerate(lanes):
                        wait_dve(g, j, "xa")
                        for ch, cs in enumerate(chunks):
                            for n, h in enumerate(heads):
                                e, q = divmod(n, NPAIR)
                                ks = slice(e * HA, e * HA + HA)
                                out = k.bank(4 * g + 2 + ch)
                                nc.tensor.matmul(out[ks, q * CH:q * CH + CH], xa[cs, cols[h]], s1[cs, n, 1, :],
                                                 start=True, stop=True)
                                last = nc.tensor.matmul(out[ks, (NPAIR + q) * HA:(NPAIR + q + 1) * HA], xa[cs, cols[h]],
                                                        ends[cs, 0, cols[h]], start=True, stop=True)
                        last.then_inc(on_pe[g], 1)
                    for g, (ex, m, mT, s1, ends, x, dw, wc, xT, gm, akv, xa, u0) in enumerate(lanes):
                        wait_dve(g, j, "u0")
                        for n, h in enumerate(heads):
                            for cs in chunks:
                                out = k.bank(4 * g)[cs, cols[h]]
                                nc.tensor.matmul(out, s1[cs, n, 1, :], u0[cs, cols[h]], start=True, stop=False)
                                last = nc.tensor.matmul(out, s1[cs, n, 3, :], v[cs, j, cols[h]], start=False, stop=True)
                        last.then_inc(on_pe[g], 1)
                        wait_dve(g, j, "qm")
                        for ch, cs in enumerate(chunks):
                            for n, h in enumerate(heads):
                                e, q = divmod(n, NPAIR)
                                ks = slice(e * HA, e * HA + HA)
                                out = k.bank(4 * g + 1 + ch)[ks, q * HA:q * HA + HA]
                                nc.tensor.matmul(out, ends[cs, 0, cols[h]], u0[cs, cols[h]], start=True, stop=False)
                                last = nc.tensor.matmul(out, ends[cs, 1, cols[h]], v[cs, j, cols[h]], start=False, stop=True)
                        last.then_inc(on_pe[g], 1)

            @block.scalar
            def _(act):
                o = Ops(nc, act, False)
                for j in range(NT):
                    for g, (ex, m, mT, s1, ends, x, dw, wc, xT, gm, akv, xa, u0) in enumerate(lanes):
                        if j:
                            act.wait_ge(on_pe[g], ON_PE.count(j - 1, "fresh"))
                        for n, (b, name, scale) in enumerate(((0, "excl", 1.0), (1, "incl", 1.0), (1, "incl", -1.0),
                                                              (2, "rest", 1.0))):
                            act.wait_ge(on_pe[g], ON_PE.count(j, name))
                            o.fn(ex[:, n], k.bank(4 * g + b), ACT.Exp, scale=scale, free=True).then_inc(on_act[g], 1)
                        act.wait_ge(on_pe[g], ON_PE.count(j, "chunk"))
                        o.fn(wc[:, :, :].rearrange("p c q -> p q c"), k.bank(4 * g + 3, NPAIR, 2), ACT.Exp,
                             free=True).then_inc(on_act[g], 1)
                    for g, (ex, m, mT, s1, ends, x, dw, wc, xT, gm, akv, xa, u0) in enumerate(lanes):
                        for q in range(NPAIR):
                            act.wait_ge(on_pe[g], ON_PE.count(j, f"turn{q}"))
                            o.copy(mT[:, q], k.bank(4 * g + q, 4, P), free=True).then_inc(on_act[g], 1)

            @block.vector
            def _(dve):
                o = Ops(nc, dve, True)

                def wait_pe(g, j, name):
                    dve.wait_ge(on_pe[g], ON_PE.count(j, name))

                def wait_act(g, j, name):
                    dve.wait_ge(on_act[g], ON_ACT.count(j, name))

                for j in range(NT):
                    for g, (ex, m, mT, s1, ends, x, dw, wc, xT, gm, akv, xa, u0) in enumerate(lanes):
                        wait_act(g, j, "excl")
                        o.stt(m[:, A], kk[:, j, :], -1.0, ex[:, 0], ALU.mult, ALU.mult, free=True)
                        wait_act(g, j, "incl")
                        o.mul(m[:, R], r[:, j, :], ex[:, 1], free=True)
                        wait_act(g, j, "inverse")
                        o.mul(m[:, B], beta[:, g, j, :], ex[:, 2], free=True)
                        o.mul(m[:, K], kd[:, g, j, :], ex[:, 2], free=True)
                        dve.drain()
                        dve.sem_inc(on_dve[g], 1)
                        wait_act(g, j, "chunk")
                        o.mul(ends[:, 0], beta[:, g, j, :], ex[:, 3], free=True)
                        o.mul(ends[:, 1], kd[:, g, j, :], ex[:, 3], free=True)
                        for ch in range(2):
                            last = o.mul(dw[:, ch], over(C("ident2"), NPAIR), spread(wc[:, ch, :], HA), free=True)
                        last.then_inc(on_dve[g], 1)
                    for g, (ex, m, mT, s1, ends, x, dw, wc, xT, gm, akv, xa, u0) in enumerate(lanes):
                        for b in range(4):
                            wait_pe(g, j, f"score{b}")
                            for i2 in range(2):
                                last = o.mul(s1[:, 2 * b + i2], k.bank(4 * g + b, 2, 4, CH)[:, i2], C("tri")[:, g], free=True)
                            last.then_inc(on_dve[g], 1)
                    for g, (ex, m, mT, s1, ends, x, dw, wc, xT, gm, akv, xa, u0) in enumerate(lanes):
                        wait_pe(g, j, "natural")
                        for e in range(2):
                            o.mul(x[:, 4 * e:4 * e + 4], k.bank(4 * g + e, 4, CH), over(C("merge")[:, g, 0, :], 4), free=e > 0)
                        o.mul(xT, s1[:, :, 0, :], over(C("merge")[:, 1 - g, 0, :], NHA), free=True)
                        o.add(x[:, :, :], x[:, :, :], over(C("ident2"), NHA))
                        o.add(xT, xT, over(C("ident2"), NHA))
                        dve.drain()
                        dve.sem_inc(on_dve[g], 1)
                        wait_pe(g, j, "akv")
                        o.copy(akv, k.bank(4 * g + 3), free=True).then_inc(on_dve[g], 1)
                    for n in LEVELS:
                        for g, (ex, m, mT, s1, ends, x, dw, wc, xT, gm, akv, xa, u0) in enumerate(lanes):
                            wait_pe(g, j, f"g{n}")
                            o.mul(gm, k.bank(4 * g, NHA, CH), over(C("merge")[:, g, n, :], NHA), free=True).then_inc(on_dve[g], 1)
                        for g, (ex, m, mT, s1, ends, x, dw, wc, xT, gm, akv, xa, u0) in enumerate(lanes):
                            wait_pe(g, j, f"c{n}")
                            if n < LEVELS[-1]:
                                o.add(x[:, :, :], x[:, :, :], k.bank(4 * g + 1, NHA, CH), free=True)
                            o.add(xT, xT, k.bank(4 * g + 2, NHA, CH))
                            dve.drain()
                            dve.sem_inc(on_dve[g], 1)
                    for g, (ex, m, mT, s1, ends, x, dw, wc, xT, gm, akv, xa, u0) in enumerate(lanes):
                        wait_pe(g, j, "xa")
                        o.copy(xa, k.bank(4 * g), free=True).then_inc(on_dve[g], 1)
                        wait_pe(g, j, "u0")
                        o.copy(u0, k.bank(4 * g + 1), free=True).then_inc(on_dve[g], 1)
                    for g, (ex, m, mT, s1, ends, x, dw, wc, xT, gm, akv, xa, u0) in enumerate(lanes):
                        wait_pe(g, j, "qm")
                        for ch, cs in enumerate(chunks):
                            both = k.bank(4 * g + 2 + ch, 2, NPAIR, CH)
                            o.add(qT[:, g, j, ch], both[:, 0], mT[:, :, R, cs], free=True)
                            last = o.add(move[:, g, j, ch], both[:, 1], dw[:, ch], free=True)
                        last.then_inc(on_dve[g], 1)
                    for g, (ex, m, mT, s1, ends, x, dw, wc, xT, gm, akv, xa, u0) in enumerate(lanes):
                        wait_pe(g, j, "y")
                        if g == 0:
                            o.copy(y[:, j, :], k.bank(4 * g), free=True).then_inc(on_dve[g], 1)
                        else:
                            o.add(y[:, j, :], y[:, j, :], k.bank(4 * g)).then_inc(on_dve[g], 1)
                        wait_pe(g, j, "fresh")
                        for ch in range(2):
                            last = o.copy(fresh[:, g, j, ch], k.bank(4 * g + 1 + ch)[:, 0:NPAIR * HA].rearrange(
                                "p (q n) -> p q n", n=HA), free=True)
                        last.then_inc(on_dve[g], 1)
        k.clear()


def rwkv_states(k, qT, move, fresh, y):
    nc = k.nc
    order = [[0, 1, 2, 3], [3, 2, 1, 0]]
    done, stored = k.sem["done"], k.sem["stored"]
    with ExitStack() as c:
        st = k.sb("states", [P, 3, 2, NPAIR, HA], ctx=c)
        with nc.Block() as block:
            @block.tensor
            def _(pe):
                for s in range(1, 3):
                    pe.wait_ge(stored, s)
                    for g in range(2):
                        jj, cc = divmod(order[g][s], 2)
                        for h in range(NHA):
                            q, ks = h // 2, slice(h % 2 * HA, h % 2 * HA + HA)
                            last = nc.tensor.matmul(k.bank(s - 1, 2, NPAIR, HA)[ks, g, q, :], move[ks, g, jj, cc, q, :],
                                                    st[ks, s - 1, g, q, :], start=True, stop=True)
                    last.then_inc(done, 1)
                pe.wait_ge(stored, 3)
                for ch in range(4):
                    jj, cc = divmod(ch, 2)
                    gs = [g for g in range(2) if order[g].index(ch)]
                    for h in range(NHA):
                        q, ks = h // 2, slice(h % 2 * HA, h % 2 * HA + HA)
                        for g in gs:
                            last = nc.tensor.matmul(k.bank(2 + 2 * jj + h % 2)[cc * CH:cc * CH + CH, q * HA:q * HA + HA],
                                                    qT[ks, g, jj, cc, q, :],
                                                    st[ks, order[g].index(ch) - 1, g, q, :],
                                                    start=g == gs[0], stop=g == gs[-1])
                last.then_inc(done, 1)

            @block.vector
            def _(dve):
                o = Ops(nc, dve, True)
                for g in range(2):
                    jj, cc = divmod(order[g][0], 2)
                    last = o.copy(st[:, 0, g], fresh[:, g, jj, cc], free=True)
                dve.drain()
                dve.sem_inc(stored, 1)
                for s in range(1, 3):
                    dve.wait_ge(done, s)
                    for g in range(2):
                        jj, cc = divmod(order[g][s], 2)
                        o.add(st[:, s, g], k.bank(s - 1, 2, NPAIR, HA)[:, g], fresh[:, g, jj, cc], free=True)
                    dve.drain()
                    dve.sem_inc(stored, 1)
                dve.wait_ge(done, 3)
                for j in range(NT):
                    for par in range(2):
                        yh = y[:, j, :].rearrange("p (q e n) -> p q e n", e=2, n=HA)[:, :, par, :]
                        o.add(yh, yh, k.bank(2 + 2 * j + par, NPAIR, HA), free=True)
        k.clear()


def head_norm(k, x, heads, width, gain, scale, c):
    nc = k.nc
    gr = k.sb("head_gain", [P, width], ctx=c)
    ss = k.sb("head_squares", [P, NT, heads], ctx=c)
    sq = k.sb("head_scratch", [P, heads * width], ctx=c)
    with nc.Block() as block:
        @block.sync
        def _(sp):
            sp.dma_start(gr[:, :], rows(gain)).then_inc(k.sem["loaded"], 16)

        @block.scalar
        def _(act):
            act.wait_ge(k.sem["reduced"], 1)
            nc.scalar.activation(ss[:, :, :], ss[:, :, :], ACT.Sqrt).then_inc(k.sem["rooted"], 1)

        @block.vector
        def _(dve):
            o = Ops(nc, dve, True)
            for j in range(NT):
                h3 = x[:, j, :].rearrange("p (h n) -> p h n", h=heads)
                s3 = sq[:, :].rearrange("p (h n) -> p h n", h=heads)
                o.mul(s3, h3, h3)
                o.sum(ss[:, j, :], s3)
            o.ts(ss[:, :, :], ss[:, :, :], 1.0 / width, ALU.mult, EPS, ALU.add).then_inc(k.sem["reduced"], 1)
            dve.wait_ge(k.sem["rooted"], 1)
            o.recip(ss[:, :, :], ss[:, :, :])
            dve.wait_ge(k.sem["loaded"], 16)
            for j in range(NT):
                h3 = x[:, j, :].rearrange("p (h n) -> p h n", h=heads)
                o.mul(h3, h3, spread(ss[:, j, :], width))
                o.mul(h3, h3, over(gr[:, :], heads))
                if scale is not None:
                    o.ts(x[:, j, :], x[:, j, :], scale, ALU.mult)
    k.clear()


def diff_attention(k, proj, q_gain, k_gain, lam_vecs, sub_g, lam_init, keep, out):
    nc = k.nc
    C = k.const
    with ExitStack() as c:
        qk = k.sb("qk", [P, 2, NT, DA], ctx=c)
        lv = k.sb("lambda_vectors", [P, 4, 64], ctx=c)
        l2 = k.sb("lambda_sums", [P, 2], ctx=c)
        lam = k.sb("minus_lambda", [P, 1], ctx=c)
        junk = k.sb("lambda_products", [P, 2, 64], ctx=c)
        qkT = k.sb("qkT", [P, 2, 4, SEQ], ctx=c)
        dist = k.sb("minus_distance", [P, NT, SEQ], ctx=c)
        load_stage(k, [(lv[:, :, :].rearrange("p a n -> p (a n)"), rows(lam_vecs)),
                       (dist[:, :, :], nc.inline_tensor(distance_tables()[0], name="distance_table").ap())])
        with nc.Block() as block:
            @block.vector
            def _(dve):
                o = Ops(nc, dve, True)
                for j in range(NT):
                    for w in range(2):
                        o.copy(qk[:, w, j, :], proj[:, j, C_RWKV + w * DA:C_RWKV + (w + 1) * DA], free=True)
                for n in range(2):
                    o.mul(junk[:, n], lv[:, 2 * n], lv[:, 2 * n + 1])
                    o.sum(l2[:, n:n + 1], junk[:, n])
                o.copy(l2[:, :], l2[:, :]).then_inc(k.sem["reduced"], 1)
                dve.wait_ge(k.sem["exped"], 1)
                o.sub(lam[:, :], l2[:, 1:2], l2[:, 0:1])
                o.sub(lam[:, :], lam[:, :], lam_init)

            @block.scalar
            def _(act):
                act.wait_ge(k.sem["reduced"], 1)
                nc.scalar.activation(l2[:, :], l2[:, :], ACT.Exp).then_inc(k.sem["exped"], 1)
        k.clear()
        with ExitStack() as c1:
            head_norm(k, qk[:, 0], 8, 64, q_gain, None, c1)
        with ExitStack() as c1:
            head_norm(k, qk[:, 1], 8, 64, k_gain, None, c1)
        turn_tokens(k, qk[:, 0], qkT[:, 0], 4)
        turn_tokens(k, qk[:, 1], qkT[:, 1], 4)
        units = [(h, j) for h in range(NHB) for j in range(NT)]
        lg = k.sb("logits", [P, 2, 2, SEQ], ctx=c)
        mx = k.sb("row_max", [P, 2, 2], ctx=c)
        sm = k.sb("row_sum", [P, 2, 2], ctx=c)
        bias = k.sb("alibi", [P, NT, SEQ], ctx=c)
        pT = k.sb("probsT", [P, 2, 2, P], ctx=c)
        S = k.sem
        with nc.Block() as block:
            @block.tensor
            def _(pe):
                def logits(n):
                    h, j = units[n]
                    if n >= 2:
                        pe.wait_ge(S["masked"], n - 1)
                    for mm in range(2):
                        ks = slice(mm * 64, mm * 64 + 64)
                        last = nc.tensor.matmul(k.bank(2 * (n % 2) + mm)[:, 0:SEQ],
                                                qkT[ks, 0, h, j * P:j * P + P], qkT[ks, 1, h, :], start=True, stop=True)
                    last.then_inc(S["summed"], 1)

                logits(0)
                for n, (h, j) in enumerate(units):
                    if n + 1 < len(units):
                        logits(n + 1)
                    pe.wait_ge(S["got"], n + 1)
                    if n >= 2:
                        pe.wait_ge(S["copied_s"], n - 1)
                    for kc in range(2):
                        last = nc.tensor.transpose(k.bank(4 + n % 2)[:, kc * P:kc * P + P],
                                                   lg[:, n % 2, 0, kc * P:kc * P + P], C("ident"))
                    last.then_inc(S["turned"], 1)
                    pe.wait_ge(S["copied_s"], n + 1)
                    if n >= 2:
                        pe.wait_ge(S["stored"], n - 1)
                    for kc in range(2):
                        last = nc.tensor.matmul(k.bank(6 + n % 2)[:, 0:P], pT[:, n % 2, kc, :],
                                                proj[:, kc, C_RWKV + 2 * DA + h * P:C_RWKV + 2 * DA + h * P + P],
                                                start=kc == 0, stop=kc == 1)
                    last.then_inc(S["done"], 1)

            @block.scalar
            def _(act):
                o = Ops(nc, act, False)
                for n in range(len(units)):
                    act.wait_ge(S["masked"], n + 1)
                    for mm in range(2):
                        o.fn(lg[:, n % 2, mm], lg[:, n % 2, mm], ACT.Exp, bias=mx[:, n % 2, mm:mm + 1],
                             total=sm[:, n % 2, mm:mm + 1], free=True).then_inc(S["exped"], 1)
                    act.wait_ge(S["turned"], n + 1)
                    o.copy(pT[:, n % 2], k.bank(4 + n % 2, 2, P), free=True).then_inc(S["copied_s"], 1)

            @block.vector
            def _(dve):
                o = Ops(nc, dve, True)
                for n, (h, j) in enumerate(units):
                    slope = 2.0 ** (-8.0 * (h + 1) / NHB)
                    if n >= 2:
                        dve.wait_ge(S["turned"], n - 1)
                    o.ts(bias[:, j], dist[:, j, :], slope, ALU.mult)
                    dve.wait_ge(S["summed"], n + 1)
                    for mm in range(2):
                        o.stt(lg[:, n % 2, mm], k.bank(2 * (n % 2) + mm)[:, 0:SEQ], 64.0 ** -0.5, bias[:, j],
                              ALU.mult, ALU.add, free=mm > 0)
                    o.max(mx[:, n % 2], lg[:, n % 2])
                    o.ts(mx[:, n % 2], mx[:, n % 2], -1.0, ALU.mult).then_inc(S["masked"], 1)
                    dve.wait_ge(S["exped"], 2 * n + 2)
                    o.recip(sm[:, n % 2], sm[:, n % 2], free=True)
                    o.ts(sm[:, n % 2, 1:2], sm[:, n % 2, 1:2], lam[:, 0:1], ALU.mult)
                    o.ts(lg[:, n % 2, 0], lg[:, n % 2, 0], sm[:, n % 2, 0:1], ALU.mult)
                    o.stt(lg[:, n % 2, 0], lg[:, n % 2, 1], sm[:, n % 2, 1:2], lg[:, n % 2, 0],
                          ALU.mult, ALU.add).then_inc(S["got"], 1)
                    dve.wait_ge(S["done"], n + 1)
                    o.copy(out[:, j, h * P:h * P + P], k.bank(6 + n % 2)[:, 0:P], free=True).then_inc(S["stored"], 1)
        k.clear()
        with ExitStack() as c1:
            head_norm(k, out, NHB, P, sub_g, keep, c1)


def first_layer(k, l, a, lam_tab):
    row = lambda name: a[name][bass.ds(l, 1), :]
    mat = lambda name: a[name][l]
    w_proj = row_weights(mat("w_in"), C_IN // WPROJ, WPROJ)
    w_br = [sum_weights(a["w_branch"][l, br], 4) for br in range(2)]
    w_mix = sum_weights(mat("w_out"), KC)
    w_up = pair_weights(mat("ffn2_in"), D_FF)
    swiglu(k, row("norm_ffn1"), pair_weights(mat("ffn1_in"), D_FF), sum_weights(mat("ffn1_out"), NF), w_proj)
    with ExitStack() as c:
        proj = k.sb("projected", [P, NT, C_IN], ctx=c)
        oa = k.sb("branch_a", [P, NT, DA], ctx=c)
        project(k, row("norm_mix"), w_proj, WPROJ, proj)
        flat = lambda name: a[name].rearrange("l h n -> l (h n)")[bass.ds(l, 1), :]
        rwkv(k, proj, row("rwkv_mu"),
             [a["decay_w0"][bass.ds(l, 1), g, :] for g in range(2)], a["decay_w2"].rearrange("l g r c -> l (g r) c")[l],
             [a["iclr_a0"][bass.ds(l, 1), g, :] for g in range(2)], a["iclr_a2"].rearrange("l g r c -> l (g r) c")[l],
             mat("gate_g2"), row("k_k"), row("k_a"), flat("r_k"), row("ln_x_g"), row("ln_x_b"), oa)
        ob = k.sb("branch_b", [P, NT, DA], ctx=c)
        lamc = k.sb("lambda_constants", [P, 2], ctx=c)
        with k.nc.Block() as block:
            @block.vector
            def _(dve):
                k.nc.vector.tensor_copy(lamc[:, :], lam_tab[:, bass.ds(l, 1), :].rearrange("p a b -> p (a b)"))
        k.clear()
        diff_attention(k, proj, row("q_gain"), row("k_gain"), flat("diff_lambda"), row("subln_g"),
                       lamc[:, 0:1], lamc[:, 1:2], ob)
        gates = proj[:, :, C_RWKV + C_ATTN:]
        with k.nc.Block() as block:
            @block.scalar
            def _(act):
                for j in range(NT):
                    k.nc.scalar.activation(gates[:, j, :], gates[:, j, :], ACT.Sigmoid)
        k.clear()
        oT = split_sb(k, "branchT", [P, 4, SEQ], c)
        for br, src in enumerate((oa, ob)):
            turn_tokens(k, src, oT, 4)

            def gated(o, j, half, bank, br=br):
                g0 = gates[:, j, half * BANK:(half + 1) * BANK]
                g1 = gates[:, j, br * D + half * BANK:br * D + (half + 1) * BANK]
                o.mul(g1, g1, bank)
                if br:
                    return o.add(g0, g0, g1)

            linear_sum_stage(k, oT, 4, w_br[br], gated, (w_br + [w_mix])[br + 1])
        mT = split_sb(k, "mergedT", [P, KC, SEQ], c)
        turn_tokens(k, gates[:, :, 0:D], mT, KC)

        def residual(o, j, half, bank):
            x = k.X[:, j, half * BANK:(half + 1) * BANK]
            return o.add(x, x, bank, free=True)

        linear_sum_stage(k, mT, KC, w_mix, residual, w_up)
    swiglu(k, row("norm_ffn2"), w_up, sum_weights(mat("ffn2_out"), NF), None)



def modulation(k, cond, wts, b, out, ahead=None):
    tiles = wts.tiles
    nc = k.nc
    with ExitStack() as c:
        cr = k.sb("cond", [P, P], ctx=c)
        cT = k.sb("condT", [P, 1, P], ctx=c)
        cb = split_sb(k, "cond_columns", [P, KC, P], c)
        br = k.sb("mod_bias", [P, tiles * BANK], ctx=c)
        with nc.Block() as block:
            @block.sync
            def _(sp):
                sp.wait_ge(k.sem["reduced"], 1)
                sp.dma_start(cr[0:KC, :], cond).then_inc(k.sem["loaded"], 16)
                sp.dma_start(br[:, :], rows(b)).then_inc(k.sem["written"], 16)
                sp.wait_ge(k.sem["written"], 16)

            @block.vector
            def _(dve):
                nc.vector.memset(cr[:, :], 0.0).then_inc(k.sem["reduced"], 1)

            @block.scalar
            def _(act):
                act.wait_ge(k.sem["loaded"], 16)
                nc.scalar.activation(cr[:, :], cr[:, :], ACT.Silu)
        k.clear()
        turn_stage(k, [([cr[:, :]], cT[:, :, :])])
        with nc.Block() as block:
            @block.vector
            def _(dve):
                nc.vector.tensor_copy(cb.hi[:, :, :], spread(cT[:, 0, 0:KC], P))
                dve.drain()
                nc.vector.tensor_tensor(cb.lo[:, :, :], spread(cT[:, 0, 0:KC], P), cb.hi[:, :, :].bitcast(F32),
                                        ALU.subtract)
        k.clear()
        linear_stage(k, lambda c_, j: cb[:, c_, :], wts, BANK,
                     lambda o, t, j, bank: o.add(out[:, bass.ds(t * BANK, BANK)], bank,
                                                 br[:, bass.ds(t * BANK, BANK)], free=True), ahead, groups=1)


def rope(k, x, heads, scratch, trig):
    nc = k.nc
    with nc.Block() as block:
        @block.vector
        def _(dve):
            o = Ops(nc, dve, True)
            for j in range(NT):
                for ax in range(2):
                    x4 = x[:, j, :].rearrange("p (h a b n) -> p h a b n", h=heads, a=2, b=2)
                    x1, x2 = x4[:, :, ax, 0, :], x4[:, :, ax, 1, :]
                    cs, sn = over(trig[:, 0, j, ax, :], heads), over(trig[:, 1, j, ax, :], heads)
                    s = scratch[:, 0:4, 0:heads * 16].rearrange("p a (h n) -> p a h n", n=16)
                    o.mul(s[:, 0], x1, cs)
                    o.mul(s[:, 1], x2, sn, free=True)
                    o.mul(s[:, 2], x1, sn, free=True)
                    o.mul(s[:, 3], x2, cs, free=True)
                    o.sub(x1, s[:, 0], s[:, 1])
                    o.add(x2, s[:, 2], s[:, 3], free=True)
    k.clear()


def window_attention(k, pr, kvc, sink, out):
    nc = k.nc
    C = k.const
    S = k.sem
    with ExitStack() as c:
        scr = k.sb("rope_scratch", [P, 4, 128], ctx=c)
        sk = k.sb("sink", [P, 8], ctx=c)
        window = k.sb("window_mask", [P, NT, SEQ], ctx=c)
        trig = k.sb("cos_sin", [P, 2, NT, 2, 16], ctx=c)
        load_stage(k, [(sk[:, :], rows(sink)),
                       (window[:, :, :], nc.inline_tensor(distance_tables()[1], name="window_table").ap()),
                       (trig[:, :, :, :, :].rearrange("p a b c d -> p (a b c d)"),
                        nc.inline_tensor(rope_table().reshape(P, -1), name="rope_table").ap())])
        rope(k, pr[:, :, 0:QW], 8, scr, trig)
        rope(k, pr[:, :, QW:QW + KVW], 2, scr, trig)
        qT = k.sb("qT", [64, 8, SEQ], ctx=c)
        kT = k.sb("kT", [64, 2, 2 * SEQ], ctx=c)
        jobs = [(pr[:, j, h * 64:h * 64 + 64], qT[:, h, j * P:j * P + P]) for h in range(8) for j in range(NT)]
        jobs += [(pr[:, j, QW + g * 64:QW + g * 64 + 64], kT[:, g, j * P:j * P + P]) for g in range(2) for j in range(NT)]
        jobs += [(kvc[:, j, g * 64:g * 64 + 64], kT[:, g, SEQ + j * P:SEQ + j * P + P]) for g in range(2) for j in range(NT)]
        with nc.Block() as block:
            @block.tensor
            def _(pe):
                for n, (src, _) in enumerate(jobs):
                    if n >= 8:
                        pe.wait_ge(S["copied_v"], n - 7)
                    nc.tensor.transpose(k.bank(n % 8)[0:64, 0:P], src, C("ident")).then_inc(S["turned"], 1)

            @block.vector
            def _(dve):
                for n, (_, dst) in enumerate(jobs):
                    dve.wait_ge(S["turned"], n + 1)
                    nc.vector.tensor_copy(dst, k.bank(n % 8)[0:64, 0:P]).then_inc(S["copied_v"], 1)
        k.clear()
        units = [(h, j) for h in range(8) for j in range(NT)]
        lg = k.sb("logits", [P, 2, 2 * SEQ], ctx=c)
        mx = k.sb("row_max", [P, 2], ctx=c)
        sm = k.sb("row_sum", [P, 2, 2], ctx=c)
        pT = k.sb("probsT", [P, 2, 4, P], ctx=c)
        with nc.Block() as block:
            @block.tensor
            def _(pe):
                def logits(n):
                    h, j = units[n]
                    if n >= 2:
                        pe.wait_ge(S["masked"], n - 1)
                    nc.tensor.matmul(k.bank(n % 2), qT[:, h, j * P:j * P + P], kT[:, h // 4, :],
                                     start=True, stop=True).then_inc(S["summed"], 1)

                logits(0)
                for n, (h, j) in enumerate(units):
                    if n + 1 < len(units):
                        logits(n + 1)
                    pe.wait_ge(S["exped"], 2 * n + 2)
                    if n >= 2:
                        pe.wait_ge(S["copied_s"], n - 1)
                    for kc in range(4):
                        last = nc.tensor.transpose(k.bank(2 + n % 2)[:, kc * P:kc * P + P],
                                                   lg[:, n % 2, kc * P:kc * P + P], C("ident"))
                    last.then_inc(S["turned"], 1)
                    pe.wait_ge(S["copied_s"], n + 1)
                    if n >= 2:
                        pe.wait_ge(S["stored"], n - 1)
                    g = h // 4
                    for kc in range(4):
                        src = (pr[:, kc, QW + KVW + g * 64:QW + KVW + g * 64 + 64] if kc < 2
                               else kvc[:, kc - 2, KVW + g * 64:KVW + g * 64 + 64])
                        last = nc.tensor.matmul(k.bank(4 + n % 2)[:, 0:64], pT[:, n % 2, kc, :], src,
                                                start=kc == 0, stop=kc == 3)
                    last.then_inc(S["done"], 1)

            @block.scalar
            def _(act):
                o = Ops(nc, act, False)
                for n, (h, j) in enumerate(units):
                    act.wait_ge(S["masked"], n + 1)
                    if n >= 2:
                        act.wait_ge(S["stored"], n - 1)
                    o.fn(lg[:, n % 2], lg[:, n % 2], ACT.Exp, bias=mx[:, n % 2:n % 2 + 1],
                         total=sm[:, n % 2, 0:1], free=True).then_inc(S["exped"], 1)
                    o.fn(sm[:, n % 2, 1:2], sk[:, h:h + 1], ACT.Exp, bias=mx[:, n % 2:n % 2 + 1],
                         free=True).then_inc(S["exped"], 1)
                    act.wait_ge(S["turned"], n + 1)
                    o.copy(pT[:, n % 2], k.bank(2 + n % 2, 4, P), free=True).then_inc(S["copied_s"], 1)

            @block.vector
            def _(dve):
                o = Ops(nc, dve, True)
                for n, (h, j) in enumerate(units):
                    if n >= 2:
                        dve.wait_ge(S["turned"], n - 1)
                    dve.wait_ge(S["summed"], n + 1)
                    o.stt(lg[:, n % 2, 0:SEQ], k.bank(n % 2)[:, 0:SEQ], 0.125, window[:, j, :], ALU.mult, ALU.add)
                    o.ts(lg[:, n % 2, SEQ:], k.bank(n % 2)[:, SEQ:], 0.125, ALU.mult, free=True)
                    o.max(mx[:, n % 2:n % 2 + 1], lg[:, n % 2])
                    o.tt(mx[:, n % 2:n % 2 + 1], mx[:, n % 2:n % 2 + 1], sk[:, h:h + 1], ALU.max)
                    o.ts(mx[:, n % 2:n % 2 + 1], mx[:, n % 2:n % 2 + 1], -1.0, ALU.mult).then_inc(S["masked"], 1)
                    dve.wait_ge(S["exped"], 2 * n + 2)
                    o.add(sm[:, n % 2, 0:1], sm[:, n % 2, 0:1], sm[:, n % 2, 1:2])
                    o.recip(sm[:, n % 2, 0:1], sm[:, n % 2, 0:1])
                    dve.wait_ge(S["done"], n + 1)
                    o.ts(out[:, j, h * 64:h * 64 + 64], k.bank(4 + n % 2)[:, 0:64], sm[:, n % 2, 0:1],
                         ALU.mult).then_inc(S["stored"], 1)
        k.clear()


def gmlp(k, pr, w_s, b_s, out):
    nc = k.nc
    C = k.const
    S = k.sem
    u = pr[:, :, QW + 2 * KVW:QW + 2 * KVW + AW]
    v = pr[:, :, QW + 2 * KVW + AW:]
    with ExitStack() as c:
        ws = k.sb("spatial", [P, GROUPS, P], ctx=c)
        wsT = k.sb("spatialT", [P, GROUPS, P], ctx=c)
        bs = k.sb("spatial_bias", [P, P], ctx=c)
        bT = k.sb("spatial_biasT", [P, 1, P], ctx=c)
        mean = k.sb("mean", [P, NT, GROUPS], ctx=c)
        var = k.sb("var", [P, NT, GROUPS], ctx=c)
        sq = k.sb("scratch", [P, AW], ctx=c)
        with nc.Block() as block:
            @block.sync
            def _(sp):
                sp.dma_start(ws[:, :, :], w_s.rearrange("g p q -> p g q")).then_inc(S["loaded"], 16)
                sp.wait_ge(S["reduced"], 1)
                sp.dma_start(bs[0:GROUPS, :], b_s).then_inc(S["loaded"], 16)
                sp.wait_ge(S["loaded"], 32)

            @block.scalar
            def _(act):
                for j in range(NT):
                    nc.scalar.activation(u[:, j, :], u[:, j, :], ACT.Gelu_apprx_tanh)
                    nc.scalar.activation(v[:, j, :], v[:, j, :], ACT.Gelu_apprx_tanh)

            @block.vector
            def _(dve):
                nc.vector.memset(bs[:, :], 0.0).then_inc(S["reduced"], 1)
        k.clear()
        turn_stage(k, [([ws[:, n + i, :] for i in range(4)], wsT[:, n:n + 4, :]) for n in (0, 4)] + [([bs[:, :]], bT[:, :, :])])
        with nc.Block() as block:
            @block.vector
            def _(dve):
                o = Ops(nc, dve, True)
                for j in range(NT):
                    h3 = v[:, j, :].rearrange("p (h n) -> p h n", h=GROUPS)
                    s3 = sq[:, :].rearrange("p (h n) -> p h n", h=GROUPS)
                    o.sum(mean[:, j, :], h3)
                    o.ts(mean[:, j, :], mean[:, j, :], 1.0 / 64, ALU.mult)
                    o.sub(h3, h3, spread(mean[:, j, :], 64))
                    o.mul(s3, h3, h3)
                    o.sum(var[:, j, :], s3)
                o.ts(var[:, :, :], var[:, :, :], 1.0 / 64, ALU.mult, EPS, ALU.add).then_inc(S["reduced"], 1)
                dve.wait_ge(S["rooted"], 1)
                o.recip(var[:, :, :], var[:, :, :])
                for j in range(NT):
                    h3 = v[:, j, :].rearrange("p (h n) -> p h n", h=GROUPS)
                    o.mul(h3, h3, spread(var[:, j, :], 64)).then_inc(S["stored"], 1)
                for j in range(NT):
                    dve.wait_ge(S["done"], j + 1)
                    for g in range(GROUPS):
                        cs = slice(g * 64, g * 64 + 64)
                        o.stt(out[:, j, cs], k.bank(j)[:, cs], bT[:, 0, g:g + 1], u[:, j, cs], ALU.add, ALU.mult, free=True)

            @block.scalar
            def _(act):
                act.wait_ge(S["reduced"], 1)
                nc.scalar.activation(var[:, :, :], var[:, :, :], ACT.Sqrt).then_inc(S["rooted"], 1)

            @block.tensor
            def _(pe):
                for j in range(NT):
                    pe.wait_ge(S["stored"], j + 1)
                    for g in range(GROUPS):
                        last = nc.tensor.matmul(k.bank(j)[:, g * 64:g * 64 + 64], wsT[:, g, :],
                                                v[:, j, g * 64:g * 64 + 64], start=True, stop=True)
                    last.then_inc(S["done"], 1)
        k.clear()


def gated_residual(k, gate, bank, o, j, half, tmp):
    cs = slice(half * BANK, (half + 1) * BANK)
    o.mul(tmp[:, :], bank, gate[:, cs])
    return o.add(k.X[:, j, cs], k.X[:, j, cs], tmp[:, :])


def attn_gmlp_layer(k, a, mod, w_cmod, w_query):
    nc = k.nc
    with ExitStack() as c:
        kvc = k.sb("context_kv", [P, NT, 2 * KVW], ctx=c)
        tmp = k.sb("scratch", [P, BANK], ctx=c)
        w = a["attn_in_w_2"][0]
        with ExitStack() as c1:
            cm = k.sb("context_mod", [P, 4 * BANK], ctx=c1)
            w_ckv = row_weights(w[:, QW:QW + 2 * KVW], 1, 2 * KVW)
            w_pr = row_weights(w, 4, IN_W // 4)
            w_mix = sum_weights(a["attn_out_w_2"][0], KC)
            modulation(k, a["c_ctx_2"].rearrange("(k p) -> k p", p=P), w_cmod, a["mod_b_2"][0:1, 0:4 * BANK], cm, w_ckv)
            cx = k.sb("context", [P, NT, D], ctx=c1)
            cT = split_sb(k, "contextT", [P, KC, SEQ], c1)
            load_stage(k, [(cx[:, :, :], a["ctx_2"][0].rearrange("(j p) d -> p j d", p=P))])
            norm_stage(k, cx, a["norm1_g_2"][0:1, :], cx, cm[:, D:2 * D], cm[:, 0:D])
            turn_tokens(k, cx, cT, KC)
            linear_stage(k, lambda c_, j: cT[:, c_, j * P:j * P + P], w_ckv, 2 * KVW,
                         lambda o, t, j, bank: o.copy(kvc[:, j, :], bank, free=True), w_pr)
        pr = k.sb("projected", [P, NT, IN_W], ctx=c)
        project(k, a["norm1_g_2"][0:1, :], w_pr, IN_W // 4, pr, (mod[:, D:2 * D], mod[:, 0:D]), w_mix)
        mix = k.sb("mixed", [P, NT, D], ctx=c)
        window_attention(k, pr, kvc, a["attn_sink_2"][0:1, :], mix[:, :, 0:QW])
        gmlp(k, pr, a["gmlp_w_s_2"][0], a["gmlp_b_s_2"][0], mix[:, :, QW:])
        mT = split_sb(k, "mixedT", [P, KC, SEQ], c)
        turn_tokens(k, mix, mT, KC)
        linear_sum_stage(k, mT, KC, w_mix,
                         lambda o, j, half, bank: gated_residual(k, mod[:, 2 * D:3 * D], bank, o, j, half, tmp), w_query)


def pool_layer(k, a, mod):
    nc = k.nc
    S = k.sem
    C = k.const
    with ExitStack() as c:
        h = k.sb("normed", [P, NT, D], ctx=c)
        norm_stage(k, k.X, a["norm1_g_2"][1:2, :], h, mod[:, D:2 * D], mod[:, 0:D])
        pw = k.sb("pool_w", [P, 4, 2, SEQ], ctx=c)
        means = k.sb("window_means", [P, 4, NT, SEQ], ctx=c)
        ps = k.sb("pool_scale", [P, D], ctx=c)
        pT = k.sb("pooledT", [P, KC, SEQ], ctx=c)
        tmp = k.sb("scratch", [P, SEQ], ctx=c)
        load_stage(k, [(pw[:, :, :, :].rearrange("p g k e -> p (g k) e"),
                        a["pool_w_2"][0].rearrange("g (k p) e -> p (g k) e", p=P)),
                       (ps[:, :], rows(a["pool_scale_2"][0:1, :])),
                       (means[:, :, :, :], nc.inline_tensor(pool_table(), name="window_mean_table").ap())])
        with nc.Block() as block:
            @block.tensor
            def _(pe):
                for cc in range(KC):
                    for s in range(NT):
                        last = nc.tensor.matmul(k.bank(cc)[:, 0:SEQ], h[:, s, cc * P:cc * P + P],
                                                means[:, cc // 2, s, :], start=s == 0, stop=s == NT - 1)
                    last.then_inc(S["summed"], 1)
                for g in range(4):
                    pe.wait_ge(S["stored"], 2 * g + 2)
                    for j in range(NT):
                        for cc in range(2):
                            last = nc.tensor.matmul(k.bank(2 * g + j)[:, 0:SEQ], pT[:, 2 * g + cc, j * P:j * P + P],
                                                    pw[:, g, cc, :], start=cc == 0, stop=cc == 1)
                        last.then_inc(S["done"], 1)

            @block.vector
            def _(dve):
                o = Ops(nc, dve, True)
                o.mul(ps[:, :], ps[:, :], mod[:, 2 * D:3 * D])
                for cc in range(KC):
                    dve.wait_ge(S["summed"], cc + 1)
                    o.copy(pT[:, cc, :], k.bank(cc)[:, 0:SEQ], free=True).then_inc(S["stored"], 1)
                for g in range(4):
                    cs = slice(g * SEQ, (g + 1) * SEQ)
                    for j in range(NT):
                        dve.wait_ge(S["done"], 2 * g + j + 1)
                        o.mul(tmp[:, :], k.bank(2 * g + j)[:, 0:SEQ], ps[:, cs])
                        o.add(k.X[:, j, cs], k.X[:, j, cs], tmp[:, :])
        k.clear()


def top16(o, nc, vals, work, idx, src):
    o._order(False)
    nc.vector.max(out=vals[:, 0:8], in_=src)
    o._order(False)
    nc.vector.max_index(out=idx[:, 0:8], in_max=vals[:, 0:8], in_values=src)
    nc.vector.match_replace(out=work, in_to_replace=vals[:, 0:8], in_values=src, imm_value=-3.0e38)
    o._order(False)
    nc.vector.max(out=vals[:, 8:16], in_=work)
    o._order(False)
    return nc.vector.max_index(out=idx[:, 8:16], in_max=vals[:, 8:16], in_values=work)


def peer(k, a, l, mod, w_query):
    nc = k.nc
    S = k.sem
    C = k.const
    with ExitStack() as c:
        h = k.sb("normed", [P, NT, D], ctx=c)
        gate = k.sb("expert_gate", [P, NT, SLOTS], ctx=c)
        ids = k.sb("expert_ids", [P, NT, SLOTS], U32, ctx=c)
        norm_stage(k, k.X, a["norm2_g_2"][l:l + 1, :], h, mod[:, 4 * D:5 * D], mod[:, 3 * D:4 * D])
        with ExitStack() as c1:
            hT = split_sb(k, "normedT", [P, KC, SEQ], c1)
            qT = k.sb("queriesT", [P, 2 * PH, SEQ], ctx=c1)
            sk = k.sb("sub_keys", [P, 2, P], ctx=c1)
            skT = k.sb("sub_keysT", [P, 2, P], ctx=c1)
            turn_tokens(k, h, hT, KC)
            load_stage(k, [(sk[:, :, :], a["peer_sub_keys_2"][l].rearrange("s n d -> n s d"))])
            turn_stage(k, [([sk[:, 0, :], sk[:, 1, :]], skT[:, :, :])])
            linear_turned_stage(k, hT, w_query, 1, lambda o, n, v, bank: o.copy(
                qT[:, bass.ds(n, 1), :].rearrange("p a n -> p (a n)"), bank[:, 0:SEQ], free=True))
            s = k.sb("key_scores", [P, 2 * PH, P], ctx=c1)
            w = k.sb("work", [P, 2, SEQ], ctx=c1)
            v1 = k.sb("key_best", [P, 2 * PH, TOPK], ctx=c1)
            i1 = k.sb("key_index", [P, 2 * PH, TOPK], U32, ctx=c1)
            f1 = k.sb("key_index_f", [P, 2 * PH, TOPK], ctx=c1)
            cand = k.sb("pair_scores", [P, PH, TOPK, TOPK], ctx=c1)
            best = k.sb("pair_best", [P, PH, TOPK], ctx=c1)
            pos = k.sb("pair_pos", [P, PH, TOPK], U32, ctx=c1)
            hi = k.sb("pair_hi", [P, 2, PH, TOPK], U32, ctx=c1)
            hf = k.sb("pair_hi_f", [P, 2, PH, TOPK], ctx=c1)
            hot = k.sb("one_hot", [P, PH, TOPK, TOPK], ctx=c1)
            pick = k.sb("picked", [P, 2, PH, TOPK], ctx=c1)
            tot = k.sb("gate_sum", [P, PH], ctx=c1)
            for j in range(NT):
                with nc.Block() as block:
                    @block.tensor
                    def _(pe):
                        for n in range(2 * PH):
                            last = nc.tensor.matmul(k.bank(n // 4)[:, n % 4 * P:n % 4 * P + P],
                                                    qT[:, n, j * P:j * P + P], skT[:, n % 2, :], start=True, stop=True)
                            if n % 4 == 3:
                                last.then_inc(S["summed"], 1)

                    @block.vector
                    def _(dve):
                        o = Ops(nc, dve, True)
                        for b in range(4):
                            dve.wait_ge(S["summed"], b + 1)
                            o.copy(s[:, 4 * b:4 * b + 4, :], k.bank(b, 4, P), free=True)
                        for n in range(2 * PH):
                            top16(o, nc, v1[:, n], w[:, n % 2, 0:P], i1[:, n], s[:, n])
                        o.copy(f1[:, :, :], i1[:, :, :])
                        for e in range(PH):
                            o.tt(cand[:, e], spread(v1[:, 2 * e], TOPK), over(v1[:, 2 * e + 1], TOPK), ALU.add, free=e > 0)
                        for e in range(PH):
                            top16(o, nc, best[:, e], w[:, e % 2], pos[:, e], cand[:, e].rearrange("p a b -> p (a b)"))
                        o.ts(hi[:, 0], pos[:, :, :], 4, ALU.logical_shift_right)
                        o.ts(hi[:, 1], pos[:, :, :], 15, ALU.bitwise_and, free=True)
                        o.copy(hf[:, :, :, :], hi[:, :, :, :])
                        for side in range(2):
                            for e in range(PH):
                                o.tt(hot[:, e], spread(hf[:, side, e], TOPK), over(C("iota16"), TOPK), ALU.is_equal,
                                     free=e > 0)
                            for e in range(PH):
                                o.mul(hot[:, e], hot[:, e], over(f1[:, 2 * e + side], TOPK), free=e > 0)
                            o.sum(pick[:, side].rearrange("p h t -> p (h t)"),
                                  hot[:, :, :, :].rearrange("p h t c -> p (h t) c"))
                        flat = lambda t: t.rearrange("p h t -> p (h t)")
                        o.stt(flat(pick[:, 0]), flat(pick[:, 0]), float(NK), flat(pick[:, 1]), ALU.mult, ALU.add)
                        o.ts(ids[:, j, :], flat(pick[:, 0]), float(l * NK * NK), ALU.add)
                        for e in range(PH):
                            o.ts(best[:, e], best[:, e], best[:, e, 0:1], ALU.subtract)
                        o.copy(tot[:, :], best[:, :, 0]).then_inc(S["reduced"], 1)
                        dve.wait_ge(S["exped"], 1)
                        o.sum(tot[:, :], best[:, :, :])
                        o.recip(tot[:, :], tot[:, :])
                        o.mul(gate[:, j, :].rearrange("p (h t) -> p h t", h=PH), best[:, :, :], spread(tot[:, :], TOPK))

                    @block.scalar
                    def _(act):
                        act.wait_ge(S["reduced"], 1)
                        nc.scalar.activation(best[:, :, :], best[:, :, :], ACT.Exp).then_inc(S["exped"], 1)
                k.clear()
        experts(k, a, h, gate, ids, mod)


def experts(k, a, h, gate, ids, mod):
    nc = k.nc
    S = k.sem
    C = k.const
    BODY = 2 * RING
    n_iter = SLOTS // BODY
    uses = SLOTS // RING
    down = a["peer_down_2"].rearrange("l e d -> (l e) d")
    up = a["peer_up_2"].rearrange("l e d -> (l e) d")
    row = k.rows
    used = [S[f"used{r}"] for r in range(RING)]
    with ExitStack() as c:
        buf = k.sb("expert_rows", [P, RING, D], ctx=c)
        idw = k.sb("ids_now", [P, 2, RING], U32, ctx=c)
        junk = k.sb("products", [P, D], ctx=c)
        dots = k.sb("dots", [P, SLOTS], ctx=c)
        dnow = k.sb("dots_now", [P, BODY], ctx=c)
        coef = k.sb("coefficients", [P, SLOTS], ctx=c)
        diag = k.sb("diagonals", [P, 4, P], ctx=c)
        zero = k.sb("zeros", [P, P], ctx=c)
        acc = k.sb("accumulated", [P, D], ctx=c)
        for j in range(NT):
            before = 16 * k.row_uses
            with nc.Block() as block:
                @block.gpsimd
                def _(pool):
                    for phase, table in enumerate((down, up)):
                        with pool.Fori(0, n_iter) as i:
                            for n in range(BODY):
                                r, half = n % RING, n // RING
                                pool.wait_ge(used[r], i * 2 + (half + phase * uses + 1))
                                if r == 0:
                                    nc.gpsimd.tensor_copy(idw[:, half, :], ids[:, j, bass.ds(i * BODY + n, RING)]
                                                          ).then_inc(S["ids_ready"], 1)
                                    pool.wait_ge(S["ids_ready"], i * 2 + (half + phase * uses + 1))
                                pool.sem_inc(S["gathers"], 1)
                                nc.gpsimd.indirect_dma_start(
                                    out=buf[:, r, :], out_offset=None, in_=table,
                                    in_offset=bass.IndirectOffsetOnAxis(ap=idw[:, half, r:r + 1], axis=0)
                                ).then_inc(row[r], 16)

                @block.vector
                def _(dve):
                    o = Ops(nc, dve, True)
                    for r in range(RING):
                        dve.sem_inc(used[r], 1)
                    with dve.Fori(0, n_iter) as i:
                        for n in range(BODY):
                            r, half = n % RING, n // RING
                            dve.drain()
                            dve.wait_ge(row[r], i * 32 + (before + 16 * half + 16))
                            o.dot(junk[:, :], buf[:, r, :], h[:, j, :], dnow[:, n:n + 1],
                                  free=True).then_inc(used[r], 1)
                        o.copy(dots[:, bass.ds(i * BODY, BODY)], dnow[:, :])
                    o.ts(acc[:, :], h[:, j, :], 0.0, ALU.mult)
                    o.ts(zero[:, :], C("ident"), 0.0, ALU.mult).then_inc(S["reduced"], 1)
                    dve.wait_ge(S["exped"], 1)
                    o.mul(coef[:, :], coef[:, :], gate[:, j, :]).then_inc(S["stored"], 1)
                    with dve.Fori(0, n_iter) as i:
                        for n in range(0, BODY, 2):
                            r, half = n % RING, n // RING
                            dve.drain()
                            dve.wait_ge(row[r], i * 32 + (before + 16 * (half + uses) + 16))
                            o.stt(acc[:, :], buf[:, r, :], coef[:, bass.ds(i * BODY + n, 1)], acc[:, :],
                                  ALU.mult, ALU.add, free=True).then_inc(used[r], 1)
                    dve.wait_ge(S["summed"], 1)
                    for half in range(2):
                        cs = slice(half * BANK, (half + 1) * BANK)
                        o.add(acc[:, cs], acc[:, cs], k.bank(half))
                        o.mul(acc[:, cs], acc[:, cs], mod[:, 5 * D + half * BANK:5 * D + (half + 1) * BANK])
                        o.add(k.X[:, j, cs], k.X[:, j, cs], acc[:, cs])

                @block.scalar
                def _(act):
                    o = Ops(nc, act, False)
                    act.wait_ge(S["reduced"], 1)
                    o.fn(coef[:, :], dots[:, :], ACT.Gelu_apprx_tanh, free=True).then_inc(S["exped"], 1)
                    act.wait_ge(S["stored"], 1)
                    act.wait_ge(S["got"], 1)
                    with act.Fori(0, n_iter) as i:
                        for m in range(RING):
                            n = 2 * m + 1
                            act.wait_ge(S["prod"], i * RING + (m + 1))
                            o.fn(diag[:, m % 4, :], C("ident"), ACT.Copy, scale=coef[:, bass.ds(i * BODY + n, 1)],
                                 free=True).then_inc(S["grown"], 1)

                @block.tensor
                def _(pe):
                    pe.wait_ge(S["reduced"], 1)
                    for half in range(2):
                        last = nc.tensor.matmul(k.bank(half), zero[:, :], h[:, j, half * BANK:(half + 1) * BANK],
                                                start=True, stop=False)
                    last.then_inc(S["got"], 1)
                    pe.sem_inc(S["prod"], 4)
                    with pe.Fori(0, n_iter) as i:
                        for m in range(RING):
                            n = 2 * m + 1
                            r, half = n % RING, n // RING
                            pe.wait_ge(S["grown"], i * RING + (m + 1))
                            pe.wait_ge(row[r], i * 32 + (before + 16 * (half + uses) + 16))
                            for hb in range(2):
                                last = nc.tensor.matmul(k.bank(hb), diag[:, m % 4, :],
                                                        buf[:, r, hb * BANK:(hb + 1) * BANK], start=False, stop=False)
                            last.then_inc(S["prod"], 1)
                            pe.wait_ge(S["prod"], i * RING + (m + 5))
                            pe.sem_inc(used[r], 1)
                    for half in range(2):
                        last = nc.tensor.matmul(k.bank(half), zero[:, :], h[:, j, half * BANK:(half + 1) * BANK],
                                                start=False, stop=True)
                    last.then_inc(S["summed"], 1)
            k.row_uses += 2 * uses
            k.clear()


INPUTS = ["x", "norm_ffn1", "ffn1_in", "ffn1_out", "norm_mix", "w_in", "rwkv_mu", "decay_w0", "decay_w2", "iclr_a0",
          "iclr_a2", "gate_g2", "k_k", "k_a", "r_k", "ln_x_g", "ln_x_b", "q_gain", "k_gain", "diff_lambda", "subln_g",
          "w_branch", "w_out", "norm_ffn2", "ffn2_in", "ffn2_out", "c_2", "ctx_2", "c_ctx_2", "mod_w_2", "mod_b_2",
          "norm1_g_2", "norm2_g_2", "attn_in_w_2", "attn_out_w_2", "attn_sink_2", "gmlp_w_s_2", "gmlp_b_s_2",
          "pool_w_2", "pool_scale_2", "peer_w_q_2", "peer_sub_keys_2", "peer_down_2", "peer_up_2", "final_g_2"]

SEMAPHORES = (["loaded", "turned", "copied_v", "copied_s", "squared", "rooted", "reduced", "summed", "drained",
               "used", "pre_done", "biased", "squashed", "exped", "masked", "lsum", "prod", "got", "corr",
               "grown", "done", "stored", "ids_ready", "gathers", "written"]
              + ["high", "low"] + [f"{e}_lane{g}" for e in ("pe", "act", "dve") for g in range(2)] + [f"used{r}" for r in range(8)])


def build(nc, a, out, stop=None):
    with ExitStack() as ctx:
        k = Kernel(nc, ctx, SEMAPHORES)
        load_stage(k, [(k.C[:, :], k.table_dram), (k.X[:, :, :], a["x"][0].rearrange("(j p) d -> p j d", p=P))])
        with ExitStack() as c:
            lam = k.sb("lambda_table", [P, DEPTH, 2], ctx=c)
            with nc.Block() as block:
                @block.vector
                def _(dve):
                    for l in range(DEPTH):
                        init = 0.8 - 0.6 * math.exp(-0.3 * l)
                        nc.vector.memset(lam[:, l, 0:1], init)
                        nc.vector.memset(lam[:, l, 1:2], 1.0 - init)
            k.clear()
            with nc.Fori(0, DEPTH) as l:
                first_layer(k, l, a, lam)
                k.restart_stream()
        if stop != "first":
            for l in range(DEPTH):
                with ExitStack() as c:
                    mod = k.sb("modulation", [P, 6 * D], ctx=c)
                    w_cmod = row_weights(a["mod_w_2"][0][:, 0:4 * BANK], 4, BANK)
                    w_query = row_weights(a["peer_w_q_2"][l], 8, 256)
                    modulation(k, a["c_2"][0].rearrange("(k p) -> k p", p=P), row_weights(a["mod_w_2"][l], 12, BANK),
                               a["mod_b_2"][l:l + 1, :], mod, (w_cmod, w_query)[l % 2])
                    if l % 2 == 0:
                        attn_gmlp_layer(k, a, mod, w_cmod, w_query)
                    else:
                        pool_layer(k, a, mod)
                    peer(k, a, l, mod, w_query)
        with ExitStack() as c:
            h = k.sb("normed", [P, NT, D], ctx=c)
            if stop is None:
                norm_stage(k, k.X, a["final_g_2"].rearrange("(a n) -> a n", a=1), h)
            src = h if stop is None else k.X
            with nc.Block() as block:
                @block.sync
                def _(sp):
                    sp.dma_start(out[0].rearrange("(j p) d -> p j d", p=P), src[:, :, :]).then_inc(k.sem["written"], 16)
                    sp.wait_ge(k.sem["written"], 16)


def kernel(**inputs):
    import concourse.bacc as bacc
    from concourse.bass_utils import run_bass_kernel_spmd

    nc = bacc.Bacc("TRN2", target_bir_lowering=False, num_devices=1)
    arrays, a = {}, {}
    for name in INPUTS:
        arrays[name] = np.ascontiguousarray(inputs[name])
        a[name] = nc.dram_tensor(name, arrays[name].shape, mybir.dt.from_np(arrays[name].dtype), kind="ExternalInput").ap()
    out = nc.dram_tensor("out", (1, SEQ, D), F32, kind="ExternalOutput").ap()
    build(nc, a, out)
    r = run_bass_kernel_spmd(nc, [arrays], core_ids=[0])
    return r.results[0]["out"]
```

```python
import math
from contextlib import ExitStack

import numpy as np

import concourse.bass as bass
from concourse import mybir

F32 = mybir.dt.float32
F32R = mybir.dt.float32r
U32 = mybir.dt.uint32
ALU = mybir.AluOpType
ACT = mybir.ActivationFunctionType
AX = mybir.AxisListType

P = 128
D = 1024
SEQ = 256
NT = SEQ // P
KC = D // P
DEPTH = 2
BANK = 512

DA = D // 2
HA = 64
NHA = DA // HA
LORA = 64
C_RWKV = 3 * DA + 3 * P
C_ATTN = 3 * DA
C_IN = C_RWKV + C_ATTN + 2 * D
D_FF = ((8 * D // 3 + 127) // 128) * 128
NF = D_FF // P
DECAY_SCALE = math.exp(-0.5)
GN_EPS = 64e-5
EPS = 1e-6
CH = 64
NPAIR = NHA // 2
NHB = 4

QW, KVW, AW = 512, 128, 512
IN_W = QW + 2 * KVW + 2 * AW
GROUPS = 8
POOL_WINDOWS = (2, 4, 8, 16)
PH, NK, TOPK = 8, 128, 16
SLOTS = PH * TOPK
FAR = -1e30
RING = 8
TILE = KC * BANK
WPROJ = 344


def constant_table():
    parts = {}
    i = np.arange(P)
    row, col = i[:, None], i[None, :]
    same = row // CH == col // CH
    parts["ident"] = np.eye(P)
    parts["ident2"] = np.concatenate([np.eye(CH)] * 2)
    s = np.arange(SEQ)
    neighbour = 0.5 * (np.abs(s[:, None] - s[None, :]) == 1)
    parts["shift"] = neighbour.reshape(NT, P, NT, P).transpose(1, 0, 2, 3)
    before = [row < col, row > col]
    upto = [row <= col, row >= col]
    parts["cum_incl"] = np.stack([-DECAY_SCALE * (same & u) for u in upto], 1)
    parts["cum_excl"] = np.stack([-DECAY_SCALE * (same & b) for b in before], 1)
    parts["cum_rest"] = np.stack([-DECAY_SCALE * (same & ~u) for u in upto], 1)
    parts["cum_chunk"] = -DECAY_SCALE * (row // CH == np.arange(2)[None, :])
    cr, cc = (row % CH), np.arange(CH)[None, :]
    parts["tri"] = np.stack([np.stack([b, u] * 2, 1) for b, u in ((cr < cc, cr <= cc), (cr > cc, cr >= cc))], 1)
    merge = []
    for g in range(2):
        for lv in range(6):
            b = 1 << lv
            later = (cr > cc) if g == 0 else (cr < cc)
            merge.append((cr // (2 * b) == cc // (2 * b)) & (cr // b != cc // b) & later)
    parts["merge"] = np.stack(merge, 1).reshape(P, 2, 6, CH)
    parts["iota16"] = np.broadcast_to(np.arange(16), (P, 16))
    place, at, flat = {}, 0, []
    for name, a in parts.items():
        a = np.ascontiguousarray(np.asarray(a, np.float32))
        shape = a.shape[1:]
        n = int(np.prod(shape))
        place[name] = (at, n, shape)
        flat.append(a.reshape(P, n))
        at += n
    return np.concatenate(flat, 1), place


def distance_tables():
    q = np.arange(P)[:, None, None] + P * np.arange(NT)[None, :, None]
    dist = np.abs(q - np.arange(SEQ)[None, None, :])
    return (-dist).astype(np.float32), np.where(dist <= 128, 0.0, FAR).astype(np.float32)


def rope_table():
    inv = np.power(np.float32(10000.0), -np.arange(16, dtype=np.float32) / np.float32(16)).astype(np.float32)
    t = np.arange(SEQ)
    ang = np.stack([(t // 64).astype(np.float32)[:, None] * inv, (t % 64).astype(np.float32)[:, None] * inv], 1)
    ang = ang.astype(np.float32).reshape(NT, P, 2, 16).transpose(1, 0, 2, 3)
    return np.ascontiguousarray(np.stack([np.cos(ang), np.sin(ang)], 1).astype(np.float32))


def pool_table():
    t = np.arange(SEQ)
    pool = []
    for w in POOL_WINDOWS:
        lo, hi = np.clip(t - w // 2, 0, SEQ), np.clip(t + w // 2, 0, SEQ)
        m = ((t[:, None] >= lo[None, :]) & (t[:, None] < hi[None, :])) / (hi - lo)[None, :].astype(np.float64)
        pool.append((m - np.eye(SEQ)).reshape(NT, P, SEQ))
    return np.ascontiguousarray(np.stack(pool).transpose(2, 0, 1, 3).astype(np.float32))


class Ops:

    def __init__(self, nc, eng, vector):
        self.nc, self.eng, self.on_vector = nc, eng, vector

    def _order(self, free):
        if not free:
            self.eng.drain()

    def tt(self, out, a, b, op, free=False):
        self._order(free)
        return self.nc.vector.tensor_tensor(out, a, b, op)

    def mul(self, out, a, b, free=False):
        return self.tt(out, a, b, ALU.mult, free)

    def add(self, out, a, b, free=False):
        return self.tt(out, a, b, ALU.add, free)

    def sub(self, out, a, b, free=False):
        return self.tt(out, a, b, ALU.subtract, free)

    def ts(self, out, a, s1, op0, s2=None, op1=None, free=False):
        self._order(free)
        if op1 is None:
            return self.nc.vector.tensor_scalar(out, a, s1, None, op0)
        return self.nc.vector.tensor_scalar(out, a, s1, s2, op0, op1)

    def stt(self, out, a, s, b, op0, op1, free=False):
        self._order(free)
        return self.nc.vector.scalar_tensor_tensor(out=out, in0=a, scalar=s, in1=b, op0=op0, op1=op1)

    def dot(self, out, a, b, total, free=False):
        self._order(free)
        return self.nc.vector.tensor_tensor_reduce(out=out, in0=a, in1=b, scale=1.0, scalar=0.0,
                                                   op0=ALU.mult, op1=ALU.add, accum_out=total)

    def sum(self, out, a, free=False):
        self._order(free)
        return self.nc.vector.reduce_sum(out, a, AX.X)

    def max(self, out, a, free=False):
        self._order(free)
        return self.nc.vector.reduce_max(out, a, AX.X)

    def copy(self, out, a, free=False):
        self._order(free)
        if self.on_vector:
            return self.nc.vector.tensor_copy(out, a)
        return self.nc.scalar.copy(out, a)

    def recip(self, out, a, free=False):
        self._order(free)
        return self.nc.vector.reciprocal(out, a)

    def fn(self, out, a, func, scale=1.0, bias=0.0, total=None, free=False):
        self._order(free)
        kw = {} if total is None else {"accum_out": total}
        return self.nc.scalar.activation(out, a, func, bias=bias, scale=scale, **kw)


class Kernel:

    def __init__(self, nc, ctx, sems):
        self.nc, self.ctx = nc, ctx
        self.sem, self.names = {}, 0
        for name in sems:
            self.sem[name] = ctx.enter_context(nc.semaphore(name))
        nums = [s.num for s in self.sem.values()]
        self.span = range(min(nums), max(nums) + 1)
        assert len(self.span) == len(nums)
        self.rows = [ctx.enter_context(nc.semaphore(f"row{r}")) for r in range(RING)]
        self.row_uses = 0
        self.arrived = [ctx.enter_context(nc.semaphore(f"arrived{u}")) for u in range(2)]
        self.fills = [0, 0]
        self.preloaded = False
        self.table, self.place = constant_table()
        self.table_dram = nc.inline_tensor(self.table, name="shape_constants").ap()
        self.C = self.sb("constants", [P, self.table.shape[1]])
        self.X = self.sb("residual", [P, NT, D])
        self.raw = self.sb("raw_weights", [P, 2, TILE])
        self.ps = ctx.enter_context(nc.psum_tensor("banks", [P, 8, BANK], F32))

    def sb(self, name, shape, dt=F32, ctx=None):
        self.names += 1
        return (ctx or self.ctx).enter_context(self.nc.sbuf_tensor(f"{name}_{self.names}", shape, dt))

    def const(self, name):
        at, n, shape = self.place[name]
        a = self.C[:, at:at + n]
        if len(shape) == 1:
            return a
        names = "abc"[:len(shape)]
        return a.rearrange(f"p ({' '.join(names)}) -> p {' '.join(names)}", **dict(zip(names, shape)))

    def bank(self, b, *dims):
        a = self.ps[:, b, :]
        if dims:
            n = int(np.prod(dims))
            names = "abc"[:len(dims)]
            a = a[:, 0:n].rearrange(f"p ({' '.join(names)}) -> p {' '.join(names)}", **dict(zip(names, dims)))
        return a

    def restart_stream(self):
        for u in range(2):
            self.nc.gpsimd.sem_clear(self.arrived[u])
        self.nc.all_engine_barrier()
        self.fills = [0, 0]

    def clear(self):
        self.nc.gpsimd.sem_clear(self.span)
        self.nc.all_engine_barrier()


def spread(ap, n):
    return ap.unsqueeze(2).to_broadcast([ap.shape[0], ap.shape[1], n])


def over(ap, n):
    return ap.unsqueeze(1).to_broadcast([ap.shape[0], n, ap.shape[1]])


def rows(ap):
    return ap.to_broadcast([P, ap.shape[1]])



def load_stage(k, pairs, ahead=None):
    nc = k.nc
    with nc.Block() as block:
        @block.sync
        def _(sp):
            for dst, src in pairs:
                sp.dma_start(dst, src).then_inc(k.sem["loaded"], 16)
            if ahead is not None:
                preload(k, sp, ahead)
            sp.wait_ge(k.sem["loaded"], 16 * len(pairs))
    k.clear()


def turn_stage(k, jobs):
    nc = k.nc
    turned, copied_v, copied_s = k.sem["turned"], k.sem["copied_v"], k.sem["copied_s"]
    ident = k.const("ident")
    with nc.Block() as block:
        @block.tensor
        def _(pe):
            for n, (sources, _) in enumerate(jobs):
                if n >= 8:
                    pe.wait_ge(copied_s if n % 2 else copied_v, (n - 8) // 2 + 1)
                for c, src in enumerate(sources):
                    last = nc.tensor.transpose(k.bank(n % 8)[:, c * P:c * P + P], src, ident)
                last.then_inc(turned, 1)

        @block.vector
        def _(dve):
            for n, (sources, dst) in enumerate(jobs):
                if n % 2 == 0:
                    dve.wait_ge(turned, n + 1)
                    nc.vector.tensor_copy(dst, k.bank(n % 8, len(sources), P)).then_inc(copied_v, 1)

        @block.scalar
        def _(act):
            for n, (sources, dst) in enumerate(jobs):
                if n % 2 == 1:
                    act.wait_ge(turned, n + 1)
                    nc.scalar.copy(dst, k.bank(n % 8, len(sources), P)).then_inc(copied_s, 1)
    k.clear()


def turn_tokens(k, src, dst, chunks):
    jobs = []
    for j in range(NT):
        for c0 in range(0, chunks, 4):
            cs = range(c0, min(c0 + 4, chunks))
            jobs.append(([src[:, j, c * P:c * P + P] for c in cs],
                         dst[:, c0:c0 + len(cs), j * P:j * P + P]))
    (turn_split_stage if isinstance(dst, Split) else turn_stage)(k, jobs)


def norm_stage(k, x, gain, out, scale_row=None, shift_row=None, ahead=None, turned_to=None, extra=None):
    nc = k.nc
    loaded, squared, rooted = k.sem["loaded"], k.sem["squared"], k.sem["rooted"]
    group = lambda to, n: to[:, n % 2 * 4:n % 2 * 4 + 4, n // 2 * P:n // 2 * P + P]
    reduced = k.sem["reduced"]
    with ExitStack() as c:
        g = k.sb("gain", [P, D], ctx=c)
        junk = k.sb("junk", [P, D], ctx=c)
        ss = k.sb("square_sums", [P, NT], ctx=c)
        rs = k.sb("root", [P, NT], ctx=c)
        with nc.Block() as block:
            @block.sync
            def _(sp):
                sp.dma_start(g[:, :], rows(gain)).then_inc(loaded, 16)
                if ahead is not None:
                    preload(k, sp, ahead)
                if extra is not None:
                    sp.dma_start(*extra).then_inc(k.sem["written"], 16)
                    sp.wait_ge(k.sem["written"], 16)

            @block.scalar
            def _(act):
                o = Ops(nc, act, False)
                for j in range(NT):
                    o.fn(junk[:, :], x[:, j, :], ACT.Square, total=ss[:, j:j + 1]).then_inc(squared, 1)
                act.wait_ge(reduced, 1)
                o.fn(rs[:, :], rs[:, :], ACT.Sqrt).then_inc(rooted, 1)
                if turned_to is not None:
                    for n in range(2 * NT):
                        act.wait_ge(k.sem["turned"], n + 1)
                        o.copy(group(turned_to.hi, n), k.bank(n, 4, P), free=True).then_inc(k.sem["copied_s"], 1)

            if turned_to is not None:
                @block.tensor
                def _(pe):
                    for n in range(2 * NT):
                        pe.wait_ge(k.sem["stored"], n // 2 + 1)
                        for i in range(4):
                            last = nc.tensor.transpose(k.bank(n)[:, i * P:(i + 1) * P],
                                                       out[:, n // 2, (n % 2 * 4 + i) * P:(n % 2 * 4 + i + 1) * P],
                                                       k.const("ident"))
                        last.then_inc(k.sem["turned"], 1)

            @block.vector
            def _(dve):
                o = Ops(nc, dve, True)
                dve.wait_ge(squared, NT)
                o.ts(rs[:, :], ss[:, :], 1.0 / D, ALU.mult, EPS, ALU.add).then_inc(reduced, 1)
                dve.wait_ge(rooted, 1)
                o.recip(rs[:, :], rs[:, :])
                dve.wait_ge(loaded, 16)
                if scale_row is not None:
                    o.stt(g[:, :], scale_row, 1.0, g[:, :], ALU.add, ALU.mult)
                for j in range(NT):
                    last = o.stt(out[:, j, :], x[:, j, :], rs[:, j:j + 1], g[:, :], ALU.mult, ALU.mult)
                    if shift_row is not None:
                        last = o.add(out[:, j, :], out[:, j, :], shift_row)
                    last.then_inc(k.sem["stored"], 1)
                if turned_to is not None:
                    for n in range(2 * NT):
                        dve.wait_ge(k.sem["copied_s"], n + 1)
                        o.sub(group(turned_to.lo, n), k.bank(n, 4, P), group(turned_to.hi, n).bitcast(F32), free=True)
    k.clear()


def steps(eng, lo, hi, body):
    pairs = (hi - lo) // 2
    if pairs > 1:
        with eng.Fori(0, pairs) as i:
            for d in range(2):
                body(i * 2 + (lo + d), (lo + d) % 2, i + (lo + d) // 2)
    else:
        pairs = 0
    for t in range(lo + 2 * pairs, hi):
        body(t, t % 2, t // 2)


class Split:

    def __init__(self, hi, lo):
        self.hi, self.lo = hi, lo

    def __getitem__(self, at):
        return Split(self.hi[at], self.lo[at])

    def rearrange(self, *a, **kw):
        return Split(self.hi.rearrange(*a, **kw), self.lo.rearrange(*a, **kw))


def split_sb(k, name, shape, ctx):
    return Split(k.sb(name + "_hi", shape, F32R, ctx), k.sb(name + "_lo", shape, F32R, ctx))


def multiply(nc, out, lhs, rhs, start, stop):
    nc.tensor.matmul(out, lhs.hi, rhs.hi, start=start, stop=False)
    nc.tensor.matmul(out, lhs.hi, rhs.lo, start=False, stop=False)
    return nc.tensor.matmul(out, lhs.lo, rhs.hi, start=False, stop=stop)


def turn_split_stage(k, jobs):
    nc = k.nc
    turned, high, low = k.sem["turned"], k.sem["copied_s"], k.sem["copied_v"]
    with nc.Block() as block:
        @block.tensor
        def _(pe):
            for n, (sources, _) in enumerate(jobs):
                if n >= 8:
                    pe.wait_ge(low, n - 7)
                for c, src in enumerate(sources):
                    last = nc.tensor.transpose(k.bank(n % 8)[:, c * P:c * P + P], src, k.const("ident"))
                last.then_inc(turned, 1)

        @block.scalar
        def _(act):
            for n, (sources, dst) in enumerate(jobs):
                act.wait_ge(turned, n + 1)
                nc.scalar.copy(dst.hi, k.bank(n % 8, len(sources), P)).then_inc(high, 1)

        @block.vector
        def _(dve):
            for n, (sources, dst) in enumerate(jobs):
                dve.wait_ge(high, n + 1)
                nc.vector.tensor_tensor(dst.lo, k.bank(n % 8, len(sources), P), dst.hi.bitcast(F32),
                                        ALU.subtract).then_inc(low, 1)
    k.clear()


class Weights:

    def __init__(self, tiles, pieces):
        self.tiles, self.pieces = tiles, pieces

    def load(self, k, sp, t, u):
        for at, shape, src in self.pieces(t):
            n = int(np.prod(shape))
            names = "ab"[:len(shape)]
            dst = k.raw[:, u, at:at + n].rearrange(f"p ({' '.join(names)}) -> p {' '.join(names)}",
                                                   **dict(zip(names, shape)))
            sp.dma_start(dst, src).then_inc(k.arrived[u], 16)

    def per_tile(self):
        return 16 * len(self.pieces(0))


def row_weights(w, tiles, width, kc=KC):
    view = w.rearrange("(k p) n -> p k n", p=P)
    return Weights(tiles, lambda t: [(0, (kc, width), view[:, :, bass.ds(t * width, width)])])


def pair_weights(w, cols):
    view = w.rearrange("(k p) n -> p k n", p=P)
    return Weights(cols // 256, lambda t: [(h * KC * 256, (KC, 256), view[:, :, bass.ds(t * 256 + h * cols, 256)])
                                           for h in range(2)])


def sum_weights(w, kc):
    view = w.rearrange("(k p) n -> p k n", p=P)
    step = 2
    return Weights(kc // step, lambda t: [(0, (step, D), view[:, bass.ds(t * step, step), :])])


def preload(k, sp, wts):
    for t in range(min(2, wts.tiles)):
        wts.load(k, sp, t, t)
    k.preloaded = True


def stream(k, block, wts, ahead, size, parts, done, done_per, finish_steps, act_steps=None):
    nc = k.nc
    high, low = k.sem["high"], k.sem["low"]
    tiles, per = wts.tiles, wts.per_tile()
    base = [f * 1 for f in k.fills]
    first = min(2, tiles) if k.preloaded else 0

    @block.sync
    def _(sp):
        for t in range(first, min(2, tiles)):
            wts.load(k, sp, t, t)

        def load(t, u, m):
            sp.wait_ge(low, t - 1)
            wts.load(k, sp, t, u)

        steps(sp, 2, tiles, load)
        if ahead is not None:
            for t in range(min(2, ahead.tiles)):
                sp.wait_ge(low, tiles)
                ahead.load(k, sp, t, t)

    @block.scalar
    def _(act):
        def part(t, u, m):
            act.wait_ge(k.arrived[u], m * per + (base[u] + per))
            if not (isinstance(t, int) and t < 2):
                act.wait_ge(done, t * done_per - done_per)
            nc.scalar.copy(parts.hi[:, u, :], k.raw[:, u, 0:size]).then_inc(high, 1)

        o = Ops(nc, act, False)

        def both(t, u, m):
            part(t, u, m)
            if act_steps is not None:
                act_steps(act, o, t - 1, 1 - u)

        part(0, 0, 0)
        if tiles > 1:
            both(1, 1, 0)
        steps(act, 2, tiles, both)
        if act_steps is not None:
            act_steps(act, o, tiles - 1, (tiles - 1) % 2)

    @block.vector
    def _(dve):
        o = Ops(nc, dve, True)

        def part(t, u, m):
            dve.wait_ge(high, t + 1)
            nc.vector.tensor_tensor(parts.lo[:, u, :], k.raw[:, u, 0:size], parts.hi[:, u, :].bitcast(F32),
                                    ALU.subtract).then_inc(low, 1)

        part(0, 0, 0)

        def both(t, u, m):
            part(t, u, m)
            finish_steps(dve, o, t - 1, 1 - u)

        steps(dve, 1, tiles, both)
        finish_steps(dve, o, tiles - 1, (tiles - 1) % 2)

    for t in range(tiles):
        k.fills[t % 2] += per
    k.preloaded = ahead is not None


def slot(parts, u, **dims):
    names = " ".join(dims)
    return parts[:, u, :].rearrange(f"p ({names}) -> p {names}", **dims)


def linear_stage(k, lhs, wts, width, finish, ahead=None, groups=NT):
    nc = k.nc
    summed, drained = k.sem["summed"], k.sem["drained"]
    size = KC * width
    with ExitStack() as c, nc.Block() as block:
        parts = split_sb(k, "weight_parts", [P, 2, size], c)

        @block.tensor
        def _(pe):
            def tile(t, u, m):
                pe.wait_ge(k.sem["low"], t + 1)
                w = slot(parts, u, k=KC, n=width)
                for j in range(groups):
                    if not (isinstance(t, int) and t < 2):
                        pe.wait_ge(drained, t * groups + (j + 1 - 2 * groups))
                    for kc_ in range(KC):
                        last = multiply(nc, k.bank(u * groups + j)[:, 0:width], lhs(kc_, j), w[:, kc_, :], kc_ == 0, kc_ == KC - 1)
                    last.then_inc(summed, 1)

            for t in range(min(2, wts.tiles)):
                tile(t, t, 0)
            steps(pe, 2, wts.tiles, tile)

        def finish_steps(dve, o, t, u):
            for j in range(groups):
                dve.wait_ge(summed, t * groups + (j + 1))
                finish(o, t, j, k.bank(u * groups + j)[:, 0:width]).then_inc(drained, 1)

        stream(k, block, wts, ahead, size, parts, summed, groups, finish_steps)
    k.clear()


def linear_sum_stage(k, lhsT, kc, wts, finish, ahead=None):
    nc = k.nc
    used = k.sem["used"]
    step = kc // wts.tiles
    with ExitStack() as c, nc.Block() as block:
        parts = split_sb(k, "weight_parts", [P, 2, step * D], c)

        @block.tensor
        def _(pe):
            for t in range(wts.tiles):
                pe.wait_ge(k.sem["low"], t + 1)
                w = slot(parts, t % 2, k=step, n=D)
                for b in range(2 * NT):
                    j, half = b // 2, b % 2
                    for s in range(step):
                        last = multiply(nc, k.bank(b), lhsT[:, t * step + s, j * P:j * P + P],
                                        w[:, s, half * BANK:(half + 1) * BANK],
                                        t + s == 0, t == wts.tiles - 1 and s == step - 1)
                    if t == wts.tiles - 1:
                        last.then_inc(k.sem["summed"], 1)
                if t < wts.tiles - 1:
                    last.then_inc(used, 1)

        def finish_steps(dve, o, t, u):
            if isinstance(t, int) and t == wts.tiles - 1:
                for b in range(2 * NT):
                    dve.wait_ge(k.sem["summed"], b + 1)
                    finish(o, b // 2, b % 2, k.bank(b))

        stream(k, block, wts, ahead, step * D, parts, used, 1, finish_steps)
    k.clear()


def linear_turned_stage(k, rhs, wts, halves, finish, pre=None, ahead=None):
    nc = k.nc
    summed, drained, pre_done = k.sem["summed"], k.sem["drained"], k.sem["pre_done"]
    size = halves * KC * 256
    with ExitStack() as c, nc.Block() as block:
        parts = split_sb(k, "weight_parts", [P, 2, size], c)

        @block.tensor
        def _(pe):
            def tile(t, u, m):
                pe.wait_ge(k.sem["low"], t + 1)
                w = slot(parts, u, h=halves, k=KC, n=256)
                for s in range(2):
                    if not (isinstance(t, int) and t < 2):
                        pe.wait_ge(drained, t * 2 + (s - 3))
                    for h in range(halves):
                        for kc_ in range(KC):
                            last = multiply(nc, k.bank(2 * u + s)[:, h * SEQ:(h + 1) * SEQ],
                                            w[:, h, kc_, s * P:s * P + P], rhs[:, kc_, :], kc_ == 0, kc_ == KC - 1)
                    last.then_inc(summed, 1)

            for t in range(min(2, wts.tiles)):
                tile(t, t, 0)
            steps(pe, 2, wts.tiles, tile)

        def finish_steps(dve, o, t, u):
            for s in range(2):
                v = 2 * u + s
                dve.wait_ge(summed if pre is None else pre_done, t * 2 + (s + 1))
                finish(o, t * 2 + s, v, k.bank(v)).then_inc(drained, 1)

        def act_steps(act, o, t, u):
            for s in range(2):
                v = 2 * u + s
                act.wait_ge(summed, t * 2 + (s + 1))
                pre(o, t * 2 + s, v, k.bank(v)).then_inc(pre_done, 1)

        stream(k, block, wts, ahead, size, parts, summed, 2, finish_steps, None if pre is None else act_steps)
    k.clear()



def swiglu(k, gain, w_in, w_out, ahead):
    with ExitStack() as c:
        hT = split_sb(k, "normedT", [P, KC, SEQ], c)
        with ExitStack() as c1:
            h = k.sb("normed", [P, NT, D], ctx=c1)
            norm_stage(k, k.X, gain, h, ahead=None if k.preloaded else w_in, turned_to=hT)
        actT = split_sb(k, "hiddenT", [P, NF, SEQ], c)
        gated = k.sb("silu_gate", [P, 4, SEQ], ctx=c)
        hidden = k.sb("hidden", [P, 4, SEQ], ctx=c)

        def pre(o, n, v, bank):
            return o.fn(gated[:, v, :], bank[:, 0:SEQ], ACT.Silu, free=True)

        def finish(o, n, v, bank):
            o.mul(hidden[:, v, :], gated[:, v, :], bank[:, SEQ:], free=True)
            hi, lo = (x[:, bass.ds(n, 1), :].rearrange("p a n -> p (a n)") for x in (actT.hi, actT.lo))
            o.copy(hi, hidden[:, v, :])
            return o.sub(lo, hidden[:, v, :], hi.bitcast(F32))

        linear_turned_stage(k, hT, w_in, 2, finish, pre, w_out)

        def residual(o, j, half, bank):
            x = k.X[:, j, half * BANK:(half + 1) * BANK]
            return o.stt(x, bank, 0.5, x, ALU.mult, ALU.add, free=True)

        linear_sum_stage(k, actT, NF, w_out, residual, ahead)


def project(k, gain, wts, width, out, mod=(None, None), ahead=None):
    with ExitStack() as c:
        h = k.sb("normed", [P, NT, D], ctx=c)
        hT = split_sb(k, "normedT", [P, KC, SEQ], c)
        norm_stage(k, k.X, gain, h, *mod, turned_to=hT)
        linear_stage(k, lambda c_, j: hT[:, c_, j * P:j * P + P], wts, width,
                     lambda o, t, j, bank: o.copy(out[:, j, bass.ds(t * width, width)], bank, free=True), ahead)


def rwkv(k, proj, mu, w0, w2, a0, a2, g2, k_k, k_a, r_k, ln_g, ln_b, out):
    nc = k.nc
    y = out
    with ExitStack() as c:
        p = proj
        sig = k.sb("decay_sigmoid", [P, 2, NT, DA], ctx=c)
        kk = k.sb("kk", [P, NT, DA], ctx=c)
        kd = k.sb("k_dir", [P, 2, NT, DA], ctx=c)
        beta = k.sb("beta", [P, 2, NT, DA], ctx=c)
        bonus = k.sb("bonus", [P, NT, NHA], ctx=c)
        tail = c.enter_context(ExitStack())
        wl = k.sb("lora_w", [P, 3, DA], ctx=tail)
        bias = k.sb("lora_bias", [P, 2, 2, DA], ctx=tail)
        per = k.sb("per_channel", [P, 3, DA], ctx=tail)
        pairs = [(wl[:, 0, :], w2), (wl[:, 1, :], a2), (wl[:, 2, :], g2),
                 (bias[:, 0, 0], rows(w0[0])), (bias[:, 0, 1], rows(w0[1])),
                 (bias[:, 1, 0], rows(a0[0])), (bias[:, 1, 1], rows(a0[1])),
                 (per[:, 0], rows(k_k)), (per[:, 1], rows(k_a)), (per[:, 2], rows(r_k))]
        cw = C_RWKV // 4
        with ExitStack() as c1:
            mur = k.sb("mu", [P, C_RWKV], ctx=c1)
            delta = k.sb("delta", [P, NT, 4, cw], ctx=c1)
            loaded, summed = k.sem["loaded"], k.sem["summed"]
            with nc.Block() as block:
                @block.sync
                def _(sp):
                    sp.dma_start(mur[:, :], rows(mu)).then_inc(loaded, 16)
                    for dst, src in pairs:
                        sp.dma_start(dst, src).then_inc(k.sem["written"], 16)
                    sp.wait_ge(k.sem["written"], 16 * len(pairs))

                @block.tensor
                def _(pe):
                    for j in range(NT):
                        for q in range(4):
                            for s in range(NT):
                                last = nc.tensor.matmul(k.bank(4 * j + q)[:, 0:cw], k.const("shift")[:, s, j, :],
                                                        proj[:, s, q * cw:(q + 1) * cw], start=s == 0, stop=s == NT - 1)
                            last.then_inc(summed, 1)

                @block.vector
                def _(dve):
                    o = Ops(nc, dve, True)
                    dve.wait_ge(loaded, 16)
                    for j in range(NT):
                        for q in range(4):
                            dve.wait_ge(summed, 4 * j + q + 1)
                            o.sub(delta[:, j, q, :], k.bank(4 * j + q)[:, 0:cw], proj[:, j, q * cw:(q + 1) * cw], free=True)
                        o.mul(delta[:, j], delta[:, j], mur[:, :].rearrange("p (q n) -> p q n", q=4))
                    for j in range(NT):
                        o.add(proj[:, j, 0:C_RWKV], proj[:, j, 0:C_RWKV], delta[:, j].rearrange("p q n -> p (q n)"))
            k.clear()
        r, kx, v = (p[:, :, n * DA:(n + 1) * DA] for n in range(3))
        gate = kx
        with ExitStack() as c1:
            low = k.sb("low", [P, NT, 3 * P], ctx=c1)
            lowT = k.sb("lowT", [P, 3, SEQ], ctx=c1)
            a = k.sb("iclr", [P, 2, NT, DA], ctx=c1)
            pre = k.sb("before_sigmoid", [P, 2, DA], ctx=c1)
            t1 = k.sb("scratch", [P, NT, DA], ctx=c1)
            nrm = k.sb("norms", [P, NT, NHA], ctx=c1)
            gate_now = k.sb("gate_now", [P, NT, DA], ctx=c1)
            with nc.Block() as block:
                @block.scalar
                def _(act):
                    o = Ops(nc, act, False)
                    l0 = 3 * DA
                    o.fn(low[:, :, 0:P], p[:, :, l0:l0 + P], ACT.Tanh, free=True)
                    o.copy(low[:, :, P:2 * P], p[:, :, l0 + P:l0 + 2 * P], free=True)
                    o.fn(low[:, :, 2 * P:], p[:, :, l0 + 2 * P:C_RWKV], ACT.Sigmoid, free=True)
            k.clear()
            turn_tokens(k, low, lowT, 3)
            jobs = [(what, g, j) for what in range(2) for g in range(2) for j in range(NT)]
            summed, biased, squashed = k.sem["summed"], k.sem["biased"], k.sem["squashed"]
            with nc.Block() as block:
                @block.tensor
                def _(pe):
                    for n, (what, g, j) in enumerate(jobs):
                        nc.tensor.matmul(k.bank(n), lowT[g * LORA:(g + 1) * LORA, what, j * P:j * P + P],
                                         wl[g * LORA:(g + 1) * LORA, what, :], start=True, stop=True).then_inc(summed, 1)
                    for j in range(NT):
                        pe.wait_ge(biased, 2)
                        nc.tensor.matmul(k.bank(j), lowT[:, 2, j * P:j * P + P], wl[:, 2, :],
                                         start=True, stop=True).then_inc(summed, 1)

                @block.scalar
                def _(act):
                    o = Ops(nc, act, False)
                    for n, (what, g, j) in enumerate(jobs):
                        act.wait_ge(biased, n + 1)
                        dst = (sig, a)[what]
                        o.fn(dst[:, g, j, :], pre[:, n % 2, :], ACT.Sigmoid, free=True).then_inc(squashed, 1)

                @block.vector
                def _(dve):
                    o = Ops(nc, dve, True)
                    for n, (what, g, j) in enumerate(jobs):
                        dve.wait_ge(summed, n + 1)
                        if n >= 2:
                            dve.wait_ge(squashed, n - 1)
                        o.add(pre[:, n % 2, :], k.bank(n), bias[:, what, g, :], free=True).then_inc(biased, 1)
                    for j in range(NT):
                        dve.wait_ge(summed, len(jobs) + j + 1)
                        o.copy(gate_now[:, j, :], k.bank(j), free=True)
                    for j in range(NT):
                        o.mul(kk[:, j, :], kx[:, j, :], per[:, 0, :])
                        o.mul(t1[:, j, :], kk[:, j, :], kk[:, j, :])
                        o.sum(nrm[:, j, :], t1[:, j, :].rearrange("p (h n) -> p h n", h=NHA))
                    o.copy(nrm[:, :, :], nrm[:, :, :]).then_inc(k.sem["reduced"], 1)
            k.clear()
            with nc.Block() as block:
                @block.scalar
                def _(act):
                    nc.scalar.activation(nrm[:, :, :], nrm[:, :, :], ACT.Sqrt).then_inc(k.sem["rooted"], 1)

                @block.vector
                def _(dve):
                    o = Ops(nc, dve, True)
                    dve.wait_ge(k.sem["rooted"], 1)
                    o.ts(nrm[:, :, :], nrm[:, :, :], 1e-12, ALU.max)
                    o.recip(nrm[:, :, :], nrm[:, :, :])
                    for j in range(NT):
                        h3 = kk[:, j, :].rearrange("p (h n) -> p h n", h=NHA)
                        o.mul(h3, h3, spread(nrm[:, j, :], HA))
                    for g in range(2):
                        for j in range(NT):
                            o.stt(kd[:, g, j, :], a[:, g, j, :], -1.0, per[:, 1, :], ALU.add, ALU.mult)
                            o.stt(kd[:, g, j, :], kd[:, g, j, :], 1.0, kx[:, j, :], ALU.add, ALU.mult)
                            o.mul(beta[:, g, j, :], kk[:, j, :], a[:, g, j, :], free=True)
                    for j in range(NT):
                        o.add(t1[:, j, :], kd[:, 0, j, :], kd[:, 1, j, :])
                        o.mul(t1[:, j, :], t1[:, j, :], r[:, j, :])
                        o.mul(t1[:, j, :], t1[:, j, :], per[:, 2, :])
                        o.sum(bonus[:, j, :], t1[:, j, :].rearrange("p (h n) -> p h n", h=NHA))
                        o.copy(gate[:, j, :], gate_now[:, j, :], free=True)
            k.clear()
        tail.close()
        qT = k.sb("queryT", [P, 2, NT, 2, NPAIR, CH], ctx=c)
        move = k.sb("transition", [P, 2, NT, 2, NPAIR, HA], ctx=c)
        fresh = k.sb("fresh_state", [P, 2, NT, 2, NPAIR, HA], ctx=c)
        rwkv_tiles(k, r, kk, kd, beta, v, sig, qT, move, fresh, y)
        rwkv_states(k, qT, move, fresh, y)
        with ExitStack() as c1:
            lg = k.sb("ln_gain", [P, DA], ctx=c1)
            lb = k.sb("ln_bias", [P, DA], ctx=c1)
            t1 = k.sb("scratch", [P, NT, DA], ctx=c1)
            mean = k.sb("mean", [P, NT, NHA], ctx=c1)
            var = k.sb("var", [P, NT, NHA], ctx=c1)
            with nc.Block() as block:
                @block.sync
                def _(sp):
                    sp.dma_start(lg[:, :], rows(ln_g)).then_inc(k.sem["loaded"], 16)
                    sp.dma_start(lb[:, :], rows(ln_b)).then_inc(k.sem["loaded"], 16)

                @block.scalar
                def _(act):
                    act.wait_ge(k.sem["reduced"], 1)
                    nc.scalar.activation(var[:, :, :], var[:, :, :], ACT.Sqrt).then_inc(k.sem["rooted"], 1)

                @block.vector
                def _(dve):
                    o = Ops(nc, dve, True)
                    for j in range(NT):
                        h3 = y[:, j, :].rearrange("p (h n) -> p h n", h=NHA)
                        t3 = t1[:, j, :].rearrange("p (h n) -> p h n", h=NHA)
                        o.sum(mean[:, j, :], h3)
                        o.ts(mean[:, j, :], mean[:, j, :], 1.0 / HA, ALU.mult)
                        o.sub(h3, h3, spread(mean[:, j, :], HA))
                        o.mul(t3, h3, h3)
                        o.sum(var[:, j, :], t3)
                    o.ts(var[:, :, :], var[:, :, :], 1.0 / HA, ALU.mult, GN_EPS, ALU.add).then_inc(k.sem["reduced"], 1)
                    dve.wait_ge(k.sem["rooted"], 1)
                    o.recip(var[:, :, :], var[:, :, :])
                    dve.wait_ge(k.sem["loaded"], 32)
                    for j in range(NT):
                        h3 = y[:, j, :].rearrange("p (h n) -> p h n", h=NHA)
                        t3 = t1[:, j, :].rearrange("p (h n) -> p h n", h=NHA)
                        o.mul(h3, h3, spread(var[:, j, :], HA))
                        o.mul(y[:, j, :], y[:, j, :], lg[:, :])
                        o.add(y[:, j, :], y[:, j, :], lb[:, :])
                        o.mul(t3, v[:, j, :].rearrange("p (h n) -> p h n", h=NHA), spread(bonus[:, j, :], HA))
                        o.add(y[:, j, :], y[:, j, :], t1[:, j, :])
                        o.mul(y[:, j, :], y[:, j, :], gate[:, j, :])
            k.clear()


class Milestones:

    def __init__(self, names):
        self.names = names

    def count(self, unit, name):
        return unit * len(self.names) + self.names.index(name) + 1


LEVELS = range(1, 6)
ON_PE = Milestones(["excl", "incl", "rest", "chunk"] + [f"turn{q}" for q in range(4)] + [f"score{b}" for b in range(4)]
                   + ["natural", "akv"] + [f"{w}{n}" for n in LEVELS for w in ("g", "c")]
                   + ["xa", "u0", "qm", "y", "fresh"])
ON_ACT = Milestones(["excl", "incl", "inverse", "rest", "chunk"] + [f"turn{q}" for q in range(4)])
ON_DVE = Milestones(["scaled", "ends"] + [f"score{b}" for b in range(4)] + ["x0", "akv"]
                    + [f"{w}{n}" for n in LEVELS for w in ("g", "x")] + ["xa", "u0", "qm", "y", "fresh"])


def rwkv_tiles(k, r, kk, kd, beta, v, sig, qT, move, fresh, y):
    nc = k.nc
    C = k.const
    A, R, B, K = range(4)
    heads = [2 * q + e for e in range(2) for q in range(NPAIR)]
    cols = [slice(h * HA, h * HA + HA) for h in range(NHA)]
    chunks = [slice(ch * CH, ch * CH + CH) for ch in range(2)]
    on_pe, on_act, on_dve = ([k.sem[f"{e}_lane{g}"] for g in range(2)] for e in ("pe", "act", "dve"))

    def grid(ap, *dims):
        names = "abc"[:len(dims)]
        return ap.rearrange(f"p ({' '.join(names)}) -> p {' '.join(names)}", **dict(zip(names, dims)))

    with ExitStack() as c:
        lanes = []
        for g in range(2):
            if g == 0:
                ex = k.sb("decays", [P, 4, DA], ctx=c)
                m = k.sb("scaled", [P, 4, DA], ctx=c)
                mT = k.sb("scaledT", [P, NPAIR, 4, P], ctx=c)
                s1 = k.sb("scores", [P, NHA, 4, CH], ctx=c)
            else:
                half = TILE // 2
                mT = grid(k.raw[:, 0, 0:half], NPAIR, 4, P)
                s1 = grid(k.raw[:, 0, half:], NHA, 4, CH)
                ex = grid(k.raw[:, 1, 0:half], 4, DA)
                m = grid(k.raw[:, 1, half:], 4, DA)
            ends = k.sb("ends", [P, 2, DA], ctx=c)
            x = k.sb("inverse", [P, NHA, CH], ctx=c)
            dw = k.sb("decay_diagonal", [P, 2, NPAIR, HA], ctx=c)
            wc = k.sb("chunk_decay", [P, 2, NPAIR], ctx=c)
            xT, gm = (grid(ex[:, n, :], NHA, CH) for n in range(2))
            akv, xa, u0 = ex[:, 2, :], ex[:, 3, :], m[:, R, :]
            lanes.append((ex, m, mT, s1, ends, x, dw, wc, xT, gm, akv, xa, u0))

        with nc.Block() as block:
            @block.tensor
            def _(pe):
                def wait_dve(g, j, name):
                    pe.wait_ge(on_dve[g], ON_DVE.count(j, name))

                def wait_act(g, j, name):
                    pe.wait_ge(on_act[g], ON_ACT.count(j, name))

                for j in range(NT):
                    for g, (ex, m, mT, s1, ends, x, dw, wc, xT, gm, akv, xa, u0) in enumerate(lanes):
                        bank = [k.bank(4 * g + b) for b in range(4)]
                        if j:
                            wait_dve(g, j - 1, "fresh")
                        sg = sig[:, g, j, :]
                        for n, name in enumerate(("cum_excl", "cum_incl", "cum_rest")):
                            nc.tensor.matmul(bank[n], C(name)[:, g, :], sg, start=True, stop=True).then_inc(on_pe[g], 1)
                        for q in range(NPAIR):
                            last = nc.tensor.matmul(bank[3][:, 2 * q:2 * q + 2], sg[:, q * P:q * P + P], C("cum_chunk"),
                                                    start=True, stop=True)
                        last.then_inc(on_pe[g], 1)
                    for g, (ex, m, mT, s1, ends, x, dw, wc, xT, gm, akv, xa, u0) in enumerate(lanes):
                        wait_act(g, j, "chunk")
                        wait_dve(g, j, "scaled")
                        for q in range(NPAIR):
                            for n in range(4):
                                last = nc.tensor.transpose(k.bank(4 * g + q)[:, n * P:n * P + P],
                                                           m[:, n, q * P:q * P + P], C("ident"))
                            last.then_inc(on_pe[g], 1)
                    for g, (ex, m, mT, s1, ends, x, dw, wc, xT, gm, akv, xa, u0) in enumerate(lanes):
                        wait_act(g, j, "turn3")
                        for b in range(4):
                            e, qh = divmod(b, 2)
                            ks = slice(e * HA, e * HA + HA)
                            for i2 in range(2):
                                for cs in chunks:
                                    for w in range(2):
                                        at = (2 * i2 + w) * 2 * CH
                                        last = nc.tensor.matmul(k.bank(4 * g + b)[cs, at:at + 2 * CH],
                                                                mT[ks, 2 * qh + i2, (B, K)[w], cs],
                                                                mT[ks, 2 * qh + i2, A:R + 1, cs], start=True, stop=True)
                            last.then_inc(on_pe[g], 1)
                    for g, (ex, m, mT, s1, ends, x, dw, wc, xT, gm, akv, xa, u0) in enumerate(lanes):
                        wait_dve(g, j, "score1")
                        for n, h in enumerate(heads):
                            e, q = divmod(n, NPAIR)
                            ks = slice(e * HA, e * HA + HA)
                            for cs in chunks:
                                last = nc.tensor.matmul(k.bank(4 * g + e)[cs, q * CH:q * CH + CH], mT[ks, q, A, cs],
                                                        mT[ks, q, B, cs], start=True, stop=True)
                        last.then_inc(on_pe[g], 1)
                        wait_dve(g, j, "score3")
                        for n, h in enumerate(heads):
                            for cs in chunks:
                                last = nc.tensor.matmul(k.bank(4 * g + 3)[cs, cols[h]], s1[cs, n, 2, :], v[cs, j, cols[h]],
                                                        start=True, stop=True)
                        last.then_inc(on_pe[g], 1)
                    for n in LEVELS:
                        for g, (ex, m, mT, s1, ends, x, dw, wc, xT, gm, akv, xa, u0) in enumerate(lanes):
                            wait_dve(g, j, f"x{n - 1}")
                            for h in range(NHA):
                                for cs in chunks:
                                    last = nc.tensor.matmul(k.bank(4 * g)[cs, cols[h]], s1[cs, h, 0, :], x[cs, h, :],
                                                            start=True, stop=True)
                            last.then_inc(on_pe[g], 1)
                        for g, (ex, m, mT, s1, ends, x, dw, wc, xT, gm, akv, xa, u0) in enumerate(lanes):
                            wait_dve(g, j, f"g{n}")
                            for h in range(NHA):
                                for cs in chunks:
                                    if n < LEVELS[-1]:
                                        nc.tensor.matmul(k.bank(4 * g + 1)[cs, cols[h]], xT[cs, h, :], gm[cs, h, :],
                                                         start=True, stop=True)
                                    last = nc.tensor.matmul(k.bank(4 * g + 2)[cs, cols[h]], gm[cs, h, :], xT[cs, h, :],
                                                            start=True, stop=True)
                            last.then_inc(on_pe[g], 1)
                    for g, (ex, m, mT, s1, ends, x, dw, wc, xT, gm, akv, xa, u0) in enumerate(lanes):
                        wait_dve(g, j, f"x{LEVELS[-1]}")
                        for b, src in ((0, m[:, A, :]), (1, akv)):
                            if b:
                                wait_dve(g, j, "akv")
                            for n, h in enumerate(heads):
                                for cs in chunks:
                                    last = nc.tensor.matmul(k.bank(4 * g + b)[cs, cols[h]], xT[cs, n, :], src[cs, cols[h]],
                                                            start=True, stop=True)
                            last.then_inc(on_pe[g], 1)
                    for g, (ex, m, mT, s1, ends, x, dw, wc, xT, gm, akv, xa, u0) in enumerate(lanes):
                        wait_dve(g, j, "xa")
                        for ch, cs in enumerate(chunks):
                            for n, h in enumerate(heads):
                                e, q = divmod(n, NPAIR)
                                ks = slice(e * HA, e * HA + HA)
                                out = k.bank(4 * g + 2 + ch)
                                nc.tensor.matmul(out[ks, q * CH:q * CH + CH], xa[cs, cols[h]], s1[cs, n, 1, :],
                                                 start=True, stop=True)
                                last = nc.tensor.matmul(out[ks, (NPAIR + q) * HA:(NPAIR + q + 1) * HA], xa[cs, cols[h]],
                                                        ends[cs, 0, cols[h]], start=True, stop=True)
                        last.then_inc(on_pe[g], 1)
                    for g, (ex, m, mT, s1, ends, x, dw, wc, xT, gm, akv, xa, u0) in enumerate(lanes):
                        wait_dve(g, j, "u0")
                        for n, h in enumerate(heads):
                            for cs in chunks:
                                out = k.bank(4 * g)[cs, cols[h]]
                                nc.tensor.matmul(out, s1[cs, n, 1, :], u0[cs, cols[h]], start=True, stop=False)
                                last = nc.tensor.matmul(out, s1[cs, n, 3, :], v[cs, j, cols[h]], start=False, stop=True)
                        last.then_inc(on_pe[g], 1)
                        wait_dve(g, j, "qm")
                        for ch, cs in enumerate(chunks):
                            for n, h in enumerate(heads):
                                e, q = divmod(n, NPAIR)
                                ks = slice(e * HA, e * HA + HA)
                                out = k.bank(4 * g + 1 + ch)[ks, q * HA:q * HA + HA]
                                nc.tensor.matmul(out, ends[cs, 0, cols[h]], u0[cs, cols[h]], start=True, stop=False)
                                last = nc.tensor.matmul(out, ends[cs, 1, cols[h]], v[cs, j, cols[h]], start=False, stop=True)
                        last.then_inc(on_pe[g], 1)

            @block.scalar
            def _(act):
                o = Ops(nc, act, False)
                for j in range(NT):
                    for g, (ex, m, mT, s1, ends, x, dw, wc, xT, gm, akv, xa, u0) in enumerate(lanes):
                        if j:
                            act.wait_ge(on_pe[g], ON_PE.count(j - 1, "fresh"))
                        for n, (b, name, scale) in enumerate(((0, "excl", 1.0), (1, "incl", 1.0), (1, "incl", -1.0),
                                                              (2, "rest", 1.0))):
                            act.wait_ge(on_pe[g], ON_PE.count(j, name))
                            o.fn(ex[:, n], k.bank(4 * g + b), ACT.Exp, scale=scale, free=True).then_inc(on_act[g], 1)
                        act.wait_ge(on_pe[g], ON_PE.count(j, "chunk"))
                        o.fn(wc[:, :, :].rearrange("p c q -> p q c"), k.bank(4 * g + 3, NPAIR, 2), ACT.Exp,
                             free=True).then_inc(on_act[g], 1)
                    for g, (ex, m, mT, s1, ends, x, dw, wc, xT, gm, akv, xa, u0) in enumerate(lanes):
                        for q in range(NPAIR):
                            act.wait_ge(on_pe[g], ON_PE.count(j, f"turn{q}"))
                            o.copy(mT[:, q], k.bank(4 * g + q, 4, P), free=True).then_inc(on_act[g], 1)

            @block.vector
            def _(dve):
                o = Ops(nc, dve, True)

                def wait_pe(g, j, name):
                    dve.wait_ge(on_pe[g], ON_PE.count(j, name))

                def wait_act(g, j, name):
                    dve.wait_ge(on_act[g], ON_ACT.count(j, name))

                for j in range(NT):
                    for g, (ex, m, mT, s1, ends, x, dw, wc, xT, gm, akv, xa, u0) in enumerate(lanes):
                        wait_act(g, j, "excl")
                        o.stt(m[:, A], kk[:, j, :], -1.0, ex[:, 0], ALU.mult, ALU.mult, free=True)
                        wait_act(g, j, "incl")
                        o.mul(m[:, R], r[:, j, :], ex[:, 1], free=True)
                        wait_act(g, j, "inverse")
                        o.mul(m[:, B], beta[:, g, j, :], ex[:, 2], free=True)
                        o.mul(m[:, K], kd[:, g, j, :], ex[:, 2], free=True)
                        dve.drain()
                        dve.sem_inc(on_dve[g], 1)
                        wait_act(g, j, "chunk")
                        o.mul(ends[:, 0], beta[:, g, j, :], ex[:, 3], free=True)
                        o.mul(ends[:, 1], kd[:, g, j, :], ex[:, 3], free=True)
                        for ch in range(2):
                            last = o.mul(dw[:, ch], over(C("ident2"), NPAIR), spread(wc[:, ch, :], HA), free=True)
                        last.then_inc(on_dve[g], 1)
                    for g, (ex, m, mT, s1, ends, x, dw, wc, xT, gm, akv, xa, u0) in enumerate(lanes):
                        for b in range(4):
                            wait_pe(g, j, f"score{b}")
                            for i2 in range(2):
                                last = o.mul(s1[:, 2 * b + i2], k.bank(4 * g + b, 2, 4, CH)[:, i2], C("tri")[:, g], free=True)
                            last.then_inc(on_dve[g], 1)
                    for g, (ex, m, mT, s1, ends, x, dw, wc, xT, gm, akv, xa, u0) in enumerate(lanes):
                        wait_pe(g, j, "natural")
                        for e in range(2):
                            o.mul(x[:, 4 * e:4 * e + 4], k.bank(4 * g + e, 4, CH), over(C("merge")[:, g, 0, :], 4), free=e > 0)
                        o.mul(xT, s1[:, :, 0, :], over(C("merge")[:, 1 - g, 0, :], NHA), free=True)
                        o.add(x[:, :, :], x[:, :, :], over(C("ident2"), NHA))
                        o.add(xT, xT, over(C("ident2"), NHA))
                        dve.drain()
                        dve.sem_inc(on_dve[g], 1)
                        wait_pe(g, j, "akv")
                        o.copy(akv, k.bank(4 * g + 3), free=True).then_inc(on_dve[g], 1)
                    for n in LEVELS:
                        for g, (ex, m, mT, s1, ends, x, dw, wc, xT, gm, akv, xa, u0) in enumerate(lanes):
                            wait_pe(g, j, f"g{n}")
                            o.mul(gm, k.bank(4 * g, NHA, CH), over(C("merge")[:, g, n, :], NHA), free=True).then_inc(on_dve[g], 1)
                        for g, (ex, m, mT, s1, ends, x, dw, wc, xT, gm, akv, xa, u0) in enumerate(lanes):
                            wait_pe(g, j, f"c{n}")
                            if n < LEVELS[-1]:
                                o.add(x[:, :, :], x[:, :, :], k.bank(4 * g + 1, NHA, CH), free=True)
                            o.add(xT, xT, k.bank(4 * g + 2, NHA, CH))
                            dve.drain()
                            dve.sem_inc(on_dve[g], 1)
                    for g, (ex, m, mT, s1, ends, x, dw, wc, xT, gm, akv, xa, u0) in enumerate(lanes):
                        wait_pe(g, j, "xa")
                        o.copy(xa, k.bank(4 * g), free=True).then_inc(on_dve[g], 1)
                        wait_pe(g, j, "u0")
                        o.copy(u0, k.bank(4 * g + 1), free=True).then_inc(on_dve[g], 1)
                    for g, (ex, m, mT, s1, ends, x, dw, wc, xT, gm, akv, xa, u0) in enumerate(lanes):
                        wait_pe(g, j, "qm")
                        for ch, cs in enumerate(chunks):
                            both = k.bank(4 * g + 2 + ch, 2, NPAIR, CH)
                            o.add(qT[:, g, j, ch], both[:, 0], mT[:, :, R, cs], free=True)
                            last = o.add(move[:, g, j, ch], both[:, 1], dw[:, ch], free=True)
                        last.then_inc(on_dve[g], 1)
                    for g, (ex, m, mT, s1, ends, x, dw, wc, xT, gm, akv, xa, u0) in enumerate(lanes):
                        wait_pe(g, j, "y")
                        if g == 0:
                            o.copy(y[:, j, :], k.bank(4 * g), free=True).then_inc(on_dve[g], 1)
                        else:
                            o.add(y[:, j, :], y[:, j, :], k.bank(4 * g)).then_inc(on_dve[g], 1)
                        wait_pe(g, j, "fresh")
                        for ch in range(2):
                            last = o.copy(fresh[:, g, j, ch], k.bank(4 * g + 1 + ch)[:, 0:NPAIR * HA].rearrange(
                                "p (q n) -> p q n", n=HA), free=True)
                        last.then_inc(on_dve[g], 1)
        k.clear()


def rwkv_states(k, qT, move, fresh, y):
    nc = k.nc
    order = [[0, 1, 2, 3], [3, 2, 1, 0]]
    done, stored = k.sem["done"], k.sem["stored"]
    with ExitStack() as c:
        st = k.sb("states", [P, 3, 2, NPAIR, HA], ctx=c)
        with nc.Block() as block:
            @block.tensor
            def _(pe):
                for s in range(1, 3):
                    pe.wait_ge(stored, s)
                    for g in range(2):
                        jj, cc = divmod(order[g][s], 2)
                        for h in range(NHA):
                            q, ks = h // 2, slice(h % 2 * HA, h % 2 * HA + HA)
                            last = nc.tensor.matmul(k.bank(s - 1, 2, NPAIR, HA)[ks, g, q, :], move[ks, g, jj, cc, q, :],
                                                    st[ks, s - 1, g, q, :], start=True, stop=True)
                    last.then_inc(done, 1)
                pe.wait_ge(stored, 3)
                for ch in range(4):
                    jj, cc = divmod(ch, 2)
                    gs = [g for g in range(2) if order[g].index(ch)]
                    for h in range(NHA):
                        q, ks = h // 2, slice(h % 2 * HA, h % 2 * HA + HA)
                        for g in gs:
                            last = nc.tensor.matmul(k.bank(2 + 2 * jj + h % 2)[cc * CH:cc * CH + CH, q * HA:q * HA + HA],
                                                    qT[ks, g, jj, cc, q, :],
                                                    st[ks, order[g].index(ch) - 1, g, q, :],
                                                    start=g == gs[0], stop=g == gs[-1])
                last.then_inc(done, 1)

            @block.vector
            def _(dve):
                o = Ops(nc, dve, True)
                for g in range(2):
                    jj, cc = divmod(order[g][0], 2)
                    last = o.copy(st[:, 0, g], fresh[:, g, jj, cc], free=True)
                dve.drain()
                dve.sem_inc(stored, 1)
                for s in range(1, 3):
                    dve.wait_ge(done, s)
                    for g in range(2):
                        jj, cc = divmod(order[g][s], 2)
                        o.add(st[:, s, g], k.bank(s - 1, 2, NPAIR, HA)[:, g], fresh[:, g, jj, cc], free=True)
                    dve.drain()
                    dve.sem_inc(stored, 1)
                dve.wait_ge(done, 3)
                for j in range(NT):
                    for par in range(2):
                        yh = y[:, j, :].rearrange("p (q e n) -> p q e n", e=2, n=HA)[:, :, par, :]
                        o.add(yh, yh, k.bank(2 + 2 * j + par, NPAIR, HA), free=True)
        k.clear()


def head_norm(k, x, heads, width, gain, scale, c):
    nc = k.nc
    gr = k.sb("head_gain", [P, width], ctx=c)
    ss = k.sb("head_squares", [P, NT, heads], ctx=c)
    sq = k.sb("head_scratch", [P, heads * width], ctx=c)
    with nc.Block() as block:
        @block.sync
        def _(sp):
            sp.dma_start(gr[:, :], rows(gain)).then_inc(k.sem["loaded"], 16)

        @block.scalar
        def _(act):
            act.wait_ge(k.sem["reduced"], 1)
            nc.scalar.activation(ss[:, :, :], ss[:, :, :], ACT.Sqrt).then_inc(k.sem["rooted"], 1)

        @block.vector
        def _(dve):
            o = Ops(nc, dve, True)
            for j in range(NT):
                h3 = x[:, j, :].rearrange("p (h n) -> p h n", h=heads)
                s3 = sq[:, :].rearrange("p (h n) -> p h n", h=heads)
                o.mul(s3, h3, h3)
                o.sum(ss[:, j, :], s3)
            o.ts(ss[:, :, :], ss[:, :, :], 1.0 / width, ALU.mult, EPS, ALU.add).then_inc(k.sem["reduced"], 1)
            dve.wait_ge(k.sem["rooted"], 1)
            o.recip(ss[:, :, :], ss[:, :, :])
            dve.wait_ge(k.sem["loaded"], 16)
            for j in range(NT):
                h3 = x[:, j, :].rearrange("p (h n) -> p h n", h=heads)
                o.mul(h3, h3, spread(ss[:, j, :], width))
                o.mul(h3, h3, over(gr[:, :], heads))
                if scale is not None:
                    o.ts(x[:, j, :], x[:, j, :], scale, ALU.mult)
    k.clear()


def diff_attention(k, proj, q_gain, k_gain, lam_vecs, sub_g, lam_init, keep, out):
    nc = k.nc
    C = k.const
    with ExitStack() as c:
        qk = k.sb("qk", [P, 2, NT, DA], ctx=c)
        lv = k.sb("lambda_vectors", [P, 4, 64], ctx=c)
        l2 = k.sb("lambda_sums", [P, 2], ctx=c)
        lam = k.sb("minus_lambda", [P, 1], ctx=c)
        junk = k.sb("lambda_products", [P, 2, 64], ctx=c)
        qkT = k.sb("qkT", [P, 2, 4, SEQ], ctx=c)
        dist = k.sb("minus_distance", [P, NT, SEQ], ctx=c)
        load_stage(k, [(lv[:, :, :].rearrange("p a n -> p (a n)"), rows(lam_vecs)),
                       (dist[:, :, :], nc.inline_tensor(distance_tables()[0], name="distance_table").ap())])
        with nc.Block() as block:
            @block.vector
            def _(dve):
                o = Ops(nc, dve, True)
                for j in range(NT):
                    for w in range(2):
                        o.copy(qk[:, w, j, :], proj[:, j, C_RWKV + w * DA:C_RWKV + (w + 1) * DA], free=True)
                for n in range(2):
                    o.mul(junk[:, n], lv[:, 2 * n], lv[:, 2 * n + 1])
                    o.sum(l2[:, n:n + 1], junk[:, n])
                o.copy(l2[:, :], l2[:, :]).then_inc(k.sem["reduced"], 1)
                dve.wait_ge(k.sem["exped"], 1)
                o.sub(lam[:, :], l2[:, 1:2], l2[:, 0:1])
                o.sub(lam[:, :], lam[:, :], lam_init)

            @block.scalar
            def _(act):
                act.wait_ge(k.sem["reduced"], 1)
                nc.scalar.activation(l2[:, :], l2[:, :], ACT.Exp).then_inc(k.sem["exped"], 1)
        k.clear()
        with ExitStack() as c1:
            head_norm(k, qk[:, 0], 8, 64, q_gain, None, c1)
        with ExitStack() as c1:
            head_norm(k, qk[:, 1], 8, 64, k_gain, None, c1)
        turn_tokens(k, qk[:, 0], qkT[:, 0], 4)
        turn_tokens(k, qk[:, 1], qkT[:, 1], 4)
        units = [(h, j) for h in range(NHB) for j in range(NT)]
        N = len(units)
        lg = k.sb("logits", [P, 3, 2, SEQ], ctx=c)
        mx = k.sb("row_max", [P, 3, 2], ctx=c)
        sm = k.sb("row_sum", [P, 3, 2], ctx=c)
        bias = k.sb("alibi", [P, 2, SEQ], ctx=c)
        pT = k.sb("probsT", [P, 2, 2, P], ctx=c)
        S = k.sem
        with nc.Block() as block:
            @block.tensor
            def _(pe):
                def logits(n):
                    h, j = units[n]
                    if n >= 2:
                        pe.wait_ge(S["masked"], n - 1)
                    for mm in range(2):
                        ks = slice(mm * 64, mm * 64 + 64)
                        last = nc.tensor.matmul(k.bank(2 * (n % 2) + mm)[:, 0:SEQ],
                                                qkT[ks, 0, h, j * P:j * P + P], qkT[ks, 1, h, :], start=True, stop=True)
                    last.then_inc(S["summed"], 1)

                def turn(n):
                    pe.wait_ge(S["got"], n + 1)
                    if n >= 2:
                        pe.wait_ge(S["copied_s"], n - 1)
                    for kc in range(2):
                        last = nc.tensor.transpose(k.bank(4 + n % 2)[:, kc * P:kc * P + P],
                                                   lg[:, n % 3, 0, kc * P:kc * P + P], C("ident"))
                    last.then_inc(S["turned"], 1)

                def values(n):
                    h, j = units[n]
                    pe.wait_ge(S["copied_s"], n + 1)
                    if n >= 2:
                        pe.wait_ge(S["stored"], n - 1)
                    for kc in range(2):
                        last = nc.tensor.matmul(k.bank(6 + n % 2)[:, 0:P], pT[:, n % 2, kc, :],
                                                proj[:, kc, C_RWKV + 2 * DA + h * P:C_RWKV + 2 * DA + h * P + P],
                                                start=kc == 0, stop=kc == 1)
                    last.then_inc(S["done"], 1)

                logits(0)
                logits(1)
                for n in range(N + 1):
                    if n < N:
                        turn(n)
                    if n + 2 < N:
                        logits(n + 2)
                    if n >= 1:
                        values(n - 1)

            @block.scalar
            def _(act):
                o = Ops(nc, act, False)

                def exps(n):
                    act.wait_ge(S["masked"], n + 1)
                    for mm in range(2):
                        o.fn(lg[:, n % 3, mm], lg[:, n % 3, mm], ACT.Exp, bias=mx[:, n % 3, mm:mm + 1],
                             total=sm[:, n % 3, mm:mm + 1], free=True).then_inc(S["exped"], 1)

                exps(0)
                for n in range(N):
                    if n + 1 < N:
                        exps(n + 1)
                    act.wait_ge(S["turned"], n + 1)
                    if n >= 2:
                        act.wait_ge(S["done"], n - 1)
                    o.copy(pT[:, n % 2], k.bank(4 + n % 2, 2, P), free=True).then_inc(S["copied_s"], 1)

            @block.vector
            def _(dve):
                o = Ops(nc, dve, True)

                def masks(n):
                    h, j = units[n]
                    o.ts(bias[:, n % 2], dist[:, j, :], 2.0 ** (-8.0 * (h + 1) / NHB), ALU.mult)
                    if n >= 3:
                        dve.wait_ge(S["turned"], n - 2)
                    dve.wait_ge(S["summed"], n + 1)
                    for mm in range(2):
                        o.stt(lg[:, n % 3, mm], k.bank(2 * (n % 2) + mm)[:, 0:SEQ], 64.0 ** -0.5, bias[:, n % 2],
                              ALU.mult, ALU.add, free=mm > 0)
                    o.max(mx[:, n % 3], lg[:, n % 3])
                    o.ts(mx[:, n % 3], mx[:, n % 3], -1.0, ALU.mult).then_inc(S["masked"], 1)

                def difference(n):
                    dve.wait_ge(S["exped"], 2 * n + 2)
                    o.recip(sm[:, n % 3], sm[:, n % 3], free=True)
                    o.ts(sm[:, n % 3, 1:2], sm[:, n % 3, 1:2], lam[:, 0:1], ALU.mult)
                    o.ts(lg[:, n % 3, 0], lg[:, n % 3, 0], sm[:, n % 3, 0:1], ALU.mult)
                    o.stt(lg[:, n % 3, 0], lg[:, n % 3, 1], sm[:, n % 3, 1:2], lg[:, n % 3, 0],
                          ALU.mult, ALU.add).then_inc(S["got"], 1)

                def store(n):
                    h, j = units[n]
                    dve.wait_ge(S["done"], n + 1)
                    o.copy(out[:, j, h * P:h * P + P], k.bank(6 + n % 2)[:, 0:P], free=True).then_inc(S["stored"], 1)

                masks(0)
                for n in range(N + 2):
                    if n + 1 < N:
                        masks(n + 1)
                    if n < N:
                        difference(n)
                    if n >= 2:
                        store(n - 2)
        k.clear()
        with ExitStack() as c1:
            head_norm(k, out, NHB, P, sub_g, keep, c1)


def first_layer(k, l, a, lam_tab):
    row = lambda name: a[name][bass.ds(l, 1), :]
    mat = lambda name: a[name][l]
    w_proj = row_weights(mat("w_in"), C_IN // WPROJ, WPROJ)
    w_br = [sum_weights(a["w_branch"][l, br], 4) for br in range(2)]
    w_mix = sum_weights(mat("w_out"), KC)
    w_up = pair_weights(mat("ffn2_in"), D_FF)
    swiglu(k, row("norm_ffn1"), pair_weights(mat("ffn1_in"), D_FF), sum_weights(mat("ffn1_out"), NF), w_proj)
    with ExitStack() as c:
        proj = k.sb("projected", [P, NT, C_IN], ctx=c)
        oa = k.sb("branch_a", [P, NT, DA], ctx=c)
        project(k, row("norm_mix"), w_proj, WPROJ, proj)
        flat = lambda name: a[name].rearrange("l h n -> l (h n)")[bass.ds(l, 1), :]
        rwkv(k, proj, row("rwkv_mu"),
             [a["decay_w0"][bass.ds(l, 1), g, :] for g in range(2)], a["decay_w2"].rearrange("l g r c -> l (g r) c")[l],
             [a["iclr_a0"][bass.ds(l, 1), g, :] for g in range(2)], a["iclr_a2"].rearrange("l g r c -> l (g r) c")[l],
             mat("gate_g2"), row("k_k"), row("k_a"), flat("r_k"), row("ln_x_g"), row("ln_x_b"), oa)
        ob = k.sb("branch_b", [P, NT, DA], ctx=c)
        lamc = k.sb("lambda_constants", [P, 2], ctx=c)
        gates = proj[:, :, C_RWKV + C_ATTN:]
        with k.nc.Block() as block:
            @block.sync
            def _(sp):
                preload(k, sp, w_br[0])

            @block.vector
            def _(dve):
                k.nc.vector.tensor_copy(lamc[:, :], lam_tab[:, bass.ds(l, 1), :].rearrange("p a b -> p (a b)"))

            @block.scalar
            def _(act):
                for j in range(NT):
                    k.nc.scalar.activation(gates[:, j, :], gates[:, j, :], ACT.Sigmoid)
        k.clear()
        diff_attention(k, proj, row("q_gain"), row("k_gain"), flat("diff_lambda"), row("subln_g"),
                       lamc[:, 0:1], lamc[:, 1:2], ob)
        oT = split_sb(k, "branchT", [P, 4, SEQ], c)
        for br, src in enumerate((oa, ob)):
            turn_tokens(k, src, oT, 4)

            def gated(o, j, half, bank, br=br):
                g0 = gates[:, j, half * BANK:(half + 1) * BANK]
                g1 = gates[:, j, br * D + half * BANK:br * D + (half + 1) * BANK]
                o.mul(g1, g1, bank)
                if br:
                    return o.add(g0, g0, g1)

            linear_sum_stage(k, oT, 4, w_br[br], gated, (w_br + [w_mix])[br + 1])
        mT = split_sb(k, "mergedT", [P, KC, SEQ], c)
        turn_tokens(k, gates[:, :, 0:D], mT, KC)

        def residual(o, j, half, bank):
            x = k.X[:, j, half * BANK:(half + 1) * BANK]
            return o.add(x, x, bank, free=True)

        linear_sum_stage(k, mT, KC, w_mix, residual, w_up)
    swiglu(k, row("norm_ffn2"), w_up, sum_weights(mat("ffn2_out"), NF), None)



class Modulation:

    TILES = 6 * D // BANK

    def __init__(self, k, cols, w, b, out, bias, out_ctx=None):
        self.k, self.cols, self.b, self.out, self.bias, self.out_ctx = k, cols, b, out, bias, out_ctx
        self.w = w.rearrange("(k p) n -> p k n", p=P)

    def load(self, sp, ahead=None):
        k, S = self.k, self.k.sem
        for t in range(self.TILES):
            if t >= 2:
                sp.wait_ge(S["prod"], t - 1)
            sp.dma_start(k.raw[:, t % 2, :].rearrange("p (k n) -> p k n", k=KC),
                         self.w[:, :, t * BANK:(t + 1) * BANK]).then_inc(S[f"slot_in{t % 2}"], 16)
            if t == 1:
                sp.dma_start(self.bias[:, :], rows(self.b)).then_inc(S["corr"], 16)
        if ahead is not None:
            sp.wait_ge(S["prod"], self.TILES)
            preload(k, sp, ahead)

    def products(self, pe, banks_free=None):
        k, S = self.k, self.k.sem
        for t in range(self.TILES):
            pe.wait_ge(S[f"slot_in{t % 2}"], 16 * (t // 2 + 1))
            if t >= 2:
                pe.wait_ge(S["drained"], t - 1)
            elif banks_free is not None:
                pe.wait_ge(banks_free, t + 1)
            for kc_ in range(KC):
                last = k.nc.tensor.matmul(k.bank(t % 2), self.cols[:, kc_, :], k.raw[:, t % 2, kc_ * BANK:(kc_ + 1) * BANK],
                                          start=kc_ == 0, stop=kc_ == KC - 1)
            last.then_inc(S["prod"], 1)

    def copies(self, act):
        k, S = self.k, self.k.sem
        for t in range(self.TILES):
            act.wait_ge(S["prod"], t + 1)
            cs = slice(t * BANK, (t + 1) * BANK)
            if self.out_ctx is not None and t < 4:
                for half in (0, 64):
                    k.nc.scalar.copy(self.out_ctx[half:half + 64, cs], k.bank(t % 2)[64:128])
            k.nc.scalar.copy(self.out[0:64, cs], k.bank(t % 2)[0:64])
            act.drain()
            k.nc.scalar.copy(self.out[64:128, cs], k.bank(t % 2)[0:64]).then_inc(S["drained"], 1)

    def add_bias(self, pool):
        k, S = self.k, self.k.sem
        pool.wait_ge(S["corr"], 16)
        for t in range(self.TILES):
            pool.wait_ge(S["drained"], t + 1)
            cs = slice(t * BANK, (t + 1) * BANK)
            k.nc.gpsimd.tensor_tensor(self.out[:, cs], self.out[:, cs], self.bias[:, cs], ALU.add)
            if self.out_ctx is not None and t < 4:
                k.nc.gpsimd.tensor_tensor(self.out_ctx[:, cs], self.out_ctx[:, cs], self.bias[:, cs], ALU.add)


def first_modulation(k, a, cols, mod, cm, cx, ahead):
    nc = k.nc
    S = k.sem
    with ExitStack() as c:
        cr = k.sb("cond", [P, P], ctx=c)
        bias = k.sb("mod_bias", [P, 6 * D], ctx=c)
        m = Modulation(k, cols, a["mod_w_2"][0], a["mod_b_2"][0:1, :], mod, bias, cm)
        conds = [x.rearrange("(k p) -> k p", p=P) for x in (a["c_2"][0], a["c_ctx_2"])]
        with nc.Block() as block:
            @block.sync
            def _(sp):
                sp.wait_ge(S["reduced"], 1)
                for n, cond in enumerate(conds):
                    sp.dma_start(cr[n * KC:(n + 1) * KC, :], cond).then_inc(S["loaded"], 16)
                m.load(sp, ahead)
                sp.dma_start(cx[:, :, :], a["ctx_2"][0].rearrange("(j p) d -> p j d", p=P)).then_inc(S["written"], 16)
                sp.wait_ge(S["written"], 16)

            @block.vector
            def _(dve):
                nc.vector.memset(cr[:, :], 0.0).then_inc(S["reduced"], 1)
                dve.wait_ge(S["turned"], 1)
                for n in range(2):
                    last = nc.vector.tensor_copy(cols[:, :, n * 64:(n + 1) * 64], spread(k.bank(7)[:, n * KC:(n + 1) * KC], 64))
                last.then_inc(S["stored"], 1)

            @block.scalar
            def _(act):
                act.wait_ge(S["loaded"], 16 * len(conds))
                nc.scalar.activation(cr[:, :], cr[:, :], ACT.Silu).then_inc(S["squashed"], 1)
                m.copies(act)

            @block.tensor
            def _(pe):
                pe.wait_ge(S["squashed"], 1)
                nc.tensor.transpose(k.bank(7)[:, 0:P], cr[:, :], k.const("ident")).then_inc(S["turned"], 1)
                pe.wait_ge(S["stored"], 1)
                m.products(pe)

            @block.gpsimd
            def _(pool):
                m.add_bias(pool)
        k.clear()


def rope(k, x, heads, scratch, trig):
    nc = k.nc
    with nc.Block() as block:
        @block.vector
        def _(dve):
            o = Ops(nc, dve, True)
            for j in range(NT):
                for ax in range(2):
                    x4 = x[:, j, :].rearrange("p (h a b n) -> p h a b n", h=heads, a=2, b=2)
                    x1, x2 = x4[:, :, ax, 0, :], x4[:, :, ax, 1, :]
                    cs, sn = over(trig[:, 0, j, ax, :], heads), over(trig[:, 1, j, ax, :], heads)
                    s = scratch[:, 0:4, 0:heads * 16].rearrange("p a (h n) -> p a h n", n=16)
                    o.mul(s[:, 0], x1, cs)
                    o.mul(s[:, 1], x2, sn, free=True)
                    o.mul(s[:, 2], x1, sn, free=True)
                    o.mul(s[:, 3], x2, cs, free=True)
                    o.sub(x1, s[:, 0], s[:, 1])
                    o.add(x2, s[:, 2], s[:, 3], free=True)
    k.clear()


def window_attention(k, pr, kvc, sink, out):
    nc = k.nc
    C = k.const
    S = k.sem
    with ExitStack() as c:
        scr = k.sb("rope_scratch", [P, 4, 128], ctx=c)
        sk = k.sb("sink", [P, 8], ctx=c)
        window = k.sb("window_mask", [P, NT, SEQ], ctx=c)
        trig = k.sb("cos_sin", [P, 2, NT, 2, 16], ctx=c)
        load_stage(k, [(sk[:, :], rows(sink)),
                       (window[:, :, :], nc.inline_tensor(distance_tables()[1], name="window_table").ap()),
                       (trig[:, :, :, :, :].rearrange("p a b c d -> p (a b c d)"),
                        nc.inline_tensor(rope_table().reshape(P, -1), name="rope_table").ap())])
        rope(k, pr[:, :, 0:QW], 8, scr, trig)
        rope(k, pr[:, :, QW:QW + KVW], 2, scr, trig)
        qT = k.sb("qT", [64, 8, SEQ], ctx=c)
        kT = k.sb("kT", [64, 2, 2 * SEQ], ctx=c)
        jobs = [(pr[:, j, h * 64:h * 64 + 64], qT[:, h, j * P:j * P + P]) for h in range(8) for j in range(NT)]
        jobs += [(pr[:, j, QW + g * 64:QW + g * 64 + 64], kT[:, g, j * P:j * P + P]) for g in range(2) for j in range(NT)]
        jobs += [(kvc[:, j, g * 64:g * 64 + 64], kT[:, g, SEQ + j * P:SEQ + j * P + P]) for g in range(2) for j in range(NT)]
        with nc.Block() as block:
            @block.tensor
            def _(pe):
                for n, (src, _) in enumerate(jobs):
                    if n >= 8:
                        pe.wait_ge(S["copied_v"], n - 7)
                    nc.tensor.transpose(k.bank(n % 8)[0:64, 0:P], src, C("ident")).then_inc(S["turned"], 1)

            @block.vector
            def _(dve):
                for n, (_, dst) in enumerate(jobs):
                    dve.wait_ge(S["turned"], n + 1)
                    nc.vector.tensor_copy(dst, k.bank(n % 8)[0:64, 0:P]).then_inc(S["copied_v"], 1)
        k.clear()
        units = [(h, j) for h in range(8) for j in range(NT)]
        N = len(units)
        lg = k.sb("logits", [P, 3, 2 * SEQ], ctx=c)
        mx = k.sb("row_max", [P, 3], ctx=c)
        sm = k.sb("row_sum", [P, 4, 2], ctx=c)
        pT = k.sb("probsT", [P, 2, 4, P], ctx=c)
        with nc.Block() as block:
            @block.tensor
            def _(pe):
                def logits(n):
                    h, j = units[n]
                    if n >= 2:
                        pe.wait_ge(S["masked"], n - 1)
                    nc.tensor.matmul(k.bank(n % 2), qT[:, h, j * P:j * P + P], kT[:, h // 4, :],
                                     start=True, stop=True).then_inc(S["summed"], 1)

                def turn(n):
                    pe.wait_ge(S["exped"], 2 * n + 2)
                    if n >= 2:
                        pe.wait_ge(S["copied_s"], n - 1)
                    for kc in range(4):
                        last = nc.tensor.transpose(k.bank(2 + n % 2)[:, kc * P:kc * P + P],
                                                   lg[:, n % 3, kc * P:kc * P + P], C("ident"))
                    last.then_inc(S["turned"], 1)

                def values(n):
                    g = units[n][0] // 4
                    pe.wait_ge(S["copied_s"], n + 1)
                    if n >= 2:
                        pe.wait_ge(S["stored"], n - 1)
                    for kc in range(4):
                        src = (pr[:, kc, QW + KVW + g * 64:QW + KVW + g * 64 + 64] if kc < 2
                               else kvc[:, kc - 2, KVW + g * 64:KVW + g * 64 + 64])
                        last = nc.tensor.matmul(k.bank(4 + n % 2)[:, 0:64], pT[:, n % 2, kc, :], src,
                                                start=kc == 0, stop=kc == 3)
                    last.then_inc(S["done"], 1)

                logits(0)
                logits(1)
                for n in range(N + 1):
                    if n < N:
                        turn(n)
                    if n + 2 < N:
                        logits(n + 2)
                    if n >= 1:
                        values(n - 1)

            @block.scalar
            def _(act):
                o = Ops(nc, act, False)

                def exps(n):
                    h = units[n][0]
                    act.wait_ge(S["masked"], n + 1)
                    if n >= 4:
                        act.wait_ge(S["stored"], n - 3)
                    o.fn(lg[:, n % 3], lg[:, n % 3], ACT.Exp, bias=mx[:, n % 3:n % 3 + 1],
                         total=sm[:, n % 4, 0:1], free=True).then_inc(S["exped"], 1)
                    o.fn(sm[:, n % 4, 1:2], sk[:, h:h + 1], ACT.Exp, bias=mx[:, n % 3:n % 3 + 1],
                         free=True).then_inc(S["exped"], 1)

                exps(0)
                for n in range(N):
                    if n + 1 < N:
                        exps(n + 1)
                    act.wait_ge(S["turned"], n + 1)
                    if n >= 2:
                        act.wait_ge(S["done"], n - 1)
                    o.copy(pT[:, n % 2], k.bank(2 + n % 2, 4, P), free=True).then_inc(S["copied_s"], 1)

            @block.vector
            def _(dve):
                o = Ops(nc, dve, True)

                def masks(n):
                    h, j = units[n]
                    if n >= 3:
                        dve.wait_ge(S["turned"], n - 2)
                    dve.wait_ge(S["summed"], n + 1)
                    o.stt(lg[:, n % 3, 0:SEQ], k.bank(n % 2)[:, 0:SEQ], 0.125, window[:, j, :], ALU.mult, ALU.add, free=True)
                    o.ts(lg[:, n % 3, SEQ:], k.bank(n % 2)[:, SEQ:], 0.125, ALU.mult, free=True)
                    o.max(mx[:, n % 3:n % 3 + 1], lg[:, n % 3])
                    o.tt(mx[:, n % 3:n % 3 + 1], mx[:, n % 3:n % 3 + 1], sk[:, h:h + 1], ALU.max)
                    o.ts(mx[:, n % 3:n % 3 + 1], mx[:, n % 3:n % 3 + 1], -1.0, ALU.mult).then_inc(S["masked"], 1)

                def store(n):
                    h, j = units[n]
                    dve.wait_ge(S["exped"], 2 * n + 2)
                    o.add(sm[:, n % 4, 0:1], sm[:, n % 4, 0:1], sm[:, n % 4, 1:2], free=True)
                    o.recip(sm[:, n % 4, 0:1], sm[:, n % 4, 0:1])
                    dve.drain()
                    dve.wait_ge(S["done"], n + 1)
                    o.ts(out[:, j, h * 64:h * 64 + 64], k.bank(4 + n % 2)[:, 0:64], sm[:, n % 4, 0:1],
                         ALU.mult, free=True).then_inc(S["stored"], 1)

                masks(0)
                for n in range(N + 2):
                    if n + 1 < N:
                        masks(n + 1)
                    if n >= 2:
                        store(n - 2)
        k.clear()


def gmlp(k, pr, w_s, b_s, out):
    nc = k.nc
    C = k.const
    S = k.sem
    u = pr[:, :, QW + 2 * KVW:QW + 2 * KVW + AW]
    v = pr[:, :, QW + 2 * KVW + AW:]
    with ExitStack() as c:
        ws = k.sb("spatial", [P, GROUPS, P], ctx=c)
        wsT = k.sb("spatialT", [P, GROUPS, P], ctx=c)
        bs = k.sb("spatial_bias", [P, P], ctx=c)
        bT = k.sb("spatial_biasT", [P, 1, P], ctx=c)
        mean = k.sb("mean", [P, NT, GROUPS], ctx=c)
        var = k.sb("var", [P, NT, GROUPS], ctx=c)
        sq = k.sb("scratch", [P, AW], ctx=c)
        with nc.Block() as block:
            @block.sync
            def _(sp):
                sp.dma_start(ws[:, :, :], w_s.rearrange("g p q -> p g q")).then_inc(S["loaded"], 16)
                sp.wait_ge(S["reduced"], 1)
                sp.dma_start(bs[0:GROUPS, :], b_s).then_inc(S["loaded"], 16)
                sp.wait_ge(S["loaded"], 32)

            @block.scalar
            def _(act):
                for j in range(NT):
                    nc.scalar.activation(u[:, j, :], u[:, j, :], ACT.Gelu_apprx_tanh)
                    nc.scalar.activation(v[:, j, :], v[:, j, :], ACT.Gelu_apprx_tanh)

            @block.vector
            def _(dve):
                nc.vector.memset(bs[:, :], 0.0).then_inc(S["reduced"], 1)
        k.clear()
        turn_stage(k, [([ws[:, n + i, :] for i in range(4)], wsT[:, n:n + 4, :]) for n in (0, 4)] + [([bs[:, :]], bT[:, :, :])])
        with nc.Block() as block:
            @block.vector
            def _(dve):
                o = Ops(nc, dve, True)
                for j in range(NT):
                    h3 = v[:, j, :].rearrange("p (h n) -> p h n", h=GROUPS)
                    s3 = sq[:, :].rearrange("p (h n) -> p h n", h=GROUPS)
                    o.sum(mean[:, j, :], h3)
                    o.ts(mean[:, j, :], mean[:, j, :], 1.0 / 64, ALU.mult)
                    o.sub(h3, h3, spread(mean[:, j, :], 64))
                    o.mul(s3, h3, h3)
                    o.sum(var[:, j, :], s3)
                o.ts(var[:, :, :], var[:, :, :], 1.0 / 64, ALU.mult, EPS, ALU.add).then_inc(S["reduced"], 1)
                dve.wait_ge(S["rooted"], 1)
                o.recip(var[:, :, :], var[:, :, :])
                for j in range(NT):
                    h3 = v[:, j, :].rearrange("p (h n) -> p h n", h=GROUPS)
                    o.mul(h3, h3, spread(var[:, j, :], 64)).then_inc(S["stored"], 1)
                for j in range(NT):
                    dve.wait_ge(S["done"], j + 1)
                    for g in range(GROUPS):
                        cs = slice(g * 64, g * 64 + 64)
                        o.stt(out[:, j, cs], k.bank(j)[:, cs], bT[:, 0, g:g + 1], u[:, j, cs], ALU.add, ALU.mult, free=True)

            @block.scalar
            def _(act):
                act.wait_ge(S["reduced"], 1)
                nc.scalar.activation(var[:, :, :], var[:, :, :], ACT.Sqrt).then_inc(S["rooted"], 1)

            @block.tensor
            def _(pe):
                for j in range(NT):
                    pe.wait_ge(S["stored"], j + 1)
                    for g in range(GROUPS):
                        last = nc.tensor.matmul(k.bank(j)[:, g * 64:g * 64 + 64], wsT[:, g, :],
                                                v[:, j, g * 64:g * 64 + 64], start=True, stop=True)
                    last.then_inc(S["done"], 1)
        k.clear()


def gated_residual(k, gate, bank, o, j, half, tmp):
    cs = slice(half * BANK, (half + 1) * BANK)
    o.mul(tmp[:, :], bank, gate[:, cs])
    return o.add(k.X[:, j, cs], k.X[:, j, cs], tmp[:, :])


def attn_gmlp_layer(k, a, cols, mod, w_query):
    nc = k.nc
    with ExitStack() as c:
        kvc = k.sb("context_kv", [P, NT, 2 * KVW], ctx=c)
        tmp = k.sb("scratch", [P, BANK], ctx=c)
        w = a["attn_in_w_2"][0]
        with ExitStack() as c1:
            cm = k.sb("context_mod", [P, 4 * BANK], ctx=c1)
            w_ckv = row_weights(w[:, QW:QW + 2 * KVW], 1, 2 * KVW)
            w_pr = row_weights(w, 4, IN_W // 4)
            w_mix = sum_weights(a["attn_out_w_2"][0], KC)
            cx = k.sb("context", [P, NT, D], ctx=c1)
            first_modulation(k, a, cols, mod, cm, cx, w_ckv)
            cT = split_sb(k, "contextT", [P, KC, SEQ], c1)
            norm_stage(k, cx, a["norm1_g_2"][0:1, :], cx, cm[:, D:2 * D], cm[:, 0:D], turned_to=cT)
            linear_stage(k, lambda c_, j: cT[:, c_, j * P:j * P + P], w_ckv, 2 * KVW,
                         lambda o, t, j, bank: o.copy(kvc[:, j, :], bank, free=True), w_pr)
        pr = k.sb("projected", [P, NT, IN_W], ctx=c)
        project(k, a["norm1_g_2"][0:1, :], w_pr, IN_W // 4, pr, (mod[:, D:2 * D], mod[:, 0:D]), w_mix)
        mix = k.sb("mixed", [P, NT, D], ctx=c)
        window_attention(k, pr, kvc, a["attn_sink_2"][0:1, :], mix[:, :, 0:QW])
        gmlp(k, pr, a["gmlp_w_s_2"][0], a["gmlp_b_s_2"][0], mix[:, :, QW:])
        mT = split_sb(k, "mixedT", [P, KC, SEQ], c)
        turn_tokens(k, mix, mT, KC)
        linear_sum_stage(k, mT, KC, w_mix,
                         lambda o, j, half, bank: gated_residual(k, mod[:, 2 * D:3 * D], bank, o, j, half, tmp), w_query)


def pool_layer(k, a, mod, w_query):
    nc = k.nc
    S = k.sem
    C = k.const
    with ExitStack() as c:
        h = k.sb("normed", [P, NT, D], ctx=c)
        norm_stage(k, k.X, a["norm1_g_2"][1:2, :], h, mod[:, D:2 * D], mod[:, 0:D])
        pw = k.sb("pool_w", [P, 4, 2, SEQ], ctx=c)
        means = k.sb("window_means", [P, 4, NT, SEQ], ctx=c)
        ps = k.sb("pool_scale", [P, D], ctx=c)
        pT = k.sb("pooledT", [P, KC, SEQ], ctx=c)
        tmp = k.sb("scratch", [P, SEQ], ctx=c)
        load_stage(k, [(pw[:, :, :, :].rearrange("p g k e -> p (g k) e"),
                        a["pool_w_2"][0].rearrange("g (k p) e -> p (g k) e", p=P)),
                       (ps[:, :], rows(a["pool_scale_2"][0:1, :])),
                       (means[:, :, :, :], nc.inline_tensor(pool_table(), name="window_mean_table").ap())],
                   w_query)
        with nc.Block() as block:
            @block.tensor
            def _(pe):
                for cc in range(KC):
                    for s in range(NT):
                        last = nc.tensor.matmul(k.bank(cc)[:, 0:SEQ], h[:, s, cc * P:cc * P + P],
                                                means[:, cc // 2, s, :], start=s == 0, stop=s == NT - 1)
                    last.then_inc(S["summed"], 1)
                for g in range(4):
                    pe.wait_ge(S["stored"], 2 * g + 2)
                    for j in range(NT):
                        for cc in range(2):
                            last = nc.tensor.matmul(k.bank(2 * g + j)[:, 0:SEQ], pT[:, 2 * g + cc, j * P:j * P + P],
                                                    pw[:, g, cc, :], start=cc == 0, stop=cc == 1)
                        last.then_inc(S["done"], 1)

            @block.vector
            def _(dve):
                o = Ops(nc, dve, True)
                o.mul(ps[:, :], ps[:, :], mod[:, 2 * D:3 * D])
                for cc in range(KC):
                    dve.wait_ge(S["summed"], cc + 1)
                    o.copy(pT[:, cc, :], k.bank(cc)[:, 0:SEQ], free=True).then_inc(S["stored"], 1)
                for g in range(4):
                    cs = slice(g * SEQ, (g + 1) * SEQ)
                    for j in range(NT):
                        dve.wait_ge(S["done"], 2 * g + j + 1)
                        o.mul(tmp[:, :], k.bank(2 * g + j)[:, 0:SEQ], ps[:, cs])
                        o.add(k.X[:, j, cs], k.X[:, j, cs], tmp[:, :])
        k.clear()


def top16(o, nc, vals, work, idx, src):
    o._order(False)
    nc.vector.max(out=vals[:, 0:8], in_=src)
    o._order(False)
    nc.vector.max_index(out=idx[:, 0:8], in_max=vals[:, 0:8], in_values=src)
    nc.vector.match_replace(out=work, in_to_replace=vals[:, 0:8], in_values=src, imm_value=-3.0e38)
    o._order(False)
    nc.vector.max(out=vals[:, 8:16], in_=work)
    o._order(False)
    return nc.vector.max_index(out=idx[:, 8:16], in_max=vals[:, 8:16], in_values=work)


class Choice:

    def __init__(self, k, l, c):
        self.k, self.l = k, l
        self.s = k.sb("key_scores", [P, NT, 2 * PH, P], ctx=c)
        self.w = k.sb("work", [P, 2, SEQ], ctx=c)
        self.v1 = k.sb("key_best", [P, 2 * PH, TOPK], ctx=c)
        self.i1 = k.sb("key_index", [P, 2 * PH, TOPK], U32, ctx=c)
        self.f1 = k.sb("key_index_f", [P, 2 * PH, TOPK], ctx=c)
        self.cand = k.sb("pair_scores", [P, 2, TOPK, TOPK], ctx=c)
        self.best = k.sb("pair_best", [P, NT, PH, TOPK], ctx=c)
        self.pos = k.sb("pair_pos", [P, PH, TOPK], U32, ctx=c)
        self.hi = k.sb("pair_hi", [P, 2, TOPK], U32, ctx=c)
        self.hf = k.sb("pair_hi_f", [P, 2, TOPK], ctx=c)
        self.hot = k.sb("one_hot", [P, 2, TOPK, TOPK], ctx=c)
        self.pick = k.sb("picked", [P, 2, PH, TOPK], ctx=c)
        self.ids = k.sb("expert_ids", [P, NT, SLOTS], U32, ctx=c)

    def keys(self, o, j, n):
        top16(o, self.k.nc, self.v1[:, n], self.w[:, n % 2, 0:P], self.i1[:, n], self.s[:, j, n])
        o.copy(self.f1[:, n], self.i1[:, n])

    def pairs(self, o, j, e):
        cand = self.cand[:, e % 2]
        o.tt(cand, spread(self.v1[:, 2 * e], TOPK), over(self.v1[:, 2 * e + 1], TOPK), ALU.add)
        top16(o, self.k.nc, self.best[:, j, e], self.w[:, e % 2], self.pos[:, e], cand.rearrange("p a b -> p (a b)"))

    def places(self, o, j, e):
        o.ts(self.hi[:, 0], self.pos[:, e], 4, ALU.logical_shift_right)
        o.ts(self.hi[:, 1], self.pos[:, e], 15, ALU.bitwise_and, free=True)
        o.copy(self.hf[:, :, :], self.hi[:, :, :])
        for side in range(2):
            o.tt(self.hot[:, side], spread(self.hf[:, side], TOPK), over(self.k.const("iota16"), TOPK), ALU.is_equal,
                 free=side > 0)
        for side in range(2):
            o.mul(self.hot[:, side], self.hot[:, side], over(self.f1[:, 2 * e + side], TOPK), free=side > 0)
        for side in range(2):
            o.sum(self.pick[:, side, e], self.hot[:, side], free=side > 0)

    def finish(self, o, j):
        flat = lambda t: t.rearrange("p h t -> p (h t)")
        o.stt(flat(self.pick[:, 0]), flat(self.pick[:, 0]), float(NK), flat(self.pick[:, 1]), ALU.mult, ALU.add)
        for e in range(PH):
            o.ts(self.best[:, j, e], self.best[:, j, e], self.best[:, j, e, 0:1], ALU.subtract, free=e > 0)
        return o.ts(self.ids[:, j, :], flat(self.pick[:, 0]), float(self.l * NK * NK), ALU.add)


def peer(k, a, l, mod, w_query, spare, cols=None):
    nc = k.nc
    with ExitStack() as c:
        h = k.sb("normed", [P, NT, D], ctx=c)
        choice = Choice(k, l, c)
        with ExitStack() as c1:
            qT = spare[:, 0:2 * PH * SEQ].rearrange("p (n t) -> p n t", t=SEQ)
            sk = k.sb("sub_keys", [P, 2, P], ctx=c1)
            skT = k.sb("sub_keysT", [P, 2, P], ctx=c1)
            with ExitStack() as c2:
                hT = split_sb(k, "normedT", [P, KC, SEQ], c2)
                norm_stage(k, k.X, a["norm2_g_2"][l:l + 1, :], h, mod[:, 4 * D:5 * D], mod[:, 3 * D:4 * D], turned_to=hT,
                           extra=(sk[:, :, :], a["peer_sub_keys_2"][l].rearrange("s n d -> n s d")))
                turn_stage(k, [([sk[:, 0, :], sk[:, 1, :]], skT[:, :, :])])
                linear_turned_stage(k, hT, w_query, 1, lambda o, n, v, bank: o.copy(
                    qT[:, bass.ds(n, 1), :].rearrange("p a n -> p (a n)"), bank[:, 0:SEQ], free=True))
            bias = k.sb("next_bias", [P, 6 * D], ctx=c1) if cols is not None else None
            choose_first(k, choice, qT, skT, None if cols is None else Modulation(
                k, cols, a["mod_w_2"][l + 1], a["mod_b_2"][l + 1:l + 2, :], spare, bias))
        experts(k, a, h, choice, mod)


def choose_first(k, choice, qT, skT, next_mod):
    nc = k.nc
    S = k.sem
    with nc.Block() as block:
        if next_mod is not None:
            @block.sync
            def _(sp):
                next_mod.load(sp)

            @block.gpsimd
            def _(pool):
                next_mod.add_bias(pool)

        @block.tensor
        def _(pe):
            for j in range(NT):
                for n in range(2 * PH):
                    last = nc.tensor.matmul(k.bank(4 * j + n // 4)[:, n % 4 * P:n % 4 * P + P],
                                            qT[:, n, j * P:j * P + P], skT[:, n % 2, :], start=True, stop=True)
                    if n % 4 == 3:
                        last.then_inc(S["summed"], 1)
            if next_mod is not None:
                next_mod.products(pe, S["copied_s"])

        @block.scalar
        def _(act):
            for b in range(4 * NT):
                act.wait_ge(S["summed"], b + 1)
                nc.scalar.copy(choice.s[:, b // 4, b % 4 * 4:b % 4 * 4 + 4, :], k.bank(b, 4, P)).then_inc(S["copied_s"], 1)
            if next_mod is not None:
                next_mod.copies(act)

        @block.vector
        def _(dve):
            o = Ops(nc, dve, True)
            for n in range(2 * PH):
                if n % 4 == 0:
                    dve.wait_ge(S["copied_s"], n // 4 + 1)
                choice.keys(o, 0, n)
            for e in range(PH):
                choice.pairs(o, 0, e)
            for e in range(PH):
                choice.places(o, 0, e)
            choice.finish(o, 0)
    k.clear()


def experts(k, a, h, choice, mod):
    nc = k.nc
    S = k.sem
    C = k.const
    BODY = 2 * RING
    n_iter = SLOTS // BODY
    uses = SLOTS // RING
    down = a["peer_down_2"].rearrange("l e d -> (l e) d")
    up = a["peer_up_2"].rearrange("l e d -> (l e) d")
    row = k.rows
    used = [S[f"used{r}"] for r in range(RING)]
    ids, best = choice.ids, choice.best
    with ExitStack() as c:
        buf = k.sb("expert_rows", [P, RING, D], ctx=c)
        idw = k.sb("ids_now", [P, 2, RING], U32, ctx=c)
        junk = k.sb("products", [P, D], ctx=c)
        dots = k.sb("dots", [P, SLOTS], ctx=c)
        dnow = k.sb("dots_now", [P, BODY], ctx=c)
        coef = k.sb("coefficients", [P, SLOTS], ctx=c)
        tot = k.sb("gate_sum", [P, PH], ctx=c)
        diag = k.sb("diagonals", [P, 4, P], ctx=c)
        zero = k.sb("zeros", [P, P], ctx=c)
        acc = k.sb("accumulated", [P, D], ctx=c)

        def landed(j, phase, half):
            return 16 * (k.row_uses + (2 * j + phase) * uses + half + 1)

        with nc.Block() as block:
            @block.gpsimd
            def _(pool):
                for j in range(NT):
                    if j > 0:
                        pool.wait_ge(S["chosen"], j)
                    for phase, table in enumerate((down, up)):
                        base = (2 * j + phase) * uses
                        with pool.Fori(0, n_iter) as i:
                            for n in range(BODY):
                                r, half = n % RING, n // RING
                                pool.wait_ge(used[r], i * 2 + (half + base + 1))
                                if r == 0:
                                    nc.gpsimd.tensor_copy(idw[:, half, :], ids[:, j, bass.ds(i * BODY + n, RING)]
                                                          ).then_inc(S["ids_ready"], 1)
                                    pool.wait_ge(S["ids_ready"], i * 2 + (half + base + 1))
                                pool.sem_inc(S["gathers"], 1)
                                nc.gpsimd.indirect_dma_start(
                                    out=buf[:, r, :], out_offset=None, in_=table,
                                    in_offset=bass.IndirectOffsetOnAxis(ap=idw[:, half, r:r + 1], axis=0)
                                ).then_inc(row[r], 16)

            @block.vector
            def _(dve):
                o = Ops(nc, dve, True)
                o.ts(zero[:, :], C("ident"), 0.0, ALU.mult).then_inc(S["reduced"], 1)
                for r in range(RING):
                    dve.sem_inc(used[r], 1)
                for j in range(NT):
                    with dve.Fori(0, n_iter) as i:
                        for n in range(BODY):
                            r, half = n % RING, n // RING
                            dve.drain()
                            dve.wait_ge(row[r], i * 32 + landed(j, 0, half))
                            o.dot(junk[:, :], buf[:, r, :], h[:, j, :], dnow[:, n:n + 1],
                                  free=True).then_inc(used[r], 1)
                        o.copy(dots[:, bass.ds(i * BODY, BODY)], dnow[:, :])
                    dve.drain()
                    dve.sem_inc(S["squared"], 1)
                    o.ts(acc[:, :], h[:, j, :], 0.0, ALU.mult, free=True)
                    dve.wait_ge(S["gate_exped"], j + 1)
                    o.sum(tot[:, :], best[:, j])
                    o.recip(tot[:, :], tot[:, :])
                    o.mul(best[:, j], best[:, j], spread(tot[:, :], TOPK))
                    dve.wait_ge(S["exped"], j + 1)
                    o.mul(coef[:, :], coef[:, :], best[:, j].rearrange("p h t -> p (h t)")).then_inc(S["stored"], 1)

                    def add_row(n, i, r, half):
                        dve.wait_ge(row[r], i * 32 + landed(j, 1, half))
                        at = i * BODY + n
                        o.stt(acc[:, :], buf[:, r, :], coef[:, at:at + 1] if isinstance(at, int) else coef[:, bass.ds(at, 1)],
                              acc[:, :], ALU.mult, ALU.add, free=True).then_inc(used[r], 1)

                    if j == 0:
                        for m in range(SLOTS // 2):
                            dve.drain()
                            add_row(2 * m % BODY, 2 * m // BODY, 2 * m % RING, 2 * m % BODY // RING)
                            if m < 4 * PH and m % 2 == 1:
                                choice.keys(o, 1, m // 2)
                            elif 4 * PH <= m < 5 * PH:
                                choice.pairs(o, 1, m - 4 * PH)
                            elif 5 * PH <= m < 7 * PH and m % 2 == 0:
                                choice.places(o, 1, (m - 5 * PH) // 2)
                            elif m == 7 * PH:
                                choice.finish(o, 1).then_inc(S["chosen"], 1)
                    else:
                        with dve.Fori(0, n_iter) as i:
                            for n in range(0, BODY, 2):
                                dve.drain()
                                add_row(n, i, n % RING, n // RING)
                    dve.wait_ge(S["summed"], j + 1)
                    for half in range(2):
                        cs = slice(half * BANK, (half + 1) * BANK)
                        o.add(acc[:, cs], acc[:, cs], k.bank(2 * j + half))
                        o.mul(acc[:, cs], acc[:, cs], mod[:, 5 * D + half * BANK:5 * D + (half + 1) * BANK])
                        o.add(k.X[:, j, cs], k.X[:, j, cs], acc[:, cs])

            @block.scalar
            def _(act):
                o = Ops(nc, act, False)
                for j in range(NT):
                    if j > 0:
                        act.wait_ge(S["chosen"], j)
                    o.fn(best[:, j], best[:, j], ACT.Exp, free=True).then_inc(S["gate_exped"], 1)
                    act.wait_ge(S["squared"], j + 1)
                    o.fn(coef[:, :], dots[:, :], ACT.Gelu_apprx_tanh).then_inc(S["exped"], 1)
                    act.wait_ge(S["stored"], j + 1)
                    with act.Fori(0, n_iter) as i:
                        for m in range(RING):
                            n = 2 * m + 1
                            act.wait_ge(S["prod"], i * RING + (m + 1 + j * SLOTS // 2))
                            o.fn(diag[:, m % 4, :], C("ident"), ACT.Copy, scale=coef[:, bass.ds(i * BODY + n, 1)],
                                 free=True).then_inc(S["grown"], 1)

            @block.tensor
            def _(pe):
                pe.wait_ge(S["reduced"], 1)
                pe.sem_inc(S["prod"], 4)
                for j in range(NT):
                    for half in range(2):
                        nc.tensor.matmul(k.bank(2 * j + half), zero[:, :], h[:, j, half * BANK:(half + 1) * BANK],
                                         start=True, stop=False)
                    base = j * SLOTS // 2
                    with pe.Fori(0, n_iter) as i:
                        for m in range(RING):
                            n = 2 * m + 1
                            r, half = n % RING, n // RING
                            pe.wait_ge(S["grown"], i * RING + (m + 1 + base))
                            pe.wait_ge(row[r], i * 32 + landed(j, 1, half))
                            for hb in range(2):
                                last = nc.tensor.matmul(k.bank(2 * j + hb), diag[:, m % 4, :],
                                                        buf[:, r, hb * BANK:(hb + 1) * BANK], start=False, stop=False)
                            last.then_inc(S["prod"], 1)
                            pe.wait_ge(S["prod"], i * RING + (m + 5 + base))
                            pe.sem_inc(used[r], 1)
                    for half in range(2):
                        last = nc.tensor.matmul(k.bank(2 * j + half), zero[:, :], h[:, j, half * BANK:(half + 1) * BANK],
                                                start=False, stop=True)
                    last.then_inc(S["summed"], 1)
        k.row_uses += 2 * NT * uses
        k.clear()


INPUTS = ["x", "norm_ffn1", "ffn1_in", "ffn1_out", "norm_mix", "w_in", "rwkv_mu", "decay_w0", "decay_w2", "iclr_a0",
          "iclr_a2", "gate_g2", "k_k", "k_a", "r_k", "ln_x_g", "ln_x_b", "q_gain", "k_gain", "diff_lambda", "subln_g",
          "w_branch", "w_out", "norm_ffn2", "ffn2_in", "ffn2_out", "c_2", "ctx_2", "c_ctx_2", "mod_w_2", "mod_b_2",
          "norm1_g_2", "norm2_g_2", "attn_in_w_2", "attn_out_w_2", "attn_sink_2", "gmlp_w_s_2", "gmlp_b_s_2",
          "pool_w_2", "pool_scale_2", "peer_w_q_2", "peer_sub_keys_2", "peer_down_2", "peer_up_2", "final_g_2"]

SEMAPHORES = (["loaded", "turned", "copied_v", "copied_s", "squared", "rooted", "reduced", "summed", "drained",
               "used", "pre_done", "biased", "squashed", "exped", "masked", "lsum", "prod", "got", "corr",
               "grown", "done", "stored", "ids_ready", "gathers", "written", "chosen", "gate_exped", "slot_in0", "slot_in1"]
              + ["high", "low"] + [f"{e}_lane{g}" for e in ("pe", "act", "dve") for g in range(2)] + [f"used{r}" for r in range(8)])


def build(nc, a, out, stop=None):
    with ExitStack() as ctx:
        k = Kernel(nc, ctx, SEMAPHORES)
        load_stage(k, [(k.C[:, :], k.table_dram), (k.X[:, :, :], a["x"][0].rearrange("(j p) d -> p j d", p=P))])
        with ExitStack() as c:
            lam = k.sb("lambda_table", [P, DEPTH, 2], ctx=c)
            with nc.Block() as block:
                @block.vector
                def _(dve):
                    for l in range(DEPTH):
                        init = 0.8 - 0.6 * math.exp(-0.3 * l)
                        nc.vector.memset(lam[:, l, 0:1], init)
                        nc.vector.memset(lam[:, l, 1:2], 1.0 - init)
            k.clear()
            with nc.Fori(0, DEPTH) as l:
                first_layer(k, l, a, lam)
                k.restart_stream()
        with ExitStack() as c:
            mod = k.sb("modulation", [P, 6 * D], ctx=c)
            cols = k.sb("condition_columns", [P, KC, P], ctx=c)
            w_query = [row_weights(a["peer_w_q_2"][l], 8, 256) for l in range(DEPTH)]
            attn_gmlp_layer(k, a, cols, mod, w_query[0])
            next_mod = k.sb("next_modulation", [P, 6 * D], ctx=c)
            peer(k, a, 0, mod, w_query[0], next_mod, cols)
            pool_layer(k, a, next_mod, w_query[1])
            peer(k, a, 1, next_mod, w_query[1], mod)
        with ExitStack() as c:
            h = k.sb("normed", [P, NT, D], ctx=c)
            if stop is None:
                norm_stage(k, k.X, a["final_g_2"].rearrange("(a n) -> a n", a=1), h)
            src = h if stop is None else k.X
            with nc.Block() as block:
                @block.sync
                def _(sp):
                    sp.dma_start(out[0].rearrange("(j p) d -> p j d", p=P), src[:, :, :]).then_inc(k.sem["written"], 16)
                    sp.wait_ge(k.sem["written"], 16)


def kernel(**inputs):
    import concourse.bacc as bacc
    from concourse.bass_utils import run_bass_kernel_spmd

    nc = bacc.Bacc("TRN2", target_bir_lowering=False, num_devices=1)
    arrays, a = {}, {}
    for name in INPUTS:
        arrays[name] = np.ascontiguousarray(inputs[name])
        a[name] = nc.dram_tensor(name, arrays[name].shape, mybir.dt.from_np(arrays[name].dtype), kind="ExternalInput").ap()
    out = nc.dram_tensor("out", (1, SEQ, D), F32, kind="ExternalOutput").ap()
    build(nc, a, out)
    r = run_bass_kernel_spmd(nc, [arrays], core_ids=[0])
    return r.results[0]["out"]
```
